# Optimizing a Trainium2 kernel written in Bass

```python
import jax, jax.numpy as jnp
from jax import lax
import numpy as np
import math

D_MODEL = 2048
BATCH = 1
SEQ = 256
DEPTH = 1

MIX_WIDTH = D_MODEL
HEAD_DIM = 128
DELTA_WIDTH = MIX_WIDTH // 2
N_DELTA_HEADS = DELTA_WIDTH // HEAD_DIM
DILATED_WIDTH = MIX_WIDTH - DELTA_WIDTH
N_DILATED_HEADS = DILATED_WIDTH // HEAD_DIM
DILATION_PAIRS = ((128, 1), (512, 4), (2048, 16))
N_BRANCH = 3
ATTN_BLOCK = 128
DELTA_CHUNK = 64
SHORT_CONV_WIDTH = 5
FFN_CONV_WIDTH = 3
D_FF = 5632
ROPE_THETA = 500000.0
ROT_DIM = HEAD_DIM // 4
NORM_EPS = 1e-6
NEG_INF = -1e30
PROJ_WIDTH = 4 * DELTA_WIDTH + 4 * N_DELTA_HEADS + 3 * N_BRANCH * DILATED_WIDTH


def rms_norm(x, w):
    xf = x.astype(jnp.float32)
    y = xf * lax.rsqrt(jnp.mean(xf * xf, axis=-1, keepdims=True) + NORM_EPS)
    return (y * w.astype(jnp.float32)).astype(x.dtype)

def l2_normalize(x):
    return x * lax.rsqrt(jnp.sum(x * x, axis=-1, keepdims=True) + NORM_EPS)

def depthwise_conv_centered(x, w):
    width, ch = w.shape
    return lax.conv_general_dilated(
        x, w[:, None, :].astype(x.dtype), window_strides=(1,),
        padding=[(width // 2, width // 2)],
        dimension_numbers=("NWC", "WIO", "NWC"), feature_group_count=ch)

def partial_rope(x, positions):
    inv_freq = ROPE_THETA ** (-jnp.arange(0, ROT_DIM, 2, dtype=jnp.float32) / ROT_DIM)
    ang = positions.astype(jnp.float32)[..., None] * inv_freq
    cos = jnp.cos(ang)[:, :, None, :]
    sin = jnp.sin(ang)[:, :, None, :]
    xr = x[..., :ROT_DIM].astype(jnp.float32)
    x1, x2 = xr[..., :ROT_DIM // 2], xr[..., ROT_DIM // 2:]
    rot = jnp.concatenate([x1 * cos - x2 * sin, x2 * cos + x1 * sin], axis=-1)
    return jnp.concatenate([rot.astype(x.dtype), x[..., ROT_DIM:]], axis=-1)

def gated_delta_chunked(q, k, v, g, beta):
    bsz, nh, s, dk = q.shape
    dv = v.shape[-1]
    c = DELTA_CHUNK
    n = s // c
    q = q.reshape(bsz, nh, n, c, dk)
    k = k.reshape(bsz, nh, n, c, dk)
    v = v.reshape(bsz, nh, n, c, dv)
    g = g.reshape(bsz, nh, n, c)
    beta = beta.reshape(bsz, nh, n, c)
    cum_g = jnp.cumsum(g, axis=-1)
    lower = np.tril(np.ones((c, c), dtype=bool))
    strict = np.tril(np.ones((c, c), dtype=bool), -1)
    gamma = jnp.exp(jnp.where(lower, cum_g[..., :, None] - cum_g[..., None, :], NEG_INF))
    k_beta = k * beta[..., None]
    a_mat = jnp.where(strict, jnp.einsum("bhnik,bhnjk->bhnij", k_beta, k) * gamma, 0.0)
    t_mat = a_mat + jnp.eye(c, dtype=jnp.float32)
    u = lax.linalg.triangular_solve(t_mat, v * beta[..., None], left_side=True,
                                    lower=True, unit_diagonal=True)
    w = lax.linalg.triangular_solve(t_mat, k_beta * jnp.exp(cum_g)[..., None], left_side=True,
                                    lower=True, unit_diagonal=True)
    qk = jnp.einsum("bhnik,bhnjk->bhnij", q, k) * gamma
    q_dec = q * jnp.exp(cum_g)[..., None]
    k_tail = k * jnp.exp(cum_g[..., -1:] - cum_g)[..., None]
    chunk_decay = jnp.exp(cum_g[..., -1])

    def step(state, xs):
        u_n, w_n, qd_n, qk_n, kt_n, dec_n = xs
        v_new = u_n - jnp.einsum("bhck,bhkv->bhcv", w_n, state)
        o_n = (jnp.einsum("bhck,bhkv->bhcv", qd_n, state)
               + jnp.einsum("bhcj,bhjv->bhcv", qk_n, v_new))
        state = state * dec_n[..., None, None] + jnp.einsum("bhck,bhcv->bhkv", kt_n, v_new)
        return state, o_n

    xs = tuple(jnp.moveaxis(t, 2, 0) for t in (u, w, q_dec, qk, k_tail, chunk_decay))
    state0 = jnp.zeros((bsz, nh, dk, dv), jnp.float32)
    _, o = lax.scan(step, state0, xs)
    return jnp.moveaxis(o, 0, 2).reshape(bsz, nh, s, dv)

def delta_mixer(qkv_raw, z, a_f, a_b, b_f, b_b, conv_w, a_log_f, a_log_b, dt_b_f, dt_b_b, norm_w):
    bsz, s, _ = qkv_raw.shape
    qkv = jax.nn.silu(depthwise_conv_centered(qkv_raw, conv_w))
    q, k, v = jnp.split(qkv.astype(jnp.float32), 3, axis=-1)
    to_heads = lambda t: t.reshape(bsz, s, N_DELTA_HEADS, HEAD_DIM).transpose(0, 2, 1, 3)
    q = l2_normalize(to_heads(q)) * (HEAD_DIM ** -0.5)
    k = l2_normalize(to_heads(k))
    v = to_heads(v)

    def gates(a, b, a_log, dt_bias):
        a = a.astype(jnp.float32).transpose(0, 2, 1)
        b = b.astype(jnp.float32).transpose(0, 2, 1)
        g = -jnp.exp(a_log.astype(jnp.float32))[:, None] * jax.nn.softplus(
            a + dt_bias.astype(jnp.float32)[:, None])
        return g, jax.nn.sigmoid(b)

    g_f, beta_f = gates(a_f, b_f, a_log_f, dt_b_f)
    g_b, beta_b = gates(a_b, b_b, a_log_b, dt_b_b)
    flip = lambda t: jnp.flip(t, axis=2)
    o = (gated_delta_chunked(q, k, v, g_f, beta_f)
         + flip(gated_delta_chunked(flip(q), flip(k), flip(v), flip(g_b), flip(beta_b))))
    o = o.transpose(0, 2, 1, 3)
    o = o * lax.rsqrt(jnp.mean(o * o, axis=-1, keepdims=True) + NORM_EPS) * norm_w.astype(jnp.float32)
    o = o * jax.nn.silu(z.astype(jnp.float32).reshape(bsz, s, N_DELTA_HEADS, HEAD_DIM))
    return o.reshape(bsz, s, DELTA_WIDTH)

def dilated_window_attention(q, k, v, dilation, half_span):
    bsz, nh, s, dh = q.shape
    length = s // dilation
    nb = -(-length // ATTN_BLOCK)
    lp = nb * ATTN_BLOCK
    span = ATTN_BLOCK + 2 * half_span
    by_residue = lambda t: t.reshape(bsz, nh, length, dilation, dh).transpose(0, 1, 3, 2, 4)
    pad_q = ((0, 0), (0, 0), (0, 0), (0, lp - length), (0, 0))
    pad_kv = ((0, 0), (0, 0), (0, 0), (half_span, lp - length + half_span), (0, 0))
    qb = jnp.pad(by_residue(q), pad_q).reshape(bsz, nh, dilation, nb, ATTN_BLOCK, dh)
    idx = (np.arange(nb) * ATTN_BLOCK)[:, None] + np.arange(span)[None, :]
    kb = jnp.take(jnp.pad(by_residue(k), pad_kv), idx, axis=3)
    vb = jnp.take(jnp.pad(by_residue(v), pad_kv), idx, axis=3)
    scores = jnp.einsum("bhrnqe,bhrnke->bhrnqk", qb, kb,
                        preferred_element_type=jnp.float32) * (dh ** -0.5)
    qpos = (np.arange(nb) * ATTN_BLOCK)[:, None] + np.arange(ATTN_BLOCK)[None, :]
    kpos = (np.arange(nb) * ATTN_BLOCK - half_span)[:, None] + np.arange(span)[None, :]
    rel = kpos[:, None, :] - qpos[:, :, None]
    mask = (np.abs(rel) <= half_span) & (kpos[:, None, :] >= 0) & (kpos[:, None, :] < length)
    scores = jnp.where(mask, scores, NEG_INF)
    m = jnp.max(scores, axis=-1, keepdims=True)
    p = jnp.exp(scores - m)
    denom = jnp.sum(p, axis=-1, keepdims=True)
    o = jnp.einsum("bhrnqk,bhrnke->bhrnqe", p, vb.astype(jnp.float32)) / denom
    lse = (m + jnp.log(denom))[..., 0]
    o = o.reshape(bsz, nh, dilation, lp, dh)[:, :, :, :length]
    o = o.transpose(0, 1, 3, 2, 4).reshape(bsz, nh, s, dh)
    lse = lse.reshape(bsz, nh, dilation, lp)[:, :, :, :length].transpose(0, 1, 3, 2).reshape(bsz, nh, s)
    return o, lse

def dilated_mixer(bq, bk, bv, positions):
    bsz, s, _ = bq.shape
    outs, lses = [], []
    for gi, (window, dilation) in enumerate(DILATION_PAIRS):
        sl = slice(gi * DILATED_WIDTH, (gi + 1) * DILATED_WIDTH)
        heads = lambda t: t[..., sl].reshape(bsz, s, N_DILATED_HEADS, HEAD_DIM)
        q = partial_rope(heads(bq), positions).transpose(0, 2, 1, 3)
        k = partial_rope(heads(bk), positions).transpose(0, 2, 1, 3)
        v = heads(bv).transpose(0, 2, 1, 3)
        o, lse = dilated_window_attention(q, k, v, dilation, window // (2 * dilation))
        outs.append(o)
        lses.append(lse)
    weights = jax.nn.softmax(jnp.stack(lses, axis=0), axis=0)
    o = jnp.sum(weights[..., None] * jnp.stack(outs, axis=0), axis=0)
    return o.transpose(0, 2, 1, 3).reshape(bsz, s, DILATED_WIDTH)

def token_mixer(n, positions, w_in, conv_qkv_w, a_log_f, a_log_b, dt_b_f, dt_b_b, delta_norm_w, w_out):
    proj = jnp.einsum("bsd,dp->bsp", n, w_in)
    sizes = [3 * DELTA_WIDTH, DELTA_WIDTH] + [N_DELTA_HEADS] * 4 + [N_BRANCH * DILATED_WIDTH] * 3
    splits = [int(i) for i in np.cumsum(sizes)[:-1]]
    qkv_a, z, a_f, a_b, b_f, b_b, bq, bk, bv = jnp.split(proj, splits, axis=-1)
    out_a = delta_mixer(qkv_a, z, a_f, a_b, b_f, b_b, conv_qkv_w,
                        a_log_f, a_log_b, dt_b_f, dt_b_b, delta_norm_w)
    out_b = dilated_mixer(bq, bk, bv, positions)
    mixed = jnp.concatenate([out_a, out_b], axis=-1).astype(n.dtype)
    return jnp.einsum("bsm,md->bsd", mixed, w_out)

def conv_gated_mlp(n, w_ffn_in, conv_ffn_w, w_ffn_out):
    up = depthwise_conv_centered(jnp.einsum("bsd,df->bsf", n, w_ffn_in), conv_ffn_w)
    gate, val = jnp.split(up, 2, axis=-1)
    return jnp.einsum("bsf,fd->bsd", jax.nn.silu(gate) * val, w_ffn_out)

def first_inputs(seed: int = 0) -> dict:
    key = jax.random.key(seed)
    ks = jax.random.split(key, 16)
    f32 = jnp.float32
    nrm = lambda k, shape, scale: jax.random.normal(k, shape, f32) * scale
    gain = lambda k, shape: 1.0 + 0.02 * jax.random.normal(k, shape, f32)

    def dt_bias(k):
        dt = jnp.exp(jax.random.uniform(k, (DEPTH, N_DELTA_HEADS), f32)
                     * (np.log(0.1) - np.log(0.001)) + np.log(0.001))
        return dt + jnp.log(-jnp.expm1(-dt))

    return {
        "x": jax.random.normal(ks[0], (BATCH, SEQ, D_MODEL), f32),
        "positions": jnp.broadcast_to(jnp.arange(SEQ, dtype=jnp.int32), (BATCH, SEQ)),
        "norm_mix_w": gain(ks[1], (DEPTH, D_MODEL)),
        "w_in": nrm(ks[2], (DEPTH, D_MODEL, PROJ_WIDTH), D_MODEL ** -0.5),
        "conv_qkv_w": nrm(ks[3], (DEPTH, SHORT_CONV_WIDTH, 3 * DELTA_WIDTH), SHORT_CONV_WIDTH ** -0.5),
        "a_log_fwd": jnp.log(jax.random.uniform(ks[4], (DEPTH, N_DELTA_HEADS), f32, 1.0, 16.0)),
        "a_log_bwd": jnp.log(jax.random.uniform(ks[5], (DEPTH, N_DELTA_HEADS), f32, 1.0, 16.0)),
        "dt_bias_fwd": dt_bias(ks[6]),
        "dt_bias_bwd": dt_bias(ks[7]),
        "delta_norm_w": gain(ks[8], (DEPTH, HEAD_DIM)),
        "w_out": nrm(ks[9], (DEPTH, MIX_WIDTH, D_MODEL), MIX_WIDTH ** -0.5),
        "norm_ffn_w": gain(ks[10], (DEPTH, D_MODEL)),
        "w_ffn_in": nrm(ks[11], (DEPTH, D_MODEL, 2 * D_FF), D_MODEL ** -0.5),
        "conv_ffn_w": nrm(ks[12], (DEPTH, FFN_CONV_WIDTH, 2 * D_FF), FFN_CONV_WIDTH ** -0.5),
        "w_ffn_out": nrm(ks[13], (DEPTH, D_FF, D_MODEL), D_FF ** -0.5),
        "norm_final_w": gain(ks[14], (D_MODEL,)),
    }

def first_block(x, positions, norm_mix_w, w_in, conv_qkv_w, a_log_fwd, a_log_bwd, dt_bias_fwd,
              dt_bias_bwd, delta_norm_w, w_out, norm_ffn_w, w_ffn_in, conv_ffn_w, w_ffn_out,
              norm_final_w):
    h = x
    for layer in range(DEPTH):
        n = rms_norm(h, norm_mix_w[layer])
        h = h + token_mixer(n, positions, w_in[layer], conv_qkv_w[layer], a_log_fwd[layer],
                            a_log_bwd[layer], dt_bias_fwd[layer], dt_bias_bwd[layer],
                            delta_norm_w[layer], w_out[layer]).astype(h.dtype)
        n = rms_norm(h, norm_ffn_w[layer])
        h = h + conv_gated_mlp(n, w_ffn_in[layer], conv_ffn_w[layer], w_ffn_out[layer]).astype(h.dtype)
    return rms_norm(h, norm_final_w)


GRID_W = 64
CTX_LEN = 256
HG_WIDTH = 1024
HY_WIDTH = D_MODEL - HG_WIDTH
HG_HEAD_DIM = 128
HG_HEADS = HG_WIDTH // HG_HEAD_DIM
HG_ROW_HEADS = HG_HEADS // 2
CHUNK = 64
SHORT_CONV = 3
N_BANDS = 16
FILTER_EMB = 1 + 2 * N_BANDS
FILTER_HIDDEN = 64
FILTER_TARGET = 1e-2
FAST_DECAY_PCT = 0.3
SLOW_DECAY_PCT = 1.5
FILTER_SHIFT = 0.05
D_FF_2 = 4 * D_MODEL
N_MOD = 6
PROJ_WIDTH_2 = 5 * HG_WIDTH + 3 * HY_WIDTH
EPS = 1e-6


def _rmsnorm(t, g):
    t32 = t.astype(jnp.float32)
    y = t32 * lax.rsqrt(jnp.mean(t32 * t32, axis=-1, keepdims=True) + EPS)
    return (y * g.astype(jnp.float32)).astype(t.dtype)

def _modulate(t, shift, scale):
    return t * (1.0 + scale) + shift

def _col_order(t, rows, inverse):
    b, l, h, d = t.shape
    nc = h - HG_ROW_HEADS
    grid = (GRID_W, rows) if inverse else (rows, GRID_W)
    col = t[:, :, HG_ROW_HEADS:].reshape(b, grid[0], grid[1], nc, d)
    col = jnp.swapaxes(col, 1, 2).reshape(b, l, nc, d)
    return jnp.concatenate([t[:, :, :HG_ROW_HEADS], col], axis=2)

def _chunk_scan(q, k, v, log_f, s0):
    b, l, h, dk = q.shape
    dv = v.shape[-1]
    n = l // CHUNK
    qc = q.reshape(b, n, CHUNK, h, dk)
    kc = k.reshape(b, n, CHUNK, h, dk)
    vc = v.reshape(b, n, CHUNK, h, dv)
    a = jnp.cumsum(log_f.reshape(b, n, CHUNK, h, dk), axis=2)
    a_end = a[:, :, -1:]
    a_mid = a[:, :, CHUNK // 2 - 1:CHUNK // 2]
    scores = jnp.einsum("bnihd,bnjhd->bnhij", qc * jnp.exp(a - a_mid), kc * jnp.exp(a_mid - a))
    tril = jnp.tril(jnp.ones((CHUNK, CHUNK), dtype=bool))
    scores = jnp.where(tril, scores, 0.0)
    o_intra = jnp.einsum("bnhij,bnjhe->bnihe", scores, vc)
    upd = jnp.einsum("bnjhd,bnjhe->bnhde", kc * jnp.exp(a_end - a), vc)
    decay = jnp.exp(a_end[:, :, 0])

    def step(s, xs):
        dec, u = xs
        return dec[..., None] * s + u, s

    s_fin, s_start = lax.scan(step, s0, (jnp.moveaxis(decay, 1, 0), jnp.moveaxis(upd, 1, 0)))
    s_start = jnp.moveaxis(s_start, 0, 1)
    o_inter = jnp.einsum("bnihd,bnhde->bnihe", qc * jnp.exp(a), s_start)
    return (o_intra + o_inter).reshape(b, l, h, dv), s_fin

def _hgrn2_mixer(p_lat, p_ctx, lb, norm_g, rows, need_ctx_out):
    f32 = jnp.float32
    lb_f = lb[0].reshape(HG_HEADS, HG_HEAD_DIM)
    lb_b = lb[1].reshape(HG_HEADS, HG_HEAD_DIM)

    def prep(p):
        p = p.astype(f32)
        b, l, _ = p.shape
        q, zf, zb, v, g = jnp.split(p, 5, axis=-1)
        hd = lambda t: t.reshape(b, l, HG_HEADS, HG_HEAD_DIM)
        f_f = lb_f + (1.0 - lb_f) * jax.nn.sigmoid(hd(zf))
        f_b = lb_b + (1.0 - lb_b) * jax.nn.sigmoid(hd(zb))
        return [hd(q), 1.0 - f_f, jnp.log(f_f), 1.0 - f_b, jnp.log(f_b), hd(v)], g

    (qc, kfc, lffc, kbc, lfbc, vc), gc = prep(p_ctx)
    lat, gl = prep(p_lat)
    ql, kfl, lffl, kbl, lfbl, vl = [_col_order(t, rows, False) for t in lat]
    b = qc.shape[0]
    zeros = jnp.zeros((b, HG_HEADS, HG_HEAD_DIM, HG_HEAD_DIM), f32)
    flip = lambda t: jnp.flip(t, axis=1)
    o_cf, s_cf = _chunk_scan(qc, kfc, vc, lffc, zeros)
    o_cb, s_cb = _chunk_scan(flip(qc), flip(kbc), flip(vc), flip(lfbc), zeros)
    o_lf, _ = _chunk_scan(ql, kfl, vl, lffl, s_cf)
    o_lb, _ = _chunk_scan(flip(ql), flip(kbl), flip(vl), flip(lfbl), s_cb)
    o_lat = _col_order(o_lf + flip(o_lb), rows, True)
    gain = norm_g.astype(f32).reshape(HG_HEADS, HG_HEAD_DIM)

    def readout(o, g):
        bb, l = o.shape[:2]
        o = o * lax.rsqrt(jnp.mean(o * o, axis=-1, keepdims=True) + EPS) * gain
        return o.reshape(bb, l, HG_WIDTH) * jax.nn.silu(g)

    out_ctx = readout(o_cf + flip(o_cb), gc) if need_ctx_out else None
    return readout(o_lat, gl), out_ctx

def _short_conv(t, w, b):
    half = SHORT_CONV // 2
    l = t.shape[1]
    tp = jnp.pad(t, ((0, 0), (half, half), (0, 0)))
    return sum(tp[:, j:j + l] * w[j] for j in range(SHORT_CONV)) + b

def _implicit_filter(l, w1, b1, freq, w2, b2, w3):
    pos = jnp.arange(l, dtype=jnp.float32)[:, None]
    t = pos / max(l - 1, 1)
    bands = jnp.linspace(1e-4, N_BANDS - 1, N_BANDS, dtype=jnp.float32)[None, :]
    ang = bands * (2.0 * math.pi) * pos / l
    z = jnp.concatenate([t, jnp.cos(ang), -jnp.sin(ang)], axis=-1)
    h = jnp.sin(freq * (z @ w1 + b1))
    h = jnp.sin(freq * (h @ w2 + b2))
    h = h @ w3
    deltas = jnp.abs(jnp.linspace(math.log(FILTER_TARGET) / SLOW_DECAY_PCT,
                                  math.log(FILTER_TARGET) / FAST_DECAY_PCT, HY_WIDTH, dtype=jnp.float32))
    deltas = jnp.tile(deltas, 2)
    return h * (jnp.exp(-t * deltas) + FILTER_SHIFT)

def _bidir_long_conv(u, filt, bias):
    l, ch = u.shape[1], u.shape[2]
    kern = jnp.concatenate([filt[:, :ch], jnp.zeros((1, ch), filt.dtype), filt[:0:-1, ch:]], axis=0)
    kern = kern * lax.rsqrt(jnp.sum(kern * kern, axis=0, keepdims=True))
    spec = jnp.fft.rfft(u, n=2 * l, axis=1) * jnp.fft.rfft(kern, axis=0)[None]
    y = jnp.fft.irfft(spec, n=2 * l, axis=1)[:, :l]
    return y + u * bias

def _hyena_mixer(p, conv_w, conv_b, w1, b1, freq, w2, b2, w3, bias):
    f32 = jnp.float32
    p = _short_conv(p.astype(f32), conv_w.astype(f32), conv_b.astype(f32))
    v, x1, x0 = jnp.split(p, 3, axis=-1)
    filt = _implicit_filter(p.shape[1], w1.astype(f32), b1.astype(f32), freq.astype(f32),
                            w2.astype(f32), b2.astype(f32), w3.astype(f32))
    return x0 * _bidir_long_conv(x1 * v, filt, bias.astype(f32))

def _sq_relu_mlp(u, w1, w2):
    return jnp.square(jax.nn.relu(u @ w1)) @ w2

def second_inputs(seed: int = 0) -> dict:
    key = jax.random.key(seed)
    ks = jax.random.split(key, 24)
    nrm = lambda k, shape, scale: scale * jax.random.normal(k, shape, jnp.float32)
    return {
        "x": nrm(ks[0], (BATCH, SEQ, D_MODEL), 1.0),
        "c": nrm(ks[1], (BATCH, D_MODEL), 1.0),
        "ctx": nrm(ks[2], (BATCH, CTX_LEN, D_MODEL), 1.0),
        "c_ctx": nrm(ks[3], (D_MODEL,), 1.0),
        "w_ada": nrm(ks[4], (DEPTH, D_MODEL, N_MOD * D_MODEL), 0.5 * D_MODEL ** -0.5),
        "b_ada": nrm(ks[5], (DEPTH, N_MOD * D_MODEL), 0.02),
        "norm1_g": 1.0 + nrm(ks[6], (DEPTH, D_MODEL), 0.05),
        "w_in": nrm(ks[7], (DEPTH, D_MODEL, PROJ_WIDTH_2), D_MODEL ** -0.5),
        "hgrn_lb_logits": nrm(ks[8], (2, DEPTH + 1, HG_WIDTH), 0.5),
        "hgrn_norm_g": 1.0 + nrm(ks[9], (DEPTH, HG_WIDTH), 0.05),
        "hy_conv_w": nrm(ks[10], (DEPTH, SHORT_CONV, 3 * HY_WIDTH), SHORT_CONV ** -0.5),
        "hy_conv_b": nrm(ks[11], (DEPTH, 3 * HY_WIDTH), 0.02),
        "flt_w1": nrm(ks[12], (DEPTH, FILTER_EMB, FILTER_HIDDEN), FILTER_EMB ** -0.5),
        "flt_b1": nrm(ks[13], (DEPTH, FILTER_HIDDEN), 0.1),
        "flt_freq": 1.0 + nrm(ks[14], (DEPTH, FILTER_HIDDEN), 0.05),
        "flt_w2": nrm(ks[15], (DEPTH, FILTER_HIDDEN, FILTER_HIDDEN), FILTER_HIDDEN ** -0.5),
        "flt_b2": nrm(ks[16], (DEPTH, FILTER_HIDDEN), 0.1),
        "flt_w3": nrm(ks[17], (DEPTH, FILTER_HIDDEN, 2 * HY_WIDTH), FILTER_HIDDEN ** -0.5),
        "hy_bias": nrm(ks[18], (DEPTH, HY_WIDTH), 0.5),
        "w_out": nrm(ks[19], (DEPTH, D_MODEL, D_MODEL), D_MODEL ** -0.5),
        "norm2_g": 1.0 + nrm(ks[20], (DEPTH, D_MODEL), 0.05),
        "w_mlp1": nrm(ks[21], (DEPTH, D_MODEL, D_FF_2), D_MODEL ** -0.5),
        "w_mlp2": nrm(ks[22], (DEPTH, D_FF_2, D_MODEL), D_FF_2 ** -0.5),
        "final_norm_g": 1.0 + nrm(ks[23], (D_MODEL,), 0.05),
    }

def second_block(x, c, ctx, c_ctx, w_ada, b_ada, norm1_g, w_in, hgrn_lb_logits, hgrn_norm_g,
              hy_conv_w, hy_conv_b, flt_w1, flt_b1, flt_freq, flt_w2, flt_b2, flt_w3, hy_bias,
              w_out, norm2_g, w_mlp1, w_mlp2, final_norm_g):
    rows = x.shape[1] // GRID_W
    hg_cols = 5 * HG_WIDTH
    lb_all = jnp.cumsum(jax.nn.softmax(hgrn_lb_logits.astype(jnp.float32), axis=1), axis=1)
    silu_c = jax.nn.silu(c)
    silu_cc = jax.nn.silu(c_ctx)
    for layer in range(DEPTH):
        need_ctx = layer + 1 < DEPTH
        m_lat = (silu_c @ w_ada[layer] + b_ada[layer])[:, None, :]
        m_ctx = silu_cc @ w_ada[layer] + b_ada[layer]
        sh1, sc1, g1, sh2, sc2, g2 = jnp.split(m_lat, N_MOD, axis=-1)
        csh1, csc1, cg1, csh2, csc2, cg2 = jnp.split(m_ctx, N_MOD, axis=-1)

        u_lat = _modulate(_rmsnorm(x, norm1_g[layer]), sh1, sc1)
        u_ctx = _modulate(_rmsnorm(ctx, norm1_g[layer]), csh1, csc1)
        p_lat = u_lat @ w_in[layer]
        p_ctx = u_ctx @ w_in[layer]

        a_lat, a_ctx = _hgrn2_mixer(p_lat[..., :hg_cols], p_ctx[..., :hg_cols], lb_all[:, layer],
                                    hgrn_norm_g[layer], rows, need_ctx)
        hy_args = (hy_conv_w[layer], hy_conv_b[layer], flt_w1[layer], flt_b1[layer], flt_freq[layer],
                   flt_w2[layer], flt_b2[layer], flt_w3[layer], hy_bias[layer])
        y_lat = _hyena_mixer(p_lat[..., hg_cols:], *hy_args)

        mix_lat = jnp.concatenate([a_lat, y_lat], axis=-1).astype(x.dtype) @ w_out[layer]
        x = x + g1 * mix_lat
        x = x + g2 * _sq_relu_mlp(_modulate(_rmsnorm(x, norm2_g[layer]), sh2, sc2), w_mlp1[layer], w_mlp2[layer])

        if need_ctx:
            y_ctx = _hyena_mixer(p_ctx[..., hg_cols:], *hy_args)
            mix_ctx = jnp.concatenate([a_ctx, y_ctx], axis=-1).astype(ctx.dtype) @ w_out[layer]
            ctx = ctx + cg1 * mix_ctx
            ctx = ctx + cg2 * _sq_relu_mlp(_modulate(_rmsnorm(ctx, norm2_g[layer]), csh2, csc2),
                                           w_mlp1[layer], w_mlp2[layer])
    return _rmsnorm(x, final_norm_g)


def setup_inputs(seed=0):
    out = dict(first_inputs(seed))
    for name, value in second_inputs(seed + 1).items():
        if name != "x":
            out[name + "_2"] = value
    return out


def reference(
    x, positions, norm_mix_w, w_in, conv_qkv_w, a_log_fwd, a_log_bwd, dt_bias_fwd, dt_bias_bwd,
    delta_norm_w, w_out, norm_ffn_w, w_ffn_in, conv_ffn_w, w_ffn_out, norm_final_w, c_2, ctx_2,
    c_ctx_2, w_ada_2, b_ada_2, norm1_g_2, w_in_2, hgrn_lb_logits_2, hgrn_norm_g_2, hy_conv_w_2,
    hy_conv_b_2, flt_w1_2, flt_b1_2, flt_freq_2, flt_w2_2, flt_b2_2, flt_w3_2, hy_bias_2,
    w_out_2, norm2_g_2, w_mlp1_2, w_mlp2_2, final_norm_g_2,
):
    x = first_block(
        x, positions, norm_mix_w, w_in, conv_qkv_w, a_log_fwd, a_log_bwd, dt_bias_fwd,
        dt_bias_bwd, delta_norm_w, w_out, norm_ffn_w, w_ffn_in, conv_ffn_w, w_ffn_out,
        norm_final_w,
    )
    return second_block(
        x, c_2, ctx_2, c_ctx_2, w_ada_2, b_ada_2, norm1_g_2, w_in_2, hgrn_lb_logits_2,
        hgrn_norm_g_2, hy_conv_w_2, hy_conv_b_2, flt_w1_2, flt_b1_2, flt_freq_2, flt_w2_2,
        flt_b2_2, flt_w3_2, hy_bias_2, w_out_2, norm2_g_2, w_mlp1_2, w_mlp2_2, final_norm_g_2,
    )


_drawn_inputs = setup_inputs


def setup_inputs(seed=0):
    import zlib

    import numpy as np

    out = dict(_drawn_inputs(seed))
    spreads = {}
    factors = {'norm_mix_w': 3.528,
     'delta_norm_w': 5.508,
     'norm_ffn_w': 3.616,
     'ctx_2': 5.973,
     'c_ctx_2': 8.0,
     'hgrn_norm_g_2': 7.646,
     'hy_conv_b_2': 4.144,
     'flt_freq_2': 3.707,
     'norm2_g_2': 3.725}
    for name, (base, spread) in spreads.items():
        noise = np.random.default_rng([zlib.crc32(name.encode()), seed]).standard_normal(out[name].shape)
        drawn = base * np.exp(spread * noise) if base else spread * noise
        out[name] = __import__('jax').numpy.asarray(drawn.astype(out[name].dtype))
    for name, factor in factors.items():
        out[name] = (out[name] * factor).astype(out[name].dtype)
    return out
```

```python
import numpy as np
from concourse import mybir
from contextlib import ExitStack

F32 = mybir.dt.float32
F32R = mybir.dt.float32r
I32 = mybir.dt.int32
ALU = mybir.AluOpType
ACT = mybir.ActivationFunctionType
AX = mybir.AxisListType

P = 128
S = 256
D = 2048
KT = D // P
NH = 8
DFF, DFF2 = 5632, 8192
EPS = 1e-6
NB = 8
RAW, SPLIT = 8, 4
AHEAD = SPLIT - 1
HD = 128
CH = 64
FFN_PARTS = [(0, 16), (16, 16), (32, 12)]
MLP_PARTS = [(0, 16), (16, 16), (32, 16), (48, 16)]
DELTA_W = 1024
GATE_COL = 4 * DELTA_W
DIL_COL = GATE_COL + 4 * NH


def shape_constants():
    i = np.arange(P)
    c = {}
    c["ident"] = np.eye(P)
    c["ones"] = np.ones((P, P))
    c["level"] = np.concatenate(
        [(((i[:, None] >> s) ^ (i[None, :] >> s)) == 1) for s in range(7)], 1).astype(np.float64)
    fwd_s, fwd_i = i[None, :] > i[:, None], i[None, :] >= i[:, None]
    bwd_s, bwd_i = i[None, :] < i[:, None], i[None, :] <= i[:, None]
    c["neg"] = np.concatenate([np.where(m, 0.0, -1e30) for m in (fwd_s, fwd_i, bwd_s, bwd_i)], 1)
    c["tri"] = np.concatenate([fwd_i, bwd_i], 1).astype(np.float64)
    t = np.arange(S)
    dist = t[None, :] - t[:, None]
    seen = [np.abs(dist) <= 64, dist % 4 == 0, dist % 16 == 0]
    m = np.stack([np.where(x, 0.0, -1e30) for x in seen])
    c["dil"] = m.reshape(3, 2, P, S).transpose(2, 1, 0, 3).reshape(P, 6 * S)
    c["reset"] = np.tile(np.concatenate([t % CH != 0, t % CH != CH - 1]).astype(np.float64), (P, 1))
    row = np.arange(P)
    c["rowsel"] = np.stack([row < 8, (row >= 8) & (row < 16), row >= 16], 1).astype(np.float64)
    c["gsign"] = np.where(row < 16, 1.0, -1.0)[:, None].repeat(2, 1)
    c["sel"] = np.stack([row % 2 == 0, row % 2 == 1], 1).astype(np.float64) * (row < 4)[:, None]
    freq = (500000.0 ** (-np.arange(0, 32, 2) / 32)).astype(np.float32)
    c["ropef"] = np.concatenate([freq, freq, np.zeros(96)])[:, None].repeat(2, 1)
    c["ropes"] = np.concatenate([-np.ones(16), np.ones(112)])[:, None].repeat(2, 1)
    c["notfirst"] = np.stack([row != 0, row >= 0], 1).astype(np.float64)
    k = (np.arange(S) + 0.5) * (2 * np.pi / (2 * S))
    ang = t[:, None] * k[None, :]
    cos, sin = np.cos(ang), np.sin(ang)
    f = np.concatenate([cos, sin], 1)
    c["dft"] = f.reshape(2, P, 2 * S).transpose(1, 0, 2).reshape(P, -1)
    inv = np.stack([cos.T, sin.T], 0) / S
    c["idft"] = inv.reshape(2, 2, P, S).transpose(2, 0, 1, 3).reshape(P, -1)
    names, cols, at = list(c), {}, 0
    for n in names:
        cols[n] = (at, c[n].shape[1])
        at += c[n].shape[1]
    table = np.concatenate([c[n] for n in names], 1).astype(np.float32)
    f32 = np.float32
    pos = np.arange(S, dtype=f32)[:, None]
    tt = pos / f32(S - 1)
    bands = np.linspace(1e-4, 15, 16, dtype=f32)[None, :]
    a = bands * f32(2.0 * np.pi) * pos / f32(S)
    z = np.concatenate([tt, np.cos(a), -np.sin(a)], -1).T.astype(f32)
    deltas = np.abs(np.linspace(np.log(1e-2) / 1.5, np.log(1e-2) / 0.3, 1024, dtype=f32))
    win = np.exp(-tt * deltas[None, :]) + f32(0.05)
    win = win.reshape(2, P, 1024).transpose(1, 0, 2).reshape(P, -1).astype(f32)
    jj = np.arange(P)
    same = (jj[:, None] // CH) == (jj[None, :] // CH)
    hm = np.stack([same & fwd_i, same & fwd_i, same & bwd_i, same & bwd_i], 1)
    return table, cols, np.ascontiguousarray(z), np.ascontiguousarray(win), \
        hm.reshape(P, 4 * P).astype(np.int32)


def blocks_of(w, tiles):
    kt = w.shape[0] // P
    return [(w, r, c) for c in tiles for r in range(kt)]


def stream(blocks, nb):
    n = len(blocks) // nb
    assert n * nb == len(blocks) and n % RAW == 0
    out = np.empty((n, P, nb * P), np.float32)
    for b, (w, r, c) in enumerate(blocks):
        out[b // nb, :, (b % nb) * P:(b % nb + 1) * P] = w[r * P:(r + 1) * P, c:c + P]
    return out


def cm(v):
    return np.ascontiguousarray(v.reshape(-1, P).T)


def lay_out(a):
    out = {}
    w_in, w_in2 = a["w_in"][0], a["w_in_2"][0]
    T = lambda *cols: list(cols)
    gate = [(w_in, r, GATE_COL) for r in range(KT)]
    delta, dil, ctx, hg, hy = [], [], [], [], []
    for h in range(NH):
        delta += blocks_of(w_in, [kind * DELTA_W + h * HD for kind in range(4)])
        dil += blocks_of(w_in, [DIL_COL + kind * 3 * 1024 + b * 1024 + h * HD
                                for kind in range(3) for b in range(3)])
        ctx += blocks_of(w_in2, T(1024 + h * HD, 2048 + h * HD, 3072 + h * HD))
        hg += blocks_of(w_in2, [kind * 1024 + h * HD for kind in range(5)])
        hy += blocks_of(w_in2, [5120 + kind * 1024 + h * HD for kind in range(3)])
    out["w_gate"] = stream(gate, 2)
    out["w_delta"] = stream(delta, 8)
    out["w_dil"] = stream(dil, 6)
    out["w_ctx"] = stream(ctx, 6)
    out["w_hg"] = stream(hg, 5)
    out["w_hy"] = stream(hy, 6)
    ada = a["w_ada_2"][0]
    out["w_ada"] = stream([(ada, r, n * 512 + c * P) for n in range(24) for r in range(KT)
                           for c in range(4)], 8)
    out["w_out"] = stream(blocks_of(a["w_out"][0], range(0, D, P)), 8)
    out["w_out2"] = stream(blocks_of(a["w_out_2"][0], range(0, D, P)), 8)
    fi, fo = a["w_ffn_in"][0], a["w_ffn_out"][0]
    up = []
    for t0, n in FFN_PARTS:
        for t in range(t0, t0 + n):
            up += blocks_of(fi, [t * P, DFF + t * P])
        out[f"w_down_{t0}"] = stream(blocks_of(fo[t0 * P:(t0 + n) * P], range(0, D, P)), n // 2)
    out["w_up"] = stream(up, 8)
    out["w_mlp1"] = stream(blocks_of(a["w_mlp1_2"][0], range(0, DFF2, P)), 8)
    m2 = []
    for t0, n in MLP_PARTS:
        m2 += blocks_of(a["w_mlp2_2"][0][t0 * P:(t0 + n) * P], range(0, D, P))
    out["w_mlp2"] = stream(m2, 8)

    tok = lambda x: np.ascontiguousarray(x[0].T.reshape(KT, P, S).transpose(1, 0, 2))
    out["x"], out["ctx"] = tok(a["x"]), tok(a["ctx_2"])
    out["cvec"] = np.ascontiguousarray(
        np.stack([a["c_2"][0], a["c_ctx_2"]]).reshape(2, KT, P).transpose(2, 1, 0))
    out["positions"] = np.ascontiguousarray(a["positions"])
    out["gains"] = np.concatenate(
        [cm(a["norm_mix_w"][0]), cm(a["norm_ffn_w"][0]), cm(a["norm_final_w"]),
         cm(a["norm1_g_2"][0]), cm(a["norm2_g_2"][0]), cm(a["final_norm_g_2"]),
         cm(a["b_ada_2"][0])], 1)
    conv = a["conv_qkv_w"][0].reshape(5, 3, NH, P).transpose(3, 2, 1, 0).reshape(P, NH, 15)
    nw = np.broadcast_to(a["delta_norm_w"][0][:, None, None], (P, NH, 1))
    out["delta_par"] = np.ascontiguousarray(np.concatenate([conv, nw], 2))
    out["ffn_par"] = np.ascontiguousarray(
        a["conv_ffn_w"][0].reshape(3, 2, 44, P).transpose(3, 2, 1, 0))
    lb = a["hgrn_lb_logits_2"].reshape(2, 2, NH, P).transpose(3, 0, 1, 2)
    out["lb_logits"] = np.ascontiguousarray(lb)
    out["hg_gain"] = cm(a["hgrn_norm_g_2"][0])
    cw = a["hy_conv_w_2"][0].reshape(3, 3, NH, P).transpose(3, 2, 1, 0).reshape(P, NH, 9)
    cb = a["hy_conv_b_2"][0].reshape(3, NH, P).transpose(2, 1, 0)
    bi = a["hy_bias_2"][0].reshape(NH, P).T[:, :, None]
    out["hy_par"] = np.ascontiguousarray(np.concatenate([cw, cb, bi], 2))
    z16 = np.zeros(16, np.float32)
    out["gate_par"] = np.ascontiguousarray(np.stack(
        [np.concatenate([a["dt_bias_fwd"][0], a["dt_bias_bwd"][0], z16]),
         np.concatenate([a["a_log_fwd"][0], a["a_log_bwd"][0], z16])], 1))
    out["flt_w1"] = np.ascontiguousarray(a["flt_w1_2"][0])
    out["flt_w2"] = np.ascontiguousarray(a["flt_w2_2"][0])
    out["flt_w3"] = np.ascontiguousarray(a["flt_w3_2"][0])
    out["flt_vec"] = np.ascontiguousarray(
        np.stack([a["flt_b1_2"][0], a["flt_b2_2"][0], a["flt_freq_2"][0]], 1))
    table, _, z, win, hm = shape_constants()
    out["const"], out["flt_z"], out["flt_win"], out["hg_mask"] = table, z, win, hm
    return out


class Phase:

    def __init__(self, name, n, items, tiles, first=0, turn=None, done=0):
        self.done = done
        self.name, self.n, self.items, self.tiles = name, n, items, tiles
        self.first = first
        self.turn, self.late = turn, False
        self.ipb, self.tpb = len(items), len(tiles)
        assert self.ipb % RAW == 0
        self.walk = [(k, kt, kt == 0, kt == kb - 1) for k, kb in enumerate(tiles) for kt in range(kb)]
        at = 0
        self.blocks = []
        for _, nb in items:
            self.blocks.append(self.walk[at:at + nb])
            at += nb
        self.evac = [[] for _ in items]
        if tiles:
            assert at == len(self.walk)
            for t, bl in enumerate(self.blocks):
                for k, _, _, last in bl:
                    if last:
                        self.evac[(t + 1) % self.ipb].append((-1 if t + 1 == self.ipb else 0, k))

    def tile_number(self, i, k):
        return i * self.tpb + (self.t0 + k)

    def tile_done(self, i, k):
        t = next(t for t, bl in enumerate(self.blocks) for b in bl if b[0] == k and b[3])
        return i * self.ipb + (self.g0 + t + 1)

    def bank_free_after(self, i, k):
        if k >= 3:
            return self.tile_number(i, k - 3) + 1
        if isinstance(i, int) and i == 0:
            return self.t0
        last = max(q for q in range(self.tpb) if q % 3 == k % 3) if self.tpb > k else 0
        return (i - 1) * self.tpb + (self.t0 + last + 1)


def phases():
    ps = [
        Phase("gate", 1, [("w_gate", 2)] * 8, [KT]),
        Phase("one", NH, [("w_delta", 8)] * 8 + [("w_dil", 6)] * 24, [KT] * 13),
        Phase("out", 4, [("w_out", 8)] * 8, [KT] * 4),
    ]
    for t0, n in FFN_PARTS:
        ps.append(Phase("up", n // 2, [("w_up", 8)] * 8, [KT] * 4, first=t0 // 2, done=t0))
        ps.append(Phase("down", 4, [(f"w_down_{t0}", n // 2)] * 8, [n] * 4))
    ps.append(Phase("ada", 12, [("w_ada", 8)] * 16, []))
    ps.append(Phase("ctx", NH, [("w_ctx", 6)] * 8, [KT] * 3))
    ps.append(Phase("two", NH, [("w_hg", 5)] * 16 + [("w_hy", 6)] * 8, [KT] * 8, turn=NH // 2))
    ps.append(Phase("out2", 4, [("w_out2", 8)] * 8, [KT] * 4))
    for t0, n in MLP_PARTS:
        ps.append(Phase("mlp1", 4, [("w_mlp1", 8)] * 8, [KT] * 4, first=t0 // 4, done=t0))
        ps.append(Phase("mlp2", 4, [("w_mlp2", 8)] * 8, [n] * 4, first=t0 // 4))
    g = t = 0
    for p, q in zip(ps, ps[1:] + [None]):
        p.g0, p.t0, p.next = g, t, q
        g += p.n * p.ipb
        t += p.n * p.tpb
    return ps


def build(nc, io, out_dram, stop=None):
    import concourse.bass as bass

    PH = phases()
    table, cols, _, _, _ = shape_constants()
    NCONST = table.shape[1]
    es = ExitStack()
    with es:
        def sb(name, shape, dt=F32):
            return es.enter_context(nc.sbuf_tensor(name, shape, dt))

        sems = {}

        def sem(name):
            if name not in sems:
                sems[name] = es.enter_context(nc.semaphore(name))
            return sems[name]

        def wait(eng, name, value):
            if not (isinstance(value, int) and value <= 0):
                eng.wait_ge(sem(name), value)

        class Chain:

            def __init__(self, name, per=None):
                self.name, self.per = name, per

            def begin(self, eng, i):
                assert self.per is not None or (isinstance(i, int) and i == 0), self.name
                self.eng, self.i, self.k = eng, i, 0

            def step(self, ins):
                ins.then_inc(sem(self.name), 1)
                self.k += 1

            def settle(self):
                i0 = 0 if self.per is None else self.i * self.per
                self.eng.wait_ge(sem(self.name), i0 + self.k)

            def end(self):
                assert self.per in (None, self.k), (self.name, self.per, self.k)
                self.per = self.k

        raw = sb("raw", [P, RAW, NB * P])
        w_hi = sb("w_hi", [P, SPLIT, NB * P], F32R)
        w_lo = sb("w_lo", [P, SPLIT, NB * P], F32R)
        act_a = sb("act_a", [P, KT, 2 * S], F32R)
        act_b = sb("act_b", [P, KT, 2 * S], F32R)
        half = sb("half", [P, 3, S])
        gains = sb("gains_sb", [P, 192])
        mod = sb("mod", [P, 2, 96])
        eye1 = sb("eye1", [P, 2 * P])
        WORK = 18560
        work = sb("work", [P, WORK])
        x = work[:, 0:KT * S].rearrange("p (k t) -> p k t", k=KT)

        class Area:

            def __init__(self, at=0):
                self.at = at

            def take(self, *shape):
                n = int(np.prod(shape))
                v = work[:, self.at:self.at + n]
                self.at += n
                assert self.at <= WORK, (self.at, WORK)
                if len(shape) == 2:
                    v = v.rearrange("p (a b) -> p a b", a=shape[0])
                elif len(shape) == 3:
                    v = v.rearrange("p (a b c) -> p a b c", a=shape[0], b=shape[1])
                elif len(shape) == 4:
                    v = v.rearrange("p (a b c d) -> p a b c d", a=shape[0], b=shape[1], c=shape[2])
                return v

        acc = es.enter_context(nc.psum_tensor("acc", [P, 3, 512], F32))
        mix = es.enter_context(nc.psum_tensor("mixp", [P, 5, 512], F32))
        ident, ones = eye1[:, 0:P], eye1[:, P:2 * P]
        A2 = lambda v, **k: v.rearrange("p (a b) -> p a b", **k)

        def raw_loaded(g0, i, ipb, t):
            return (i * (ipb // RAW)) * 16 + ((g0 + t) // RAW + 1) * 16

        def load_items(sp, ph, i, t):
            name, nb = ph.items[t]
            same = [q for q, (nm, _) in enumerate(ph.items) if nm == name]
            src = io[name][(i + ph.first) * len(same) + (t - same[0])]
            wait(sp, "lo_ready", i * ph.ipb + (ph.g0 + t + 1 - RAW))
            sp.dma_start(raw[:, t % RAW, 0:nb * P], src)\
              .then_inc(sem(f"raw_loaded{t % RAW}"), 16)

        def split_hi(act, ph, i, t):
            nb = ph.items[t][1]
            wait(act, f"raw_loaded{t % RAW}", raw_loaded(ph.g0, i, ph.ipb, t))
            wait(act, "item_used", i * ph.ipb + (ph.g0 + t + 1 - SPLIT))
            act.activation(w_hi[:, t % SPLIT, 0:nb * P], raw[:, t % RAW, 0:nb * P], ACT.Copy)\
               .then_inc(sem("hi_ready"), 1)

        def split_lo(dve, ph, i, t):
            nb = ph.items[t][1]
            wait(dve, "hi_ready", i * ph.ipb + (ph.g0 + t + 1))
            dve.tensor_tensor(w_lo[:, t % SPLIT, 0:nb * P], raw[:, t % RAW, 0:nb * P],
                              w_hi[:, t % SPLIT, 0:nb * P], ALU.subtract).then_inc(sem("lo_ready"), 1)

        def bodies(eng, ph, body):
            ph.late = False
            body(0, True, ph.n == 1)
            at = 1
            for late, end in ((False, ph.turn), (True, ph.n - 1)):
                if end is not None and end > at:
                    ph.late = late
                    with eng.Fori(at, end) as i:
                        body(i, False, False)
                    at = end
            if ph.n > 1:
                body(ph.n - 1, False, True)

        def hop(live, q):
            for _, rate, gen in live:
                if q < rate:
                    next(gen, None)

        def run_out(gen):
            for _ in gen:
                pass

        class Mixers:

            def __init__(self, plan):
                self.plan = plan

            def start(self, t, i, first):
                got = []
                for at, length, rate, fn, off in self.plan:
                    if at == t and not (first and off < 0):
                        got.append([at + length, rate, fn(i + off)])
                return got

            def finish(self, n):
                for _, _, _, fn, off in self.plan:
                    if off < 0:
                        run_out(fn(n - 1))

        def drive(eng, ph, split, evac, mixers):
            def body(i, first, last):
                live = []
                for t in range(ph.ipb):
                    if t + AHEAD < ph.ipb:
                        split(eng, ph, i, t + AHEAD)
                    elif not last:
                        split(eng, ph, i + 1, t + AHEAD - ph.ipb)
                    elif ph.next:
                        split(eng, ph.next, 0, t + AHEAD - ph.ipb)
                    for off, k in ph.evac[t]:
                        if not (first and off < 0):
                            evac(i + off, k)
                    live = [m for m in live if m[0] > t] + mixers.start(t, i, first)
                    for q in range(2):
                        hop(live, q)
                    for m in live:
                        if m[0] == t + 1:
                            assert next(m[2], "end") == "end", ph.name
            bodies(eng, ph, body)
            for off, k in ph.evac[0]:
                if off < 0:
                    evac(ph.n - 1, k)
            mixers.finish(ph.n)

        def drive_pe(pe, ph, block, mixers):
            def body(i, first, last):
                live = []
                for t in range(ph.ipb):
                    nb = ph.items[t][1]
                    wait(pe, "lo_ready", i * ph.ipb + (ph.g0 + t + 1))
                    live = [m for m in live if m[0] > t] + mixers.start(t, i, first)
                    cuts, ins = [nb * q // 2 for q in range(3)], None
                    for q in range(2):
                        for b in range(cuts[q], cuts[q + 1]):
                            ins = block(i, t, b) or ins
                        if q == 1:
                            ins.then_inc(sem("item_used"), 1)
                        hop(live, q)
            bodies(pe, ph, body)
            mixers.finish(ph.n)

        def gemm_block(pe, ph, src):
            def block(i, t, b):
                k, kt, first, last = ph.blocks[t][b]
                if first:
                    wait(pe, "tile_out", ph.bank_free_after(i, k))
                wh = w_hi[:, t % SPLIT, b * P:(b + 1) * P]
                wl = w_lo[:, t % SPLIT, b * P:(b + 1) * P]
                bank = acc[:, k % 3, :]
                if last:
                    pe.matmul(bank[:, 0:S], wl, src[:, kt, 0:S], start=False, stop=False)
                    ins = pe.matmul(bank, wh, src[:, kt, :], start=False, stop=True)
                else:
                    pe.matmul(bank, wh, src[:, kt, :], start=first, stop=False)
                    ins = pe.matmul(bank[:, 0:S], wl, src[:, kt, 0:S], start=False, stop=False)
                return ins
            return block

        ends = {"pe": 0, "act": 0, "dve": 0}
        LATER = NH + 1

        def act_half(act, ph, scale=None):
            def evac(i, k):
                wait(act, "item_used", ph.tile_done(i, k))
                kw = {} if scale is None else {"scale": scale(i, k)}
                act.activation(half[:, k % 3, :], acc[:, k % 3, S:2 * S], ACT.Copy, **kw)\
                   .then_inc(sem("half_ready"), 1)
            return evac

        def dve_whole(dve, ph, dst, order=None):
            def evac(i, k):
                wait(dve, "half_ready", ph.tile_number(i, k) + 1)
                a, b = acc[:, k % 3, 0:S], half[:, k % 3, :]
                o = dst(i, k)
                if order is not None and order(i, k):
                    a = a.rearrange("p (r c) -> p c r", c=64)
                    b = b.rearrange("p (r c) -> p c r", c=64)
                    o = o.rearrange("p (c r) -> p c r", r=4)
                dve.tensor_tensor(o, a, b, ALU.add).then_inc(sem("tile_out"), 1)
            return evac

        class Norm:

            count = splits = 0

            def __init__(self, src, gain, dst, shift=None, plain=None):
                ar = Area(WORK - 4096)
                self.sq, self.u = ar.take(2, 512), ar.take(4, S)
                self.v, self.y, self.t, self.h = [ar.take(S) for _ in range(4)]
                self.src, self.gain, self.dst, self.shift, self.plain = src, gain, dst, shift, plain
                self.n = Norm.count
                Norm.count += 1
                self.m = Norm.splits
                Norm.splits += plain is None
                self.chain = "norm_dve_steps"

            def pe(self, pe):
                n = self.n
                for j in range(8):
                    wait(pe, "norm_square", 8 * n + j + 1)
                    pe.matmul(mix[:, 0, :], ones, self.sq[:, j % 2, :], start=(j == 0), stop=(j == 7))\
                      .then_inc(sem("norm_summed"), 1)

            def act(self, act):
                n = self.n
                for j in range(8):
                    if j >= 2:
                        wait(act, "norm_summed", 8 * n + j - 1)
                    act.activation(self.sq[:, j % 2, :], self.src[:, 2 * j:2 * j + 2, :], ACT.Square)\
                       .then_inc(sem("norm_square"), 1)
                wait(act, "norm_summed", 8 * n + 8)
                act.activation(self.h, mix[:, 0, S:2 * S], ACT.Copy).then_inc(sem("norm_half"), 1)
                wait(act, "norm_mean", n + 1)
                act.activation(self.t, self.v, ACT.Ln).then_inc(sem("norm_act_steps"), 1)
                act.wait_ge(sem("norm_act_steps"), n + 1)
                act.activation(self.y, self.t, ACT.Exp, scale=-0.5).then_inc(sem("norm_guess"), 1)
                for j in range(KT if self.plain is None else 0):
                    wait(act, "norm_scaled", KT * n + j + 1)
                    kw = {} if self.shift is None else {"bias": self.shift[:, j:j + 1]}
                    act.activation(self.dst[:, j, 0:S], self.u[:, j % 4, :],
                                   ACT.Copy if self.shift is None else ACT.Identity, **kw)\
                       .then_inc(sem("norm_hi"), 1)

            def dve(self, dve):
                n, c = self.n, sem(self.chain)
                k = 4 * n
                wait(dve, "norm_half", n + 1)
                dve.tensor_tensor(self.v, mix[:, 0, 0:S], self.h, ALU.add).then_inc(c, 1)
                dve.wait_ge(c, k + 1)
                dve.tensor_scalar(self.v, self.v, 1.0 / D, EPS, ALU.mult, ALU.add)\
                   .then_inc(sem("norm_mean"), 1)
                wait(dve, "norm_guess", n + 1)
                dve.tensor_tensor(self.t, self.y, self.y, ALU.mult).then_inc(c, 1)
                dve.wait_ge(c, k + 2)
                dve.scalar_tensor_tensor(self.t, self.t, -0.5, self.v, ALU.mult, ALU.mult).then_inc(c, 1)
                dve.wait_ge(c, k + 3)
                dve.scalar_tensor_tensor(self.y, self.t, 1.5, self.y, ALU.add, ALU.mult).then_inc(c, 1)
                dve.wait_ge(c, k + 4)

                def lo(j):
                    wait(dve, "norm_hi", KT * self.m + j + 1)
                    if self.shift is None:
                        dve.tensor_tensor(self.dst[:, j, S:2 * S], self.u[:, j % 4, :],
                                          self.dst[:, j, 0:S], ALU.subtract)\
                           .then_inc(sem("norm_lo"), 1)
                    else:
                        dve.scalar_tensor_tensor(self.dst[:, j, S:2 * S], self.u[:, j % 4, :],
                                                 self.shift[:, j:j + 1], self.dst[:, j, 0:S],
                                                 ALU.add, ALU.subtract).then_inc(sem("norm_lo"), 1)
                for j in range(KT):
                    if self.plain is None and j >= 4:
                        wait(dve, "norm_lo", KT * self.m + j - 3)
                    o = self.u[:, j % 4, :] if self.plain is None else self.plain[:, j, :]
                    dve.scalar_tensor_tensor(o, self.src[:, j, :], self.gain[:, j:j + 1], self.y,
                                             ALU.mult, ALU.mult).then_inc(sem("norm_scaled"), 1)
                    if self.plain is None and j >= 2:
                        lo(j - 2)
                if self.plain is None:
                    lo(KT - 2)
                    lo(KT - 1)

        def rsqrt_act(act, ch, v, y, t, scale, bias, ready):
            ch.step(act.activation(t, v, ACT.Ln, scale=scale, bias=bias))
            ch.settle()
            act.activation(y, t, ACT.Exp, scale=-0.5).then_inc(sem(ready), 1)

        def newton(ch, dve, v, y, t, w, scale, bias):
            ch.step(dve.tensor_scalar(w, v, scale, bias, ALU.mult, ALU.add))
            ch.step(dve.tensor_tensor(t, y, y, ALU.mult))
            ch.settle()
            ch.step(dve.scalar_tensor_tensor(t, t, -0.5, w, ALU.mult, ALU.mult))
            ch.settle()
            ch.step(dve.scalar_tensor_tensor(t, t, 1.5, y, ALU.add, ALU.mult))
            ch.settle()

        def bc(v, n):
            return v.unsqueeze(1).to_broadcast([v.shape[0], n, v.shape[1]])

        def const(ar, name):
            at, n = cols[name]
            v = ar.take(n)
            return v, (v, io["const"][:, at:at + n])

        g_scr = nc.dram_tensor("gate_rows", (NH, 4, S), F32, kind="Internal").ap()
        k_scr = nc.dram_tensor("filter_spectra", (NH, P, 4 * P), F32, kind="Internal").ap()
        x_scr = nc.dram_tensor("residual", (P, KT, S), F32, kind="Internal").ap()

        ar = Area(KT * S)
        ada_c, ada_th, ada_lo = ar.take(KT, 2), ar.take(KT, 2), ar.take(KT, 2)
        ada_sel, ld_sel = const(ar, "sel")
        ada_row = ar.take(512)
        ctx_tok = x
        lbl = ar.take(2, 2, NH)
        stat = act_a[:, :, 0:P]

        def ada_prologue_act(act):
            act.wait_ge(sem("c_loaded"), 16)
            act.activation(ada_th, ada_c, ACT.Tanh, scale=0.5).then_inc(sem("c_steps"), 1)
            act.wait_ge(sem("c_steps"), 3)
            act.wait_ge(sem("stat_clear"), 1)
            act.activation(stat[:, :, 0:2], ada_c, ACT.Copy).then_inc(sem("c_steps"), 1)
            act.wait_ge(sem("c_lo"), 1)

        def ada_prologue_dve(dve):
            dve.memset(act_a[:, :, 0:P].bitcast(F32), 0.0).then_inc(sem("stat_clear"), 1)
            dve.wait_ge(sem("c_steps"), 1)
            dve.scalar_tensor_tensor(ada_c, ada_th, 1.0, ada_c, ALU.add, ALU.mult)\
               .then_inc(sem("c_steps"), 1)
            dve.wait_ge(sem("c_steps"), 2)
            dve.tensor_scalar(ada_c, ada_c, 0.5, None, ALU.mult).then_inc(sem("c_steps"), 1)
            dve.wait_ge(sem("c_steps"), 4)
            dve.tensor_tensor(stat[:, :, 2:4], ada_c, stat[:, :, 0:2], ALU.subtract)\
               .then_inc(sem("c_lo"), 1)

        def ada_block(pe, ph):
            def block(i, t, b):
                if b % 4:
                    return None
                kt, bank = (2 * t + b // 4) % KT, acc[:, t // 8, :]
                if kt == 0:
                    wait(pe, "ada_row_ready", i * 2 + (t // 8 - 1))
                ws = slice(b * P, (b + 4) * P)
                pe.matmul(bank, stat[:, kt, :], w_hi[:, t % SPLIT, ws], start=(kt == 0), stop=False)
                ins = pe.matmul(bank, stat[:, kt, :], w_lo[:, t % SPLIT, ws], start=False,
                                stop=(kt == KT - 1))
                return ins
            return block

        def ada_mix_pe(pe, part):
            def gen(i):
                wait(pe, "ada_row_ready", i * 2 + (part + 1))
                wait(pe, "ada_mod", i * 2 + part)
                for c in range(4):
                    ins = pe.matmul(mix[:, 0, 2 * c:2 * c + 2], ada_row[0:4, c * P:(c + 1) * P],
                                    ada_sel[0:4, :], start=True, stop=True)
                ins.then_inc(sem("ada_turned"), 1)
                yield
            return gen

        def ada_mix_act(act, part):
            def gen(i):
                wait(act, "item_used", i * 16 + (PHD["ada"].g0 + 8 * part + 8))
                wait(act, "ada_turned", i * 2 + part)
                act.activation(ada_row[0:4, :], acc[0:4, part, :], ACT.Copy)\
                   .then_inc(sem("ada_row_ready"), 1)
                yield
            return gen

        def ada_mix_dve(dve, part):
            def gen(i):
                wait(dve, "ada_turned", i * 2 + (part + 1))
                b = gains[:, bass.ds(i * 8 + (96 + 4 * part), 4)]
                dve.tensor_tensor(mod[:, :, bass.ds(i * 8 + 4 * part, 4)],
                                  mix[:, 0, 0:8].rearrange("p (c v) -> p v c", v=2),
                                  bc(b, 2), ALU.add).then_inc(sem("ada_mod"), 1)
                yield
            return gen

        ar = Area(KT * S)
        s0 = ar.take(NH, 2, HD)
        lbs = ar.take(NH, 2, 3)
        two_base = ar.at
        lbt = ar.take(2, 2, NH)
        c_z = ar.take(3, S)
        c_p = ar.take(2, 3)
        c_th, c_kk, c_lf, c_w = ar.take(2, S), ar.take(2, S), ar.take(2, S), ar.take(2, S)
        c_one = ar.take(S)
        c_cum = ar.take(2, S + 1)
        c_vT, c_kT = ar.take(2, P), ar.take(4, P)
        c_d = Chain("ctx_dve_steps", per=5)

        def ctx_prologue_act(act):
            act.wait_ge(sem("lb_handoff"), 1)
            act.activation(lbt[:, 1], lbt[:, 0], ACT.Tanh, scale=0.5).then_inc(sem("lb_handoff"), 1)

        def ctx_prologue_dve(dve):
            dve.wait_ge(sem("small2_loaded"), 16 * 2)
            dve.tensor_tensor(lbt[:, 0], lbl[:, :, 0, :], lbl[:, :, 1, :], ALU.subtract)\
               .then_inc(sem("lb_handoff"), 1)
            dve.wait_ge(sem("lb_handoff"), 2)
            v = lambda k: lbs[:, :, :, k].rearrange("p h d -> p d h")
            dve.tensor_scalar(v(0), lbt[:, 1], -0.25, 0.25, ALU.mult, ALU.add)
            dve.tensor_scalar(v(1), lbt[:, 1], 0.25, 0.75, ALU.mult, ALU.add)
            dve.tensor_scalar(v(2), lbt[:, 1], 0.25, -0.25, ALU.mult, ALU.add)
            dve.memset(c_one, 1.0)
            dve.memset(c_cum, 0.0).then_inc(sem("ctx_ready"), 1)
            dve.wait_ge(sem("ctx_ready"), 1)

        def ctx_mix_act(act):
            def gen(i):
                wait(act, "tile_out", PHD["ctx"].tile_number(i, 1) + 1)
                act.activation(c_th, c_z[:, 0:2, :], ACT.Tanh, scale=0.5).then_inc(sem("hgrn_tanh"), 1)
                yield
                wait(act, "hgrn_par", i + 1)
                act.wait_ge(sem("hgrn_tanh"), i + 1)
                for d in range(2):
                    ins = act.activation(c_lf[:, d, :], c_th[:, d, :], ACT.Ln, scale=c_p[:, d, 0:1],
                                         bias=c_p[:, d, 1:2])
                ins.then_inc(sem("hgrn_log"), 1)
                yield
                yield
                wait(act, "ctx_cum", i + 1)
                act.activation(c_w[:, 0, :], c_cum[:, 0, 1:S + 1], ACT.Exp)
                act.activation(c_w[:, 1, :], c_cum[:, 1, 0:S], ACT.Exp).then_inc(sem("ctx_decay"), 1)
                yield
                yield
                wait(act, "hgrn_kT", i + 1)
                act.activation(c_kT, mix[:, 1, :].rearrange("p (a b) -> p a b", a=4), ACT.Copy)\
                   .then_inc(sem("hgrn_kT_out"), 1)
                yield
                yield
                yield
            return gen

        def ctx_mix_dve(dve):
            ch = c_d

            def gen(i):
                ch.begin(dve, i)
                dve.tensor_copy(c_p, lbs[:, bass.ds(i, 1), :, :].squeeze(1)).then_inc(sem("hgrn_par"), 1)
                yield
                wait(dve, "hgrn_vT", i + 1)
                ch.step(dve.tensor_copy(c_vT, A2(mix[:, 0, 0:2 * P], a=2)))
                wait(dve, "hgrn_tanh", i + 1)
                dve.wait_ge(sem("hgrn_par"), i + 1)
                for d in range(2):
                    ch.step(dve.tensor_scalar(c_kk[:, d, :], c_th[:, d, :], c_p[:, d, 2:3],
                                              c_p[:, d, 0:1], ALU.mult, ALU.add))
                yield
                wait(dve, "hgrn_log", i + 1)
                ch.step(dve.tensor_tensor_scan(c_cum[:, 0, 0:S][:, ::-1], c_one, c_lf[:, 0, ::-1], 0.0,
                                               ALU.mult, ALU.add))
                dve.tensor_tensor_scan(c_cum[:, 1, 1:S + 1], c_one, c_lf[:, 1, :], 0.0,
                                       ALU.mult, ALU.add).then_inc(sem("ctx_cum"), 1)
                yield
                wait(dve, "ctx_decay", i + 1)
                ch.settle()
                dve.tensor_tensor(c_w, c_w, c_kk, ALU.mult).then_inc(sem("ctx_kw"), 1)
                yield
                yield
                yield
                yield
                wait(dve, "ctx_state", i + 1)
                ch.step(dve.tensor_copy(s0[:, bass.ds(i, 1), :, :].squeeze(1),
                                        A2(mix[:, 2, 0:2 * P], a=2)))
                yield
                ch.end()
            return gen

        def ctx_mix_pe(pe):
            def gen(i):
                wait(pe, "tile_out", PHD["ctx"].tile_number(i, 2) + 1)
                for k in range(2):
                    ins = pe.transpose(mix[:, 0, k * P:(k + 1) * P], c_z[:, 2, k * P:(k + 1) * P], ident)
                ins.then_inc(sem("hgrn_vT"), 1)
                yield
                yield
                yield
                yield
                wait(pe, "ctx_kw", i + 1)
                for d in range(2):
                    for k in range(2):
                        ins = pe.transpose(mix[:, 1, (2 * d + k) * P:(2 * d + k + 1) * P],
                                           c_w[:, d, k * P:(k + 1) * P], ident)
                ins.then_inc(sem("hgrn_kT"), 1)
                yield
                yield
                wait(pe, "hgrn_kT_out", i + 1)
                for d in range(2):
                    for k in range(2):
                        ins = pe.matmul(mix[:, 2, d * P:(d + 1) * P], c_kT[:, 2 * d + k, :],
                                        c_vT[:, k, :], start=(k == 0), stop=(k == 1))
                ins.then_inc(sem("ctx_state"), 1)
                yield
                yield
            return gen

        ar = Area(0)
        d_t, dl = ar.take(4, S), ar.take(9, S)
        dil_mask, ld_dil = const(ar, "dil")
        rope_cs, rope_sn = ar.take(S), ar.take(S)
        dl_vT = ar.take(6, P)
        r0 = ar.at
        dl_p, dl_pT = ar.take(6, S), ar.take(6, S)
        one_alt = Area(r0)
        d_bc, d_e, d_x, d_z = one_alt.take(2, 2, S), one_alt.take(2, 2, S), one_alt.take(4, P), \
            one_alt.take(4, P)
        d_bq, d_y = ar.take(2, 2, S), ar.take(4, P)
        d_bv, d_bk, d_kt = ar.take(4, P), ar.take(2, P), ar.take(2, P)
        d_wn, d_v1, d_v2 = ar.take(2, P), ar.take(2, P), ar.take(2, P)
        d_s, d_qd = ar.take(2, P), ar.take(2, P)
        d_c = ar.take(3, S)
        d_th = ar.take(3, S)
        d_kq = ar.take(2, S)
        lev, ld_lev = const(ar, "level")
        neg, ld_neg = const(ar, "neg")
        d_par, d_gt = ar.take(NH, 16), ar.take(NH, 16)
        d_hp, d_gs = ar.take(16), ar.take(16)
        dl_m = ar.take(2, 4)
        g_par = ar.take(2)
        g_row = ar.take(S)
        ar = Area(r0)
        tri, ld_tri = const(ar, "tri")
        gsign, ld_gsign = const(ar, "gsign")
        ropef, ld_ropef = const(ar, "ropef")
        ropes, ld_ropes = const(ar, "ropes")
        g_x, g_a, g_b, g_l = [ar.take(S) for _ in range(4)]
        g_T, g_T2, g_tot = ar.take(2, 32), ar.take(2, 32), ar.take(2, 16)
        g_na = ar.take(2)
        r_ang, r_k, r_cos, r_sin = [ar.take(S) for _ in range(4)]
        r_pos = ar.take(S)
        assert ar.at <= r0 + 6000
        GQ = dict(g=0, b=4, gb=8, tail=12)

        def gate_dve(dve):
            c = sem("gate_dve_steps")
            n = [0]

            def do(ins):
                ins.then_inc(c, 1)
                n[0] += 1

            def settle():
                dve.wait_ge(c, n[0])
            R = slice(0, 32)
            dve.wait_ge(sem("one_loaded"), 16 * ONE_LOADS)
            do(dve.tensor_copy(r_ang[R], r_pos[R].bitcast(I32)))
            settle()
            do(dve.tensor_scalar(r_ang[R], r_ang[R], ropef[R, 0:1], None, ALU.mult))
            settle()
            MAGIC = 12582912.0
            two_pi = 2 * np.pi
            c1 = float(np.float32(6.28125))
            c2 = float(np.float32(two_pi - c1))
            c3 = float(np.float32(two_pi - c1 - c2))
            for out, shift in ((r_cos, 0.25), (r_sin, 0.0)):
                do(dve.tensor_scalar(r_k[R], r_ang[R], float(1 / two_pi), shift, ALU.mult, ALU.add))
                settle()
                do(dve.tensor_scalar(r_k[R], r_k[R], MAGIC, None, ALU.add))
                settle()
                do(dve.tensor_scalar(r_k[R], r_k[R], MAGIC, None, ALU.subtract))
                settle()
                do(dve.scalar_tensor_tensor(out[R], r_k[R], -c1, r_ang[R], ALU.mult, ALU.add))
                settle()
                do(dve.scalar_tensor_tensor(out[R], r_k[R], -c2, out[R], ALU.mult, ALU.add))
                settle()
                do(dve.scalar_tensor_tensor(out[R], r_k[R], -c3, out[R], ALU.mult, ALU.add))
                settle()
                do(dve.tensor_scalar(out[R], out[R], float(shift * two_pi), 3.1415925, ALU.add, ALU.min))
                settle()
                ins = dve.tensor_scalar(out[R], out[R], -3.1415925, None, ALU.max)
                ins.then_inc(sem("rope_angle"), 1)
            dve.wait_ge(sem("rope_sine"), 2)
            do(dve.tensor_scalar(rope_sn[R], rope_sn[R], ropes[R, 0:1], None, ALU.mult))

            wait(dve, "tile_out", PHD["gate"].t0 + 1)
            do(dve.tensor_scalar(g_x[R], d_t[R, 0, :], gsign[R, 0:1], g_par[R, 0:1], ALU.mult, ALU.add))
            settle()
            do(dve.tensor_scalar(g_b[R], g_x[R], 0.0, None, ALU.max))
            dve.scalar_tensor_tensor(g_a[R], g_x[R], -1.0, g_x[R], ALU.mult, ALU.min)\
               .then_inc(sem("gate_minus_abs"), 1)
            dve.wait_ge(sem("gate_soft"), 1)
            do(dve.tensor_tensor(g_b[R], g_b[R], g_l[R], ALU.add))
            do(dve.tensor_scalar(g_na[R, 1:2], g_na[R, 0:1], -1.0, None, ALU.mult))
            settle()
            dve.tensor_scalar(g_l[R], g_b[R], g_na[R, 1:2], None, ALU.mult).then_inc(sem("gate_handoff"), 1)
            dve.wait_ge(sem("gate_handoff"), 2)
            dve.tensor_copy(g_T, A2(mix[:, 0, 0:64], a=2)).then_inc(sem("gate_handoff"), 1)
            dve.wait_ge(sem("gate_handoff"), 4)
            for k in range(2):
                f = mix[:, 1, 64 * k:64 * k + 8]
                b = mix[:, 1, 64 * k + 40:64 * k + 48]
                do(dve.tensor_copy(g_T2[:, k, 0:8], f))
                do(dve.tensor_copy(g_T2[:, k, 8:16], b))
                do(dve.tensor_copy(g_tot[:, k, :], mix[:, 1, 128 + 32 * k:128 + 32 * k + 16]))
            settle()
            dve.tensor_tensor(g_T2[:, :, 16:32], g_T2[:, :, 0:16], g_T[:, :, 16:32], ALU.add)\
               .then_inc(sem("gate_handoff"), 1)
            dve.wait_ge(sem("gate_handoff"), 5)

            def hv(kind):
                return d_gt[:, :, GQ[kind]:GQ[kind] + 4].rearrange("p h (d k) -> p k d h", d=2)

            def tv(v, at):
                return v[:, :, at:at + 16].rearrange("p k (d h) -> p k d h", d=2)
            for k in range(2):
                do(dve.tensor_scalar(hv("g")[:, k], tv(g_T2, 0)[:, k], -1.0, None, ALU.mult))
                do(dve.tensor_copy(hv("b")[:, k], tv(g_T, 16)[:, k]))
                do(dve.tensor_copy(hv("gb")[:, k], tv(g_T2, 16)[:, k]))
                do(dve.tensor_tensor(hv("tail")[:, k], tv(g_tot, 0)[:, k], tv(g_T2, 0)[:, k],
                                     ALU.subtract))
            settle()
            dve.wait_ge(sem("gate_handoff"), 6)
            dve.tensor_copy(g_row[R], mix[0:32, 2, 0:S]).then_inc(sem("gate_row_out"), 1)
            dve.wait_ge(sem("gate_exp"), 1)
            dve.tensor_scalar(d_gt[:, :, 4:8], d_gt[:, :, 4:8], 0.5, None, ALU.mult)\
               .then_inc(sem("gate_done"), 1)

        def gate_act(act):
            R = slice(0, 32)
            for k, (out, a) in enumerate(((rope_cs, r_cos), (rope_sn, r_sin))):
                wait(act, "rope_angle", k + 1)
                act.activation(out[R], a[R], ACT.Sin).then_inc(sem("rope_sine"), 1)
            act.wait_ge(sem("gate_minus_abs"), 1)
            act.activation(g_a[R], g_a[R], ACT.Exp).then_inc(sem("gate_act_steps"), 1)
            act.activation(g_na[R, 0:1], g_par[R, 1:2], ACT.Exp).then_inc(sem("gate_act_steps"), 1)
            act.wait_ge(sem("gate_act_steps"), 2)
            act.activation(g_l[R], g_a[R], ACT.Ln, bias=1.0).then_inc(sem("gate_soft"), 1)
            act.wait_ge(sem("gate_row_out"), 1)
            act.activation(d_gt[:, :, 4:16], d_gt[:, :, 4:16], ACT.Exp).then_inc(sem("gate_exp"), 1)

        def gate_pe(pe):
            pe.wait_ge(sem("gate_handoff"), 1)
            for k in range(2):
                ins = pe.transpose(mix[:, 0, 32 * k:32 * k + 32], g_l[0:32, k * P:(k + 1) * P],
                                   ident[0:32, 0:32])
            ins.then_inc(sem("gate_handoff"), 1)
            pe.wait_ge(sem("gate_handoff"), 3)
            for k in range(2):
                for d in range(2):
                    pe.matmul(mix[:, 1, 64 * k + 32 * d:64 * k + 32 * d + 32],
                              tri[:, d * P:(d + 1) * P], g_T[:, k, :], start=True, stop=True)
                ins = pe.matmul(mix[:, 1, 128 + 32 * k:128 + 32 * k + 32], ones, g_T[:, k, :],
                                start=True, stop=True)
            ins.then_inc(sem("gate_handoff"), 1)
            pe.wait_ge(sem("gate_handoff"), 5)
            for k in range(2):
                ins = pe.transpose(mix[0:32, 2, k * P:(k + 1) * P], g_T2[:, k, :], ident)
            ins.then_inc(sem("gate_handoff"), 1)

        FIRST, SECOND = (0, 1), (1, 0)
        dd = {n: Chain(f"delta_{n}_steps") for n in ("act", "dve")}

        def delta_act(act):
            ch = dd["act"]

            def gen(i):
                ch.begin(act, i)
                yield
                wait(act, "delta_conv", i + 1)
                act.activation(d_th, d_c, ACT.Tanh, scale=0.5).then_inc(sem("delta_tanh"), 1)
                yield
                wait(act, "delta_silu", i + 1)
                act.activation(d_th[:, 0:2, :], d_c[:, 0:2, :], ACT.Square, scale=0.5)\
                   .then_inc(sem("delta_square"), 1)
                yield
                wait(act, "delta_norm", i + 1)
                rsqrt_act(act, ch, A2(mix[:, 0, :], a=2), d_kq, d_e[:, 0, :, :], 1.0, EPS,
                          "delta_guess")
                yield
                wait(act, "delta_diff", i + 1)
                act.activation(d_e, d_e, ACT.Exp).then_inc(sem("delta_gamma"), 1)
                for d in range(2):
                    k = SECOND[d]
                    ins = act.activation(d_wn[:, d, :], d_bc[:, d, 1, k * P:(k + 1) * P], ACT.Exp)
                ins.then_inc(sem("delta_eg"), 1)
                wait(act, "delta_turned", i + 1)
                kT = lambda k: mix[:, 1, k * P:(k + 1) * P]
                vT = lambda k: mix[:, 1, (2 + k) * P:(3 + k) * P]
                for d in range(2):
                    for k in range(2):
                        g = GQ["b"] + 2 * d + k
                        act.activation(d_bv[:, 2 * d + k, :], vT(k), ACT.Copy, scale=d_gs[:, g:g + 1])
                    g = GQ["gb"] + 2 * d + SECOND[d]
                    act.activation(d_bk[:, d, :], kT(SECOND[d]), ACT.Copy, scale=d_gs[:, g:g + 1])
                    g = GQ["tail"] + 2 * d + FIRST[d]
                    ins = act.activation(d_kt[:, d, :], kT(FIRST[d]), ACT.Copy, scale=d_gs[:, g:g + 1])
                ins.then_inc(sem("delta_TM"), 1)
                yield
                for s in range(14):
                    yield
                wait(act, "delta_v1", i + 1)
                act.activation(d_wn, A2(mix[:, 3, 2 * P:4 * P], a=2), ACT.Copy, scale=-1.0)\
                   .then_inc(sem("delta_wn"), 1)
                act.activation(d_th[:, 2, :], d_t[:, 3, :], ACT.Tanh, scale=0.5)\
                   .then_inc(sem("rule_gtanh"), 1)
                yield
                yield
                yield
                wait(act, "rule_o", i + 1)
                act.activation(d_th[:, 0, :], mix[:, 0, 0:S], ACT.Square).then_inc(sem("rule_osq"), 1)
                yield
                wait(act, "rule_onorm", i + 1)
                rsqrt_act(act, ch, mix[:, 1, 0:S], d_y[:, 0:2, :].rearrange("p a b -> p (a b)"),
                          d_y[:, 2:4, :].rearrange("p a b -> p (a b)"), 1.0 / HD, EPS, "rule_guess")
                yield
                wait(act, "rule_out", i + 1)
                act.activation(act_b[:, bass.ds(i, 1), 0:S].squeeze(1), d_c[:, 0, :], ACT.Copy)\
                   .then_inc(sem("rule_hi"), 1)
                yield
                ch.end()
            return gen

        def delta_dve(dve):
            ch = dd["dve"]

            def gen(i):
                ch.begin(dve, i)
                wait(dve, "rule_hi", i)
                ch.step(dve.tensor_copy(d_hp, d_par[:, bass.ds(i, 1), :].squeeze(1)))
                ch.step(dve.tensor_copy(d_gs, d_gt[:, bass.ds(i, 1), :].squeeze(1)))
                ch.settle()
                for c in range(3):
                    ch.step(dve.tensor_scalar(d_c[:, c, :], d_t[:, c, :], d_hp[:, 5 * c + 2:5 * c + 3],
                                              None, ALU.mult))
                for j in (0, 1, 3, 4):
                    s = j - 2
                    o = slice(max(0, -s), S - max(0, s))
                    a = slice(max(0, s), S + min(0, s))
                    ch.settle()
                    for c in range(3):
                        ins = dve.scalar_tensor_tensor(d_c[:, c, o], d_t[:, c, a],
                                                       d_hp[:, 5 * c + j:5 * c + j + 1], d_c[:, c, o],
                                                       ALU.mult, ALU.add)
                        if j < 4:
                            ch.step(ins)
                ins.then_inc(sem("delta_conv"), 1)
                yield
                wait(dve, "delta_tanh", i + 1)
                dve.scalar_tensor_tensor(d_c, d_th, 1.0, d_c, ALU.add, ALU.mult)\
                   .then_inc(sem("delta_silu"), 1)
                yield
                yield
                wait(dve, "delta_guess", i + 1)
                ch.step(dve.tensor_scalar(d_bq[:, 0, :, :], A2(mix[:, 0, :], a=2), EPS, None, ALU.add))
                y, t, w = d_kq, d_bq[:, 1, :, :], d_bq[:, 0, :, :]
                ch.step(dve.tensor_tensor(t, y, y, ALU.mult))
                ch.settle()
                ch.step(dve.scalar_tensor_tensor(t, t, -0.5, w, ALU.mult, ALU.mult))
                ch.settle()
                ch.step(dve.scalar_tensor_tensor(t, t, 1.5, y, ALU.add, ALU.mult))
                ch.settle()
                ch.step(dve.scalar_tensor_tensor(d_kq[:, 0, :], d_c[:, 1, :], 0.5, t[:, 1, :],
                                                 ALU.mult, ALU.mult))
                dve.scalar_tensor_tensor(d_kq[:, 1, :], d_c[:, 0, :], 0.5 * HD ** -0.5, t[:, 0, :],
                                         ALU.mult, ALU.mult).then_inc(sem("delta_kq"), 1)
                wait(dve, "bc_loaded", i * 16 + 16)
                for d in range(2):
                    for k in range(2):
                        ins = dve.scalar_tensor_tensor(
                            d_e[:, d, :, k * P:(k + 1) * P], d_bc[:, d, :, k * P:(k + 1) * P],
                            d_gs[:, 2 * d + k:2 * d + k + 1],
                            A2(neg[:, 2 * d * P:(2 * d + 2) * P], a=2), ALU.add, ALU.add)
                ins.then_inc(sem("delta_diff"), 1)
                yield
                wait(dve, "delta_gamma", i + 1)
                wait(dve, "delta_gram", i + 1)
                for d in range(2):
                    for kind in range(2):
                        g = mix[:, 2, :].rearrange("p (k c j) -> p k c j", k=2, c=2)[:, :, kind, :]
                        dve.tensor_tensor(A2(d_bq[:, d, kind, :], a=2), A2(d_e[:, d, kind, :], a=2), g,
                                          ALU.mult)
                wait(dve, "delta_eg", i + 1)
                wait(dve, "delta_kq", i + 1)
                for d in range(2):
                    k = SECOND[d]
                    dve.tensor_tensor(d_qd[:, d, :], d_kq[:, 1, k * P:(k + 1) * P], d_wn[:, d, :],
                                      ALU.mult)
                dve.tensor_copy(d_x, bc(ident, 4)).then_inc(sem("delta_bq"), 1)
                yield
                for s in range(7):
                    wait(dve, "delta_ax", i * 7 + (s + 1))
                    dve.tensor_tensor(d_y, A2(mix[:, 2, :], a=4), bc(lev[:, s * P:(s + 1) * P], 4),
                                      ALU.mult).then_inc(sem("delta_y"), 1)
                    yield
                    wait(dve, "delta_xy", i * 7 + (s + 1))
                    z0 = bc(ident, 4) if s == 0 else d_z
                    ins = dve.tensor_tensor(d_z, z0, A2(mix[:, 4, :], a=4), ALU.subtract)
                    if s < 6:
                        xy = d_y if s == 0 else A2(mix[:, 3, :], a=4)
                        ins = dve.tensor_tensor(d_x, d_x, xy, ALU.subtract)
                    ins.then_inc(sem("delta_level"), 1)
                    yield
                wait(dve, "delta_first", i + 1)
                dve.tensor_copy(d_v1, A2(mix[:, 3, 0:2 * P], a=2)).then_inc(sem("delta_v1"), 1)
                yield
                wait(dve, "delta_st", i + 1)
                dve.tensor_copy(d_s, A2(mix[:, 4, 0:2 * P], a=2)).then_inc(sem("delta_s"), 1)
                yield
                wait(dve, "delta_second", i + 1)
                dve.tensor_copy(d_v2, A2(mix[:, 2, 0:2 * P], a=2)).then_inc(sem("delta_v2"), 1)
                yield
                wait(dve, "rule_gtanh", i + 1)
                ch.step(dve.scalar_tensor_tensor(d_c[:, 1, :], d_th[:, 2, :], 1.0, d_t[:, 3, :],
                                                 ALU.add, ALU.mult))
                yield
                wait(dve, "rule_guess", i + 1)
                y = d_y[:, 0:2, :].rearrange("p a b -> p (a b)")
                w = d_y[:, 2:4, :].rearrange("p a b -> p (a b)")
                newton(ch, dve, mix[:, 1, 0:S], y, d_th[:, 1, :], w, 1.0 / HD, EPS)
                ch.step(dve.scalar_tensor_tensor(d_c[:, 0, :], mix[:, 0, 0:S], d_hp[:, 15:16],
                                                 d_th[:, 1, :], ALU.mult, ALU.mult))
                ch.settle()
                dve.scalar_tensor_tensor(d_c[:, 0, :], d_c[:, 0, :], 0.5, d_c[:, 1, :], ALU.mult,
                                         ALU.mult).then_inc(sem("rule_out"), 1)
                yield
                wait(dve, "rule_hi", i + 1)
                o = act_b[:, bass.ds(i, 1), :].squeeze(1)
                ch.step(dve.tensor_tensor(o[:, S:2 * S], d_c[:, 0, :], o[:, 0:S], ALU.subtract))
                yield
                ch.end()
            return gen

        def delta_pe(pe):
            def gen(i):
                yield
                yield
                yield
                wait(pe, "dil_lo", i)
                wait(pe, "delta_square", i + 1)
                pe.matmul(mix[:, 0, :], ones, d_th[:, 0:2, :], start=True, stop=True)\
                  .then_inc(sem("delta_norm"), 1)
                yield
                wait(pe, "delta_kq", i + 1)
                for k in range(2):
                    pe.transpose(mix[:, 1, k * P:(k + 1) * P], d_kq[:, 0, k * P:(k + 1) * P], ident)
                for k in range(2):
                    ins = pe.transpose(mix[:, 1, (2 + k) * P:(3 + k) * P], d_c[:, 2, k * P:(k + 1) * P],
                                       ident)
                ins.then_inc(sem("delta_turned"), 1)
                for k in range(2):
                    ins = pe.matmul(mix[:, 2, 2 * k * P:2 * (k + 1) * P], d_kq[:, 0, k * P:(k + 1) * P],
                                    d_kq[:, :, k * P:(k + 1) * P], start=True, stop=True)
                ins.then_inc(sem("delta_gram"), 1)
                yield
                for s in range(7):
                    if s == 0:
                        wait(pe, "delta_bq", i + 1)
                    else:
                        wait(pe, "delta_level", i * 7 + s)
                    for m in range(4):
                        b = d_bq[:, m // 2, 0, (m % 2) * P:(m % 2 + 1) * P]
                        ins = pe.matmul(mix[:, 2, m * P:(m + 1) * P], b, d_x[:, m, :], start=True,
                                        stop=True)
                    ins.then_inc(sem("delta_ax"), 1)
                    yield
                    wait(pe, "delta_y", i * 7 + (s + 1))
                    for m in range(4):
                        z = d_z[:, m, :] if s else ident
                        if 0 < s < 6:
                            pe.matmul(mix[:, 3, m * P:(m + 1) * P], z, d_y[:, m, :], start=True,
                                      stop=True)
                        ins = pe.matmul(mix[:, 4, m * P:(m + 1) * P], d_y[:, m, :], z, start=True,
                                        stop=True)
                    ins.then_inc(sem("delta_xy"), 1)
                    yield
                wait(pe, "delta_level", i * 7 + 7)
                wait(pe, "delta_TM", i + 1)
                for d in range(2):
                    pe.matmul(mix[:, 3, d * P:(d + 1) * P], d_z[:, 2 * d + FIRST[d], :],
                              d_bv[:, 2 * d + FIRST[d], :], start=True, stop=True)
                    ins = pe.matmul(mix[:, 3, (2 + d) * P:(3 + d) * P], d_bk[:, d, :],
                                    d_z[:, 2 * d + SECOND[d], :], start=True, stop=True)
                ins.then_inc(sem("delta_first"), 1)
                yield
                wait(pe, "delta_v1", i + 1)
                for d in range(2):
                    ins = pe.matmul(mix[:, 4, d * P:(d + 1) * P], d_kt[:, d, :], d_v1[:, d, :],
                                    start=True, stop=True)
                ins.then_inc(sem("delta_st"), 1)
                yield
                wait(pe, "delta_s", i + 1)
                wait(pe, "delta_wn", i + 1)
                for d in range(2):
                    pe.matmul(mix[:, 2, d * P:(d + 1) * P], d_z[:, 2 * d + SECOND[d], :],
                              d_bv[:, 2 * d + SECOND[d], :], start=True, stop=False)
                    ins = pe.matmul(mix[:, 2, d * P:(d + 1) * P], d_wn[:, d, :], d_s[:, d, :],
                                    start=False, stop=True)
                ins.then_inc(sem("delta_second"), 1)
                yield
                wait(pe, "delta_v2", i + 1)
                for k in range(2):
                    o, ks = mix[:, 0, k * P:(k + 1) * P], slice(k * P, (k + 1) * P)
                    f, b = (0, 1) if k == 0 else (1, 0)
                    pe.matmul(o, d_v1[:, f, :], d_bq[:, f, 1, ks], start=True, stop=False)
                    pe.matmul(o, d_s[:, b, :], d_qd[:, b, :], start=False, stop=False)
                    ins = pe.matmul(o, d_v2[:, b, :], d_bq[:, b, 1, ks], start=False, stop=True)
                ins.then_inc(sem("rule_o"), 1)
                yield
                wait(pe, "rule_osq", i + 1)
                pe.matmul(mix[:, 1, 0:S], ones, d_th[:, 0, :], start=True, stop=True)\
                  .then_inc(sem("rule_onorm"), 1)
                yield
                yield
            return gen

        dl_d = Chain("dil_dve_steps", per=6)

        def dil_dve(dve):
            ch = dl_d

            def gen(i):
                ch.begin(dve, i)
                R = slice(0, 32)
                qk, t1, t2 = dl[R, 0:6, :], dl_p[R], dl_pT[R]
                ch.step(dve.tensor_tensor(t1, qk, bc(rope_cs[R], 6), ALU.mult))
                ch.step(dve.stream_shuffle(t2, qk, [(m + 16) % 32 for m in range(32)]))
                ch.settle()
                ch.step(dve.tensor_tensor(t2, t2, bc(rope_sn[R], 6), ALU.mult))
                ch.settle()
                dve.tensor_tensor(qk, t1, t2, ALU.add).then_inc(sem("dil_rope"), 1)
                yield
                wait(dve, "dil_scores", i + 1)
                ch.step(dve.scalar_tensor_tensor(
                    dl_p.rearrange("p a b -> p (a b)"), mix[:, 0:3, :].rearrange("p a b -> p (a b)"),
                    HD ** -0.5, dil_mask, ALU.mult, ALU.add))
                yield
                ch.settle()
                ch.step(dve.tensor_reduce(dl_m[:, :, 0], dl_p.rearrange("p (q b) s -> p q (b s)", q=2),
                                          AX.X, ALU.max))
                ch.settle()
                dve.tensor_scalar(dl_m[:, :, 1], dl_m[:, :, 0], -1.0, None, ALU.mult)\
                   .then_inc(sem("dil_max"), 1)
                yield
                yield
                wait(dve, "dil_exp", i + 1)
                ch.step(dve.reciprocal(dl_m[:, :, 3], dl_m[:, :, 2]))
                ch.settle()
                for q in range(2):
                    ins = dve.tensor_scalar(dl_p[:, 3 * q:3 * q + 3, :], dl_p[:, 3 * q:3 * q + 3, :],
                                            dl_m[:, q, 3:4], None, ALU.mult)
                ins.then_inc(sem("dil_probs"), 1)
                yield
                wait(dve, "dil_turned", i + 1)
                dve.tensor_copy(dl_pT[:, 4:6, :], A2(mix[:, 2, :], a=2))\
                   .then_inc(sem("dil_pT_dve"), 1)
                yield
                wait(dve, "pair_hi", i + 1)
                o = act_b[:, bass.ds(i + NH, 1), S:2 * S].squeeze(1)
                dve.tensor_tensor(o, mix[:, 3, 0:S], act_b[:, bass.ds(i + NH, 1), 0:S].squeeze(1),
                                  ALU.subtract).then_inc(sem("dil_lo"), 1)
                yield
                ch.end()
            return gen

        def dil_act(act):
            def gen(i):
                yield
                wait(act, "dil_vT", i + 1)
                v = mix[:, 3:5, :].rearrange("p a (b c) -> p (a b) c", b=4)
                act.activation(dl_vT, v[:, 0:6, :], ACT.Copy).then_inc(sem("dil_vT_out"), 1)
                yield
                yield
                wait(act, "dil_max", i + 1)
                for q in range(2):
                    ins = act.activation(dl_p[:, 3 * q:3 * q + 3, :], dl_p[:, 3 * q:3 * q + 3, :],
                                         ACT.Exp, bias=dl_m[:, q, 1:2], accum_out=dl_m[:, q, 2:3])
                ins.then_inc(sem("dil_exp"), 1)
                yield
                yield
                wait(act, "dil_turned", i + 1)
                act.activation(dl_pT[:, 0:4, :],
                               mix[:, 0:2, :].rearrange("p a (b c) -> p (a b) c", b=2),
                               ACT.Copy).then_inc(sem("dil_pT_act"), 1)
                yield
                wait(act, "dil_out", i + 1)
                act.activation(act_b[:, bass.ds(i + NH, 1), 0:S].squeeze(1), mix[:, 3, 0:S], ACT.Copy)\
                   .then_inc(sem("pair_hi"), 1)
                yield
            return gen

        def dil_pe(pe):
            def gen(i):
                yield
                wait(pe, "dil_rope", i + 1)
                for q in range(2):
                    for b in range(3):
                        m = 3 * q + b
                        ins = pe.matmul(mix[:, m // 2, (m % 2) * S:(m % 2 + 1) * S],
                                        dl[:, b, q * P:(q + 1) * P], dl[:, 3 + b, :], start=True,
                                        stop=True)
                ins.then_inc(sem("dil_scores"), 1)
                for m in range(6):
                    ins = pe.transpose(mix[:, 3 + m // 4, (m % 4) * P:(m % 4 + 1) * P],
                                       dl[:, 6 + m // 2, (m % 2) * P:(m % 2 + 1) * P], ident)
                ins.then_inc(sem("dil_vT"), 1)
                yield
                yield
                yield
                yield
                wait(pe, "dil_probs", i + 1)
                for m in range(6):
                    for q in range(2):
                        at = (m % 2) * S + q * P
                        ins = pe.transpose(mix[:, m // 2, at:at + P],
                                           dl_p[:, 3 * q + m // 2, (m % 2) * P:(m % 2 + 1) * P], ident)
                ins.then_inc(sem("dil_turned"), 1)
                yield
                wait(pe, "dil_pT_dve", i + 1)
                wait(pe, "dil_pT_act", i + 1)
                wait(pe, "dil_vT_out", i + 1)
                for m in range(6):
                    ins = pe.matmul(mix[:, 3, 0:S], dl_vT[:, m, :], dl_pT[:, m, :], start=(m == 0),
                                    stop=(m == 5))
                ins.then_inc(sem("dil_out"), 1)
                yield
            return gen

        ar = Area(KT * S)
        up, cv, u_th = ar.take(4, S), ar.take(4, S), ar.take(2, S)
        ffn_par = ar.take(44, 6)

        def up_dve(dve, ph):
            def gen(i):
                wait(dve, "tile_out", ph.tile_number(i, 3) + 1)
                for pr in range(2):
                    n = ph.done + pr
                    w = [ffn_par[:, bass.ds(i * 2 + n, 1), :].squeeze(1)[:, c:c + 1]
                         for c in range(6)]
                    c0 = 2 * pr
                    k = sem("up_dve_steps")
                    for h in range(2):
                        ins = dve.tensor_scalar(cv[:, c0 + h, :], up[:, c0 + h, :], w[3 * h + 1], None,
                                                ALU.mult)
                    ins.then_inc(k, 1)
                    dve.wait_ge(k, (i * 2 + n) * 2 + 1)
                    for h in range(2):
                        ins = dve.scalar_tensor_tensor(cv[:, c0 + h, 1:S], up[:, c0 + h, 0:S - 1],
                                                       w[3 * h], cv[:, c0 + h, 1:S], ALU.mult, ALU.add)
                    ins.then_inc(k, 1)
                    dve.wait_ge(k, (i * 2 + n) * 2 + 2)
                    for h in range(2):
                        ins = dve.scalar_tensor_tensor(cv[:, c0 + h, 0:S - 1], up[:, c0 + h, 1:S],
                                                       w[3 * h + 2], cv[:, c0 + h, 0:S - 1], ALU.mult,
                                                       ALU.add)
                    ins.then_inc(sem("up_conv"), 1)
                    yield
                    wait(dve, "up_tanh", i * 2 + (n + 1))
                    dve.scalar_tensor_tensor(cv[:, c0, :], u_th[:, pr, :], 1.0, cv[:, c0, :], ALU.add,
                                             ALU.mult).then_inc(sem("up_silu"), 1)
                    dve.wait_ge(sem("up_silu"), i * 2 + (n + 1))
                    dve.scalar_tensor_tensor(cv[:, c0, :], cv[:, c0, :], 0.5, cv[:, c0 + 1, :],
                                             ALU.mult, ALU.mult).then_inc(sem("up_prod"), 1)
                    yield
                    wait(dve, "up_hi", i * 2 + (n + 1))
                    o = act_b[:, bass.ds(i * 2 + pr, 1), :].squeeze(1)
                    dve.tensor_tensor(o[:, S:2 * S], cv[:, c0, :], o[:, 0:S], ALU.subtract)\
                       .then_inc(sem("up_lo"), 1)
                    yield
                    yield
            return gen

        def up_act(act, ph):
            def gen(i):
                for pr in range(2):
                    n = ph.done + pr
                    wait(act, "up_conv", i * 2 + (n + 1))
                    act.activation(u_th[:, pr, :], cv[:, 2 * pr, :], ACT.Tanh, scale=0.5)\
                       .then_inc(sem("up_tanh"), 1)
                    yield
                    wait(act, "up_prod", i * 2 + (n + 1))
                    act.activation(act_b[:, bass.ds(i * 2 + pr, 1), 0:S].squeeze(1), cv[:, 2 * pr, :],
                                   ACT.Copy).then_inc(sem("up_hi"), 1)
                    yield
                    yield
                    yield
            return gen

        def nothing(eng, hops):
            def gen(i):
                for _ in range(hops):
                    yield
            return gen

        def mlp_dve(dve, ph):
            def gen(i):
                n = ph.done // 4
                wait(dve, "tile_out", ph.tile_number(i, 3) + 1)
                dve.scalar_tensor_tensor(cv, up, 0.0, up, ALU.max, ALU.mult)\
                   .then_inc(sem("mlp_square"), 1)
                yield
                wait(dve, "mlp_hi", i + (n + 1))
                o = act_b[:, bass.ds(i * 4, 4), :]
                dve.tensor_tensor(o[:, :, S:2 * S], cv, o[:, :, 0:S], ALU.subtract)\
                   .then_inc(sem("mlp_lo"), 1)
                yield
            return gen

        def mlp_act(act, ph):
            def gen(i):
                n = ph.done // 4
                wait(act, "mlp_square", i + (n + 1))
                act.activation(act_b[:, bass.ds(i * 4, 4), 0:S], cv, ACT.Copy)\
                   .then_inc(sem("mlp_hi"), 1)
                yield
                yield
            return gen

        ar = Area(KT * S + 2048 + 1024)
        part = ar.take(2, S)

        def dve_residual(dve, ph, gate=None):
            def evac(i, k):
                n = ph.tile_number(i, k)
                wait(dve, "half_ready", n + 1)
                a, b, t = acc[:, k % 3, 0:S], half[:, k % 3, :], part[:, k % 2, :]
                if gate is None:
                    ins = dve.tensor_tensor(t, a, b, ALU.add)
                else:
                    ins = dve.scalar_tensor_tensor(t, a, gate(i, k), b, ALU.mult, ALU.add)
                ins.then_inc(sem("tile_out"), 1)
                wait(dve, "tile_out", n + 1)
                xt = x[:, bass.ds(i * 4 + k, 1), :].squeeze(1)
                dve.tensor_tensor(xt, xt, t, ALU.add)
            return evac

        ar = Area(0)
        h_z, y_t = ar.take(5, S), ar.take(3, S)
        dft, ld_dft = const(ar, "dft")
        idft, ld_idft = const(ar, "idft")
        assert ar.at <= KT * S
        ar = Area(two_base)
        y_rs, y_ss, y_par, h_gain = ar.take(NH), ar.take(NH), ar.take(NH, 13), ar.take(NH)
        h_reset, ld_reset = const(ar, "reset")
        h_reset = A2(h_reset, a=2)
        pro_base = ar.at
        h_mask = ar.take(4, P)
        h_p, h_g1 = ar.take(2, 3), ar.take(1)
        h_th, h_lf, h_kk, h_a = ar.take(2, S), ar.take(2, S), ar.take(2, S), ar.take(2, S)
        h_e1, h_e2, h_e3, h_e4, h_qa = [ar.take(2, S) for _ in range(5)]
        h_sc, h_vT, h_kT = ar.take(4, P), ar.take(2, P), ar.take(4, P)
        h_s = ar.take(2, 4, P)
        h_o = ar.take(3, S)
        y_hp = ar.take(13)
        y_rs1 = ar.take(1)
        y_c, y_u, y_uT, y_k, y_y, y_w = ar.take(3, S), ar.take(S), ar.take(2, P), ar.take(4, P), \
            ar.take(4, P), ar.take(4, P)
        hh = {n: Chain(f"hg_{n}_steps") for n in ("act", "dve")}

        def update_place(d, c):
            at = [(dd_, cc) for dd_ in range(2) for cc in range(3)
                  if (cc if dd_ == 0 else 3 - cc) % 2 == (c if d == 0 else 3 - c) % 2].index((d, c))
            return mix[:, 3 + (c if d == 0 else 3 - c) % 2, at * P:(at + 1) * P]

        MID, END = (31, 32), (63, 0)

        ar = Area(pro_base)
        f_z, f_w1, f_w2, f_w3, f_vec = ar.take(S), ar.take(64), ar.take(64), ar.take(2048), ar.take(3)
        f_nf, ld_nf = const(ar, "notfirst")
        f_win = ar.take(2, 1024)
        f_h, f_r, f_h2 = ar.take(S), ar.take(S), ar.take(S)
        f_a, f_b, f_q = ar.take(2, 512), ar.take(2, 512), ar.take(2, 512)
        f_t = ar.take(512)
        f_k = ar.take(4, 512)
        two_pro_end = ar.at
        assert two_pro_end <= WORK

        def filter_dve(dve):
            c, n = sem("filter_dve_steps"), [0]

            def do(ins):
                ins.then_inc(c, 1)
                n[0] += 1

            def settle():
                dve.wait_ge(c, n[0])
            R = slice(0, 64)
            dve.wait_ge(sem("two_loaded"), 16 * TWO_LOADS)
            MAGIC = 12582912.0
            two_pi = 2 * np.pi
            c1 = float(np.float32(6.28125))
            c2 = float(np.float32(two_pi - c1))
            for layer in range(2):
                dve.wait_ge(sem("filter_pre"), layer + 1)
                do(dve.tensor_scalar(f_h[R], mix[0:64, 0, 0:S], f_vec[R, layer:layer + 1],
                                     f_vec[R, 2:3], ALU.add, ALU.mult))
                settle()
                do(dve.tensor_scalar(f_r[R], f_h[R], float(1 / two_pi), None, ALU.mult))
                settle()
                do(dve.tensor_scalar(f_r[R], f_r[R], MAGIC, None, ALU.add))
                settle()
                do(dve.tensor_scalar(f_r[R], f_r[R], MAGIC, None, ALU.subtract))
                settle()
                do(dve.scalar_tensor_tensor(f_h[R], f_r[R], -c1, f_h[R], ALU.mult, ALU.add))
                settle()
                do(dve.scalar_tensor_tensor(f_h[R], f_r[R], -c2, f_h[R], ALU.mult, ALU.add))
                settle()
                dve.tensor_scalar(f_h[R], f_h[R], 3.1415925, -3.1415925, ALU.min, ALU.max)\
                   .then_inc(sem("filter_arg"), 1)
            for cb in range(2):
                for k in range(2):
                    win = f_win[:, k, cb * 512:(cb + 1) * 512]
                    m = 2 * cb + k
                    dve.wait_ge(sem("filter_taps"), m + 1)
                    if k == 0 and cb:
                        dve.wait_ge(sem("filter_spec"), 1)
                        dve.wait_ge(sem("filter_power"), 1)
                    do(dve.tensor_tensor(f_t, mix[:, 0, :], win, ALU.mult))
                    do(dve.scalar_tensor_tensor(f_q[:, k, :], mix[:, 1, :], f_nf[:, k:k + 1], win,
                                                ALU.mult, ALU.mult))
                    settle()
                    do(dve.tensor_tensor(f_a[:, k, :], f_t, f_q[:, k, :], ALU.add))
                    do(dve.tensor_tensor(f_b[:, k, :], f_t, f_q[:, k, :], ALU.subtract))
                    do(dve.tensor_tensor(f_t, f_t, f_t, ALU.mult))
                    do(dve.tensor_tensor(f_q[:, k, :], f_q[:, k, :], f_q[:, k, :], ALU.mult))
                    settle()
                    dve.tensor_tensor(f_q[:, k, :], f_q[:, k, :], f_t, ALU.add)\
                       .then_inc(sem("filter_ab"), 1)
                dve.wait_ge(sem("filter_power"), cb + 1)
                dve.tensor_copy(y_ss[:, 4 * cb:4 * cb + 4], mix[:, 4, 0:4]).then_inc(sem("filter_norm"), 1)
            dve.wait_ge(sem("filter_norm"), 4)
            t, u = f_t[:, 0:NH], f_t[:, 16:16 + NH]
            do(dve.tensor_tensor(u, y_rs, y_rs, ALU.mult))
            settle()
            do(dve.scalar_tensor_tensor(u, u, -0.5, y_ss, ALU.mult, ALU.mult))
            settle()
            do(dve.scalar_tensor_tensor(y_rs, u, 1.5, y_rs, ALU.add, ALU.mult))
            settle()

        def filter_act(act):
            R = slice(0, 64)
            act.wait_ge(sem("filter_arg"), 1)
            act.activation(f_h2[R], f_h[R], ACT.Sin).then_inc(sem("filter_sin"), 1)
            act.wait_ge(sem("filter_arg"), 2)
            act.activation(f_h2[R], f_h[R], ACT.Sin).then_inc(sem("filter_sin"), 1)
            for cb in range(2):
                act.wait_ge(sem("filter_spec"), cb + 1)
                if cb:
                    act.wait_ge(sem("spec_stored"), 16 * 4)
                act.activation(f_k, mix[:, 0:4, :], ACT.Copy).then_inc(sem("filter_spec_out"), 1)
            act.wait_ge(sem("filter_norm"), 2)
            act.activation(f_t[:, 32:32 + NH], y_ss, ACT.Ln).then_inc(sem("filter_norm"), 1)
            act.wait_ge(sem("filter_norm"), 3)
            act.activation(y_rs, f_t[:, 32:32 + NH], ACT.Exp, scale=-0.5)\
               .then_inc(sem("filter_norm"), 1)

        def filter_pe(pe):
            pe.wait_ge(sem("two_loaded"), 16 * TWO_LOADS)
            pe.matmul(mix[0:64, 0, 0:S], f_w1[0:33, :], f_z[0:33, :], start=True, stop=True)\
              .then_inc(sem("filter_pre"), 1)
            pe.wait_ge(sem("filter_sin"), 1)
            pe.matmul(mix[0:64, 0, 0:S], f_w2[0:64, :], f_h2[0:64, :], start=True, stop=True)\
              .then_inc(sem("filter_pre"), 1)
            pe.wait_ge(sem("filter_sin"), 2)
            for cb in range(2):
                for k in range(2):
                    m = 2 * cb + k
                    if m:
                        pe.wait_ge(sem("filter_ab"), m)
                    if cb and not k:
                        pe.wait_ge(sem("filter_spec_out"), cb)
                    for d in range(2):
                        at = d * 1024 + cb * 512
                        ins = pe.matmul(mix[:, d, :], f_h2[0:64, k * P:(k + 1) * P],
                                        f_w3[0:64, at:at + 512], start=True, stop=True)
                    ins.then_inc(sem("filter_taps"), 1)
                pe.wait_ge(sem("filter_ab"), 2 * cb + 2)
                for j in range(4):
                    for k in range(2):
                        ins = pe.matmul(mix[:, 4, j:j + 1], f_q[:, k, j * P:(j + 1) * P], ones[:, 0:1],
                                        start=(k == 0), stop=(k == 1))
                ins.then_inc(sem("filter_power"), 1)
                for part_, src in enumerate((f_a, f_b)):
                    for q in range(2):
                        for k in range(2):
                            at = k * 2 * S + part_ * S + q * P
                            ins = pe.matmul(mix[:, 2 * part_ + q, :], dft[:, at:at + P], src[:, k, :],
                                            start=(k == 0), stop=(k == 1))
                ins.then_inc(sem("filter_spec"), 1)

        def filter_sp(sp):
            for cb in range(2):
                sp.wait_ge(sem("filter_spec_out"), cb + 1)
                for j in range(4):
                    sp.dma_start(A2(k_scr[4 * cb + j], a=4), f_k[:, :, j * P:(j + 1) * P])\
                      .then_inc(sem("spec_stored"), 16)

        def hg_act(act):
            ch = hh["act"]

            def make(columns):
                def gen(i):
                    ch.begin(act, i)
                    wait(act, "tile_out", PHD["two"].tile_number(i, 2) + 1)
                    act.activation(h_th, h_z[:, 1:3, :], ACT.Tanh, scale=0.5).then_inc(sem("hgrn_tanh"), 1)
                    yield
                    wait(act, "hgrn_par", i + LATER)
                    act.wait_ge(sem("hgrn_tanh"), i + LATER)
                    for d in range(2):
                        ins = act.activation(h_lf[:, d, :], h_th[:, d, :], ACT.Ln,
                                             scale=h_p[:, d, 0:1], bias=h_p[:, d, 1:2])
                    ins.then_inc(sem("hgrn_log"), 1)
                    yield
                    yield
                    wait(act, "hg_exponents", i + 1)
                    act.activation(h_e1, h_lf, ACT.Exp)
                    act.activation(h_e2, h_lf, ACT.Exp, scale=-1.0)
                    act.activation(h_e4, h_a, ACT.Exp)
                    act.activation(h_e3, h_e3, ACT.Exp).then_inc(sem("hg_decays"), 1)
                    yield
                    wait(act, "hgrn_kT", i + LATER)
                    act.activation(h_kT, A2(mix[:, 2, :], a=4), ACT.Copy).then_inc(sem("hgrn_kT_out"), 1)
                    yield
                    yield
                    wait(act, "rule_o", i + LATER)
                    act.activation(h_o[:, 0, :], mix[:, 0, 0:S], ACT.Square).then_inc(sem("rule_osq"), 1)
                    act.activation(h_o[:, 1, :], h_z[:, 4, :], ACT.Tanh, scale=0.5)\
                       .then_inc(sem("rule_gtanh"), 1)
                    yield
                    wait(act, "rule_onorm", i + LATER)
                    rsqrt_act(act, ch, mix[:, 1, 0:S], h_e1[:, 0, :], h_e1[:, 1, :], 1.0 / HD, EPS,
                              "rule_guess")
                    yield
                    wait(act, "rule_out", i + LATER)
                    act.activation(act_b[:, bass.ds(i, 1), 0:S].squeeze(1), h_o[:, 0, :], ACT.Copy)\
                       .then_inc(sem("rule_hi"), 1)
                    yield
                    ch.end()
                return gen
            return make

        def hg_dve(dve):
            ch = hh["dve"]

            def make(columns):
                def gen(i):
                    ch.begin(dve, i)
                    ch.step(dve.tensor_copy(h_g1, h_gain[:, bass.ds(i, 1)]))
                    dve.tensor_copy(h_p, lbs[:, bass.ds(i, 1), :, :].squeeze(1))\
                       .then_inc(sem("hgrn_par"), 1)
                    wait(dve, "hgrn_vT", i + LATER)
                    dve.tensor_copy(h_vT, A2(mix[:, 0, 0:2 * P], a=2)).then_inc(sem("hg_vT_out"), 1)
                    yield
                    wait(dve, "hgrn_tanh", i + LATER)
                    dve.wait_ge(sem("hgrn_par"), i + LATER)
                    for d in range(2):
                        ch.step(dve.tensor_scalar(h_kk[:, d, :], h_th[:, d, :], h_p[:, d, 2:3],
                                                  h_p[:, d, 0:1], ALU.mult, ALU.add))
                    yield
                    wait(dve, "hgrn_log", i + LATER)
                    ch.step(dve.tensor_tensor_scan(h_a[:, 0, :], h_reset[:, 0, :], h_lf[:, 0, :], 0.0,
                                                   ALU.mult, ALU.add))
                    ch.step(dve.tensor_tensor_scan(h_a[:, 1, ::-1], h_reset[:, 1, ::-1],
                                                   h_lf[:, 1, ::-1], 0.0, ALU.mult, ALU.add))
                    ch.settle()
                    for d in range(2):
                        a = h_a[:, d, :].rearrange("p (c t) -> p c t", t=CH)
                        mid = a[:, :, MID[d]:MID[d] + 1].to_broadcast([P, 4, CH])
                        end = a[:, :, END[d]:END[d] + 1].to_broadcast([P, 4, CH])
                        dve.tensor_tensor(h_lf[:, d, :].rearrange("p (c t) -> p c t", t=CH), a, mid,
                                          ALU.subtract)
                        ins = dve.tensor_tensor(h_e3[:, d, :].rearrange("p (c t) -> p c t", t=CH), end,
                                                a, ALU.subtract)
                    ins.then_inc(sem("hg_exponents"), 1)
                    yield
                    wait(dve, "hg_decays", i + 1)
                    q = bc(h_z[:, 0, :], 2)
                    dve.tensor_tensor(h_e1, h_e1, q, ALU.mult)
                    dve.tensor_tensor(h_e2, h_e2, h_kk, ALU.mult)
                    dve.tensor_tensor(h_e3, h_e3, h_kk, ALU.mult)
                    dve.tensor_tensor(h_qa, h_e4, q, ALU.mult).then_inc(sem("hg_products"), 1)
                    yield
                    wait(dve, "hg_scores", i + 1)
                    ch.step(dve.tensor_copy(h_s[:, :, 0, :], s0[:, bass.ds(i, 1), :, :].squeeze(1)))
                    dve.copy_predicated(h_sc, h_mask.bitcast(I32), A2(mix[:, 1, :], a=4))\
                       .then_inc(sem("hg_masked"), 1)
                    yield
                    wait(dve, "hg_upd", i + 1)
                    ch.settle()
                    for c in range(3):
                        for d in range(2):
                            chunk = c if d == 0 else 3 - c
                            e = chunk * CH + END[d]
                            ins = dve.scalar_tensor_tensor(
                                h_s[:, d, c + 1, :], h_s[:, d, c, :], h_e4[:, d, e:e + 1],
                                update_place(d, c), ALU.mult, ALU.add)
                            if c < 2:
                                ch.step(ins)
                        if c < 2:
                            ch.settle()
                    ins.then_inc(sem("hg_states"), 1)
                    yield
                    wait(dve, "rule_gtanh", i + LATER)
                    ch.step(dve.scalar_tensor_tensor(h_o[:, 1, :], h_o[:, 1, :], 1.0, h_z[:, 4, :],
                                                     ALU.add, ALU.mult))
                    yield
                    wait(dve, "rule_guess", i + LATER)
                    newton(ch, dve, mix[:, 1, 0:S], h_e1[:, 0, :], h_e2[:, 0, :], h_e2[:, 1, :],
                           1.0 / HD, EPS)
                    ch.step(dve.scalar_tensor_tensor(h_e2[:, 1, :], mix[:, 0, 0:S], h_g1,
                                                     h_e2[:, 0, :], ALU.mult, ALU.mult))
                    ch.settle()
                    o, v, g = h_o[:, 0, :], h_e2[:, 1, :], h_o[:, 1, :]
                    if columns:
                        o = o.rearrange("p (r c) -> p c r", c=64)
                        g = g.rearrange("p (r c) -> p c r", c=64)
                        v = v.rearrange("p (c r) -> p c r", r=4)
                    dve.scalar_tensor_tensor(o, v, 0.5, g, ALU.mult, ALU.mult)\
                       .then_inc(sem("rule_out"), 1)
                    yield
                    wait(dve, "rule_hi", i + LATER)
                    o = act_b[:, bass.ds(i, 1), :].squeeze(1)
                    ch.step(dve.tensor_tensor(o[:, S:2 * S], h_o[:, 0, :], o[:, 0:S], ALU.subtract))
                    yield
                    ch.end()
                return gen
            return make

        def hg_pe(pe):
            def make(columns):
                def gen(i):
                    wait(pe, "tile_out", PHD["two"].tile_number(i, 3) + 1)
                    wait(pe, "hy_out", i)
                    for k in range(2):
                        ins = pe.transpose(mix[:, 0, k * P:(k + 1) * P], h_z[:, 3, k * P:(k + 1) * P],
                                           ident)
                    ins.then_inc(sem("hgrn_vT"), 1)
                    yield
                    yield
                    yield
                    yield
                    wait(pe, "hg_products", i + 1)
                    for m in range(4):
                        d, ks = m // 2, slice((m % 2) * P, (m % 2 + 1) * P)
                        ins = pe.matmul(mix[:, 1, m * P:(m + 1) * P], h_e2[:, d, ks], h_e1[:, d, ks],
                                        start=True, stop=True)
                    ins.then_inc(sem("hg_scores"), 1)
                    for m in range(4):
                        d, ks = m // 2, slice((m % 2) * P, (m % 2 + 1) * P)
                        ins = pe.transpose(mix[:, 2, m * P:(m + 1) * P], h_e3[:, d, ks], ident)
                    ins.then_inc(sem("hgrn_kT"), 1)
                    yield
                    wait(pe, "hgrn_kT_out", i + LATER)
                    wait(pe, "hg_vT_out", i + 1)
                    for m in range(6):
                        d, c = m // 3, m % 3
                        chunk = c if d == 0 else 3 - c
                        r = slice((chunk % 2) * CH, (chunk % 2 + 1) * CH)
                        ins = pe.matmul(update_place(d, c),
                                        h_kT[r, 2 * d + chunk // 2, :], h_vT[r, chunk // 2, :],
                                        start=True, stop=True)
                    ins.then_inc(sem("hg_upd"), 1)
                    yield
                    wait(pe, "hg_masked", i + 1)
                    wait(pe, "hg_states", i + 1)
                    for k in range(2):
                        o = mix[:, 0, k * P:(k + 1) * P]
                        for d in range(2):
                            pe.matmul(o, h_vT[:, k, :], h_sc[:, 2 * d + k, :], start=(d == 0),
                                      stop=False)
                        for chunk in (2 * k, 2 * k + 1):
                            oc = mix[:, 0, chunk * CH:(chunk + 1) * CH]
                            for d in range(2):
                                c = chunk if d == 0 else 3 - chunk
                                ins = pe.matmul(oc, h_s[:, d, c, :],
                                                h_qa[:, d, chunk * CH:(chunk + 1) * CH], start=False,
                                                stop=(chunk % 2 == 1 and d == 1))
                    ins.then_inc(sem("rule_o"), 1)
                    yield
                    wait(pe, "rule_osq", i + LATER)
                    pe.matmul(mix[:, 1, 0:S], ones, h_o[:, 0, :], start=True, stop=True)\
                      .then_inc(sem("rule_onorm"), 1)
                    yield
                    yield
                return gen
            return make

        yd = Chain("hy_dve_steps", per=18)

        def hy_dve(dve):
            ch = yd

            def gen(i):
                ch.begin(dve, i)
                ch.step(dve.tensor_copy(y_hp, y_par[:, bass.ds(i, 1), :].squeeze(1)))
                ch.step(dve.tensor_copy(y_rs1, y_rs[:, bass.ds(i, 1)]))
                ch.settle()
                for c in range(3):
                    ch.step(dve.tensor_scalar(y_c[:, c, :], y_t[:, c, :], y_hp[:, 3 * c + 1:3 * c + 2],
                                              y_hp[:, 9 + c:10 + c], ALU.mult, ALU.add))
                for j, o, a in ((0, slice(1, S), slice(0, S - 1)), (2, slice(0, S - 1), slice(1, S))):
                    ch.settle()
                    for c in range(3):
                        ch.step(dve.scalar_tensor_tensor(y_c[:, c, o], y_t[:, c, a],
                                                         y_hp[:, 3 * c + j:3 * c + j + 1], y_c[:, c, o],
                                                         ALU.mult, ALU.add))
                ch.settle()
                dve.tensor_tensor(y_u, y_c[:, 0, :], y_c[:, 1, :], ALU.mult).then_inc(sem("hy_u"), 1)
                yield
                wait(dve, "hy_uT", i + 1)
                dve.tensor_copy(y_uT, A2(mix[:, 0, 0:2 * P], a=2)).then_inc(sem("hy_uT_out"), 1)
                yield
                wait(dve, "hy_spec", i + 1)
                wait(dve, "spec_loaded", i * 16 + 16)
                u, f, y, w = A2(mix[:, 1, :], a=4), y_k, y_y, y_w
                C, N = slice(0, 2), slice(2, 4)
                ch.step(dve.tensor_tensor(y[:, C], u[:, C], f[:, C], ALU.mult))
                ch.step(dve.tensor_tensor(w[:, C], u[:, N], f[:, N], ALU.mult))
                ch.step(dve.tensor_tensor(y[:, N], u[:, C], f[:, N], ALU.mult))
                ch.step(dve.tensor_tensor(w[:, N], u[:, N], f[:, C], ALU.mult))
                ch.settle()
                dve.tensor_tensor(y[:, C], y[:, C], w[:, C], ALU.subtract)
                dve.tensor_tensor(y[:, N], y[:, N], w[:, N], ALU.add).then_inc(sem("hy_prod"), 1)
                yield
                wait(dve, "hy_back", i + 1)
                ch.step(dve.tensor_scalar(y_c[:, 0, :], mix[:, 2, 0:S], y_rs1, None, ALU.mult))
                ch.settle()
                ch.step(dve.scalar_tensor_tensor(y_c[:, 0, :], y_u, y_hp[:, 12:13], y_c[:, 0, :],
                                                 ALU.mult, ALU.add))
                ch.settle()
                dve.tensor_tensor(y_c[:, 0, :], y_c[:, 0, :], y_c[:, 2, :], ALU.mult)\
                   .then_inc(sem("hy_out"), 1)
                yield
                wait(dve, "pair_hi", i + LATER)
                o = act_b[:, bass.ds(i + NH, 1), :].squeeze(1)
                ch.step(dve.tensor_tensor(o[:, S:2 * S], y_c[:, 0, :], o[:, 0:S], ALU.subtract))
                yield
                ch.end()
            return gen

        def hy_act(act):
            def gen(i):
                for _ in range(3):
                    yield
                wait(act, "hy_out", i + 1)
                act.activation(act_b[:, bass.ds(i + NH, 1), 0:S].squeeze(1), y_c[:, 0, :], ACT.Copy)\
                   .then_inc(sem("pair_hi"), 1)
                yield
                yield
            return gen

        def hy_pe(pe):
            def gen(i):
                yield
                wait(pe, "rule_out", i + LATER)
                wait(pe, "hy_u", i + 1)
                for k in range(2):
                    ins = pe.transpose(mix[:, 0, k * P:(k + 1) * P], y_u[:, k * P:(k + 1) * P], ident)
                ins.then_inc(sem("hy_uT"), 1)
                yield
                wait(pe, "hy_uT_out", i + 1)
                for m in range(4):
                    for k in range(2):
                        at = k * 2 * S + m * P
                        ins = pe.matmul(mix[:, 1, m * P:(m + 1) * P], dft[:, at:at + P], y_uT[:, k, :],
                                        start=(k == 0), stop=(k == 1))
                ins.then_inc(sem("hy_spec"), 1)
                yield
                wait(pe, "hy_prod", i + 1)
                for m in range(4):
                    ins = pe.matmul(mix[:, 2, 0:S], y_y[:, m, :], idft[:, m * S:(m + 1) * S],
                                    start=(m == 0), stop=(m == 3))
                ins.then_inc(sem("hy_back"), 1)
                yield
                yield
            return gen

        PHD = {}
        for p_ in PH:
            PHD.setdefault(p_.name, p_)
        ups = [p_ for p_ in PH if p_.name == "up"]
        downs = [p_ for p_ in PH if p_.name == "down"]
        mlp1s = [p_ for p_ in PH if p_.name == "mlp1"]
        mlp2s = [p_ for p_ in PH if p_.name == "mlp2"]

        MEETS = ["normed_mix", "one_done", "out_done", "normed_ffn"]
        for k in range(len(ups)):
            MEETS += [f"up_done_{k}", f"down_done_{k}"]
        MEETS += ["normed_final", "ada_done", "normed_ctx", "ctx_done", "normed_two", "two_done",
                  "out2_done", "normed_mlp"]
        for k in range(len(mlp1s)):
            MEETS += [f"mlp1_done_{k}", f"mlp2_done_{k}"]
        MEETS += ["finished"]

        def at_meet(eng, name):
            eng.wait_ge(sem("phase_end"), 3 * (MEETS.index(name) + 1))

        def meet(eng, who, name):
            assert MEETS[ends[who]] == name, (name, MEETS[ends[who]])
            ends[who] += 1
            eng.drain().then_inc(sem("phase_end"), 1)
            eng.wait_ge(sem("phase_end"), 3 * ends[who])

        tokens_in = Area(WORK - 8192).take(KT, S)
        gm = sb("gain_mod", [P, 3, KT])
        norms = [
            Norm(tokens_in, gains[:, 0:16], act_a),
            Norm(x, gains[:, 16:32], act_a),
            Norm(x, gains[:, 32:48], None, plain=x),
            Norm(tokens_in, gm[:, 0, :], act_a, shift=mod[:, 1, 0:16]),
            Norm(x, gm[:, 1, :], act_a, shift=mod[:, 0, 0:16]),
            Norm(x, gm[:, 2, :], act_a, shift=mod[:, 0, 48:64]),
            Norm(x, gains[:, 80:96], None, plain=x),
        ]
        g1 = lambda i, k: mod[:, 0, bass.ds(i * 4 + (32 + k), 1)]
        g2 = lambda i, k: mod[:, 0, bass.ds(i * 4 + (80 + k), 1)]

        ONE = [ld_dil, ld_lev, ld_neg, ld_tri, ld_gsign, ld_ropef, ld_ropes,
               (d_par, io["delta_par"]), (g_par[0:32], io["gate_par"]),
               (r_pos[0:32].bitcast(I32), io["positions"][0].partition_broadcast(32))]
        TWO = [ld_dft, ld_idft, ld_reset, ld_nf, (f_z[0:33], io["flt_z"]), (f_w1[0:33], io["flt_w1"]),
               (f_w2[0:64], io["flt_w2"]), (f_w3[0:64], io["flt_w3"]), (f_vec[0:64], io["flt_vec"]),
               (f_win.rearrange("p a b -> p (a b)"), io["flt_win"]), (y_par, io["hy_par"]),
               (h_gain, io["hg_gain"])]
        ONE_LOADS, TWO_LOADS = len(ONE), len(TWO)

        block = es.enter_context(nc.Block())

        @block.sync
        def _(sp):
            def load(dst, src, name):
                sp.dma_start(dst, src).then_inc(sem(name), 16)

            def run(ph, once=None, extra=None):
                def body(i, first, last):
                    for t in range(ph.ipb):
                        load_items(sp, ph, i, t)
                        if once and first and t == AHEAD:
                            once()
                        if extra:
                            extra(i, t, first)
                bodies(sp, ph, body)

            def load_for_one():
                at_meet(sp, "normed_mix")
                for dst, src in ONE:
                    load(dst, src, "one_loaded")

            def rows(i, t, first):
                if t != 15:
                    return
                if first:
                    sp.wait_ge(sem("gate_row_out"), 1)
                    for d in range(2):
                        for kind in range(2):
                            r = 16 * (1 - kind) + 8 * d
                            load(g_scr[:, 2 * d + kind, :], g_row[r:r + 8, :], "rows_stored")
                    sp.wait_ge(sem("rows_stored"), 64)
                src = g_scr[i].rearrange("a s -> (a s)").partition_broadcast(P)
                wait(sp, "dil_lo", i)
                load(d_bc.rearrange("p a b s -> p (a b s)"), src, "bc_loaded")

            def load_residual():
                at_meet(sp, "one_done")
                load(x, io["x"], "x_loaded")

            def load_for_ffn():
                at_meet(sp, "out_done")
                load(ffn_par.rearrange("p a b -> p (a b)"), io["ffn_par"], "ffn_par_loaded")

            def load_for_block_two():
                at_meet(sp, "normed_final")
                load(x_scr, x, "x_spilled")
                load(tokens_in, io["ctx"], "ctx_loaded")
                load(ada_c.rearrange("p a b -> p (a b)"), io["cvec"], "c_loaded")
                load(ada_sel, ld_sel[1], "small2_loaded")
                load(lbl, io["lb_logits"], "small2_loaded")

            def load_for_two():
                at_meet(sp, "normed_two")
                sp.wait_ge(sem("x_spilled"), 16)
                for dst, src in TWO:
                    load(dst, src, "two_loaded")
                filter_sp(sp)
                sp.wait_ge(sem("filter_done"), 3)
                load(h_mask.rearrange("p a b -> p (a b)").bitcast(I32), io["hg_mask"], "mask_loaded")

            def spectra(i, t, first):
                if t == 15:
                    if first:
                        sp.wait_ge(sem("spec_stored"), 16 * NH)
                    wait(sp, "hy_prod", i)
                    load(y_k.rearrange("p a b -> p (a b)"), k_scr[i], "spec_loaded")

            def reload_residual():
                at_meet(sp, "two_done")
                load(x, x_scr, "x_loaded")

            load(tokens_in, io["x"], "x_loaded")
            load(gains[:, :], io["gains"], "small_loaded")
            load(eye1[:, :], io["const"][:, 0:2 * P], "small_loaded")
            run(PHD["gate"])
            run(PHD["one"], load_for_one, rows)
            run(PHD["out"], load_residual)
            for u, dn in zip(ups, downs):
                run(u, load_for_ffn if u is ups[0] else None)
                run(dn)
            run(PHD["ada"], load_for_block_two)
            run(PHD["ctx"])
            run(PHD["two"], load_for_two, spectra)
            run(PHD["out2"], reload_residual)
            for u, dn in zip(mlp1s, mlp2s):
                run(u)
                run(dn)
            at_meet(sp, "finished")
            load(out_dram, x, "out_stored")
            sp.wait_ge(sem("out_stored"), 16)

        @block.scalar
        def _(act):
            def phase(ph, evac, plan=()):
                drive(act, ph, split_hi, evac, Mixers(plan))
            act.wait_ge(sem("x_loaded"), 16)
            act.wait_ge(sem("small_loaded"), 32)
            norms[0].act(act)
            for t in range(AHEAD):
                split_hi(act, PHD["gate"], 0, t)
            meet(act, "act", "normed_mix")
            phase(PHD["gate"], act_half(act, PHD["gate"]))
            gate_act(act)
            ph = PHD["one"]
            phase(ph, act_half(act, ph), [(0, 8, 1, dil_act(act), -1), (6, 26, 1, delta_act(act), 0)])
            meet(act, "act", "one_done")
            phase(PHD["out"], act_half(act, PHD["out"]))
            meet(act, "act", "out_done")
            norms[1].act(act)
            meet(act, "act", "normed_ffn")
            for k, (u, dn) in enumerate(zip(ups, downs)):
                phase(u, act_half(act, u), [(0, 8, 1, up_act(act, u), -1)])
                meet(act, "act", f"up_done_{k}")
                phase(dn, act_half(act, dn))
                meet(act, "act", f"down_done_{k}")
            norms[2].act(act)
            meet(act, "act", "normed_final")
            ada_prologue_act(act)
            phase(PHD["ada"], None, [(0, 1, 1, ada_mix_act(act, 1), -1),
                                        (8, 1, 1, ada_mix_act(act, 0), 0)])
            meet(act, "act", "ada_done")
            act.wait_ge(sem("ctx_loaded"), 16)
            norms[3].act(act)
            ctx_prologue_act(act)
            meet(act, "act", "normed_ctx")
            phase(PHD["ctx"], act_half(act, PHD["ctx"]), [(0, 8, 2, ctx_mix_act(act), -1)])
            meet(act, "act", "ctx_done")
            norms[4].act(act)
            meet(act, "act", "normed_two")
            filter_act(act)
            act.drain().then_inc(sem("filter_done"), 1)
            ph = PHD["two"]
            hg = hg_act(act)
            phase(ph, act_half(act, ph), [(0, 8, 1, hy_act(act), -1),
                                          (13, 11, 1, lambda i: hg(ph.late)(i), 0)])
            meet(act, "act", "two_done")
            phase(PHD["out2"], act_half(act, PHD["out2"], g1))
            meet(act, "act", "out2_done")
            norms[5].act(act)
            meet(act, "act", "normed_mlp")
            for k, (u, dn) in enumerate(zip(mlp1s, mlp2s)):
                phase(u, act_half(act, u), [(0, 2, 1, mlp_act(act, u), -1)])
                meet(act, "act", f"mlp1_done_{k}")
                phase(dn, act_half(act, dn, g2))
                meet(act, "act", f"mlp2_done_{k}")
            norms[6].act(act)
            meet(act, "act", "finished")

        @block.vector
        def _(dve):
            def phase(ph, evac, plan=()):
                drive(dve, ph, split_lo, evac, Mixers(plan))
            dve.wait_ge(sem("x_loaded"), 16)
            dve.wait_ge(sem("small_loaded"), 32)
            norms[0].dve(dve)
            for t in range(AHEAD):
                split_lo(dve, PHD["gate"], 0, t)
            meet(dve, "dve", "normed_mix")
            ph = PHD["gate"]
            phase(ph, dve_whole(dve, ph, lambda i, k: d_t[:, 0, :]))
            gate_dve(dve)
            ph = PHD["one"]
            phase(ph, dve_whole(dve, ph, lambda i, k: d_t[:, k, :] if k < 4 else dl[:, k - 4, :]),
                  [(0, 8, 1, dil_dve(dve), -1), (6, 26, 1, delta_dve(dve), 0)])
            meet(dve, "dve", "one_done")
            dve.wait_ge(sem("x_loaded"), 32)
            phase(PHD["out"], dve_residual(dve, PHD["out"]))
            meet(dve, "dve", "out_done")
            norms[1].dve(dve)
            meet(dve, "dve", "normed_ffn")
            dve.wait_ge(sem("ffn_par_loaded"), 16)
            for k, (u, dn) in enumerate(zip(ups, downs)):
                phase(u, dve_whole(dve, u, lambda i, k: up[:, k, :]), [(0, 8, 1, up_dve(dve, u), -1)])
                meet(dve, "dve", f"up_done_{k}")
                phase(dn, dve_residual(dve, dn))
                meet(dve, "dve", f"down_done_{k}")
            norms[2].dve(dve)
            meet(dve, "dve", "normed_final")
            ada_prologue_dve(dve)
            phase(PHD["ada"], None, [(0, 1, 1, ada_mix_dve(dve, 1), -1),
                                        (8, 1, 1, ada_mix_dve(dve, 0), 0)])
            meet(dve, "dve", "ada_done")
            for m, (v, at, g) in enumerate(((1, 16, 48), (0, 16, 48), (0, 64, 64))):
                ins = dve.scalar_tensor_tensor(gm[:, m, :], mod[:, v, at:at + KT], 1.0,
                                               gains[:, g:g + KT], ALU.add, ALU.mult)
            ins.then_inc(sem("gains_ready"), 1)
            dve.wait_ge(sem("gains_ready"), 1)
            dve.wait_ge(sem("ctx_loaded"), 16)
            norms[3].dve(dve)
            ctx_prologue_dve(dve)
            meet(dve, "dve", "normed_ctx")
            ph = PHD["ctx"]
            phase(ph, dve_whole(dve, ph, lambda i, k: c_z[:, k, :]), [(0, 8, 2, ctx_mix_dve(dve), -1)])
            meet(dve, "dve", "ctx_done")
            norms[4].dve(dve)
            meet(dve, "dve", "normed_two")
            filter_dve(dve)
            dve.drain().then_inc(sem("filter_done"), 1)
            dve.wait_ge(sem("filter_done"), 3)
            dve.memset(h_sc, 0.0).then_inc(sem("scores_clear"), 1)
            dve.wait_ge(sem("scores_clear"), 1)
            dve.wait_ge(sem("mask_loaded"), 16)
            ph = PHD["two"]
            hg = hg_dve(dve)
            phase(ph, dve_whole(dve, ph, lambda i, k: h_z[:, k, :] if k < 5 else y_t[:, k - 5, :],
                                lambda i, k: PHD["two"].late and k < 4),
                  [(0, 8, 1, hy_dve(dve), -1), (13, 11, 1, lambda i: hg(ph.late)(i), 0)])
            meet(dve, "dve", "two_done")
            dve.wait_ge(sem("x_loaded"), 48)
            phase(PHD["out2"], dve_residual(dve, PHD["out2"], g1))
            meet(dve, "dve", "out2_done")
            norms[5].dve(dve)
            meet(dve, "dve", "normed_mlp")
            for k, (u, dn) in enumerate(zip(mlp1s, mlp2s)):
                phase(u, dve_whole(dve, u, lambda i, k: up[:, k, :]), [(0, 2, 1, mlp_dve(dve, u), -1)])
                meet(dve, "dve", f"mlp1_done_{k}")
                phase(dn, dve_residual(dve, dn, g2))
                meet(dve, "dve", f"mlp2_done_{k}")
            norms[6].dve(dve)
            meet(dve, "dve", "finished")

        @block.tensor
        def _(pe):
            def phase(ph, src, plan=()):
                drive_pe(pe, ph, gemm_block(pe, ph, src), Mixers(plan))
            pe.wait_ge(sem("small_loaded"), 32)
            norms[0].pe(pe)
            meet(pe, "pe", "normed_mix")
            phase(PHD["gate"], act_a)
            pe.wait_ge(sem("one_loaded"), 16 * ONE_LOADS)
            gate_pe(pe)
            phase(PHD["one"], act_a, [(0, 8, 1, dil_pe(pe), -1), (6, 26, 1, delta_pe(pe), 0)])
            meet(pe, "pe", "one_done")
            phase(PHD["out"], act_b)
            meet(pe, "pe", "out_done")
            norms[1].pe(pe)
            meet(pe, "pe", "normed_ffn")
            for k, (u, dn) in enumerate(zip(ups, downs)):
                phase(u, act_a)
                meet(pe, "pe", f"up_done_{k}")
                phase(dn, act_b)
                meet(pe, "pe", f"down_done_{k}")
            norms[2].pe(pe)
            meet(pe, "pe", "normed_final")
            pe.wait_ge(sem("c_lo"), 1)
            pe.wait_ge(sem("small2_loaded"), 32)
            drive_pe(pe, PHD["ada"], ada_block(pe, PHD["ada"]), Mixers([(0, 1, 1, ada_mix_pe(pe, 1), -1),
                                        (8, 1, 1, ada_mix_pe(pe, 0), 0)]))
            meet(pe, "pe", "ada_done")
            norms[3].pe(pe)
            meet(pe, "pe", "normed_ctx")
            phase(PHD["ctx"], act_a, [(0, 8, 2, ctx_mix_pe(pe), -1)])
            meet(pe, "pe", "ctx_done")
            norms[4].pe(pe)
            meet(pe, "pe", "normed_two")
            filter_pe(pe)
            pe.drain().then_inc(sem("filter_done"), 1)
            ph = PHD["two"]
            hg = hg_pe(pe)
            phase(ph, act_a, [(0, 8, 1, hy_pe(pe), -1), (13, 11, 1, lambda i: hg(ph.late)(i), 0)])
            meet(pe, "pe", "two_done")
            phase(PHD["out2"], act_b)
            meet(pe, "pe", "out2_done")
            norms[5].pe(pe)
            meet(pe, "pe", "normed_mlp")
            for k, (u, dn) in enumerate(zip(mlp1s, mlp2s)):
                phase(u, act_a)
                meet(pe, "pe", f"mlp1_done_{k}")
                phase(dn, act_b)
                meet(pe, "pe", f"mlp2_done_{k}")
            norms[6].pe(pe)
            meet(pe, "pe", "finished")

    return nc


def kernel(**inputs):
    import concourse.bacc as bacc
    from concourse.bass_utils import run_bass_kernel_spmd

    arrays = lay_out({k: np.asarray(v) for k, v in inputs.items()})
    nc = bacc.Bacc("TRN2", target_bir_lowering=False, num_devices=1)
    io = {}
    for name, a in arrays.items():
        io[name] = nc.dram_tensor(name, a.shape, mybir.dt.from_np(a.dtype), kind="ExternalInput").ap()
    out = nc.dram_tensor("out", (P, KT, S), F32, kind="ExternalOutput").ap()
    build(nc, io, out)
    got = run_bass_kernel_spmd(nc, [arrays], core_ids=[0]).results[0]["out"]
    return np.ascontiguousarray(np.asarray(got).transpose(2, 1, 0).reshape(1, S, D))
```

```python
import numpy as np
from concourse import mybir
from contextlib import ExitStack

F32 = mybir.dt.float32
F32R = mybir.dt.float32r
I32 = mybir.dt.int32
ALU = mybir.AluOpType
ACT = mybir.ActivationFunctionType
AX = mybir.AxisListType

P = 128
S = 256
D = 2048
KT = D // P
NH = 8
DFF, DFF2 = 5632, 8192
EPS = 1e-6
NB = 8
RAW, SPLIT = 8, 4
ADA_FIRST = 8
AHEAD = SPLIT - 1
HD = 128
CH = 64
FFN_PARTS = [(0, 16), (16, 16), (32, 12)]
MLP_PARTS = [(0, 16), (16, 16), (32, 16), (48, 16)]
DELTA_W = 1024
GATE_COL = 4 * DELTA_W
DIL_COL = GATE_COL + 4 * NH


def shape_constants():
    i = np.arange(P)
    c = {}
    c["ident"] = np.eye(P)
    c["ones"] = np.ones((P, P))
    c["level"] = np.concatenate(
        [(((i[:, None] >> s) ^ (i[None, :] >> s)) == 1) for s in range(7)], 1).astype(np.float64)
    fwd_s, fwd_i = i[None, :] > i[:, None], i[None, :] >= i[:, None]
    bwd_s, bwd_i = i[None, :] < i[:, None], i[None, :] <= i[:, None]
    c["neg"] = np.concatenate([np.where(m, 0.0, -1e30) for m in (fwd_s, fwd_i, bwd_s, bwd_i)], 1)
    c["tri"] = np.concatenate([fwd_i, bwd_i], 1).astype(np.float64)
    t = np.arange(S)
    dist = t[None, :] - t[:, None]
    seen = [np.abs(dist) <= 64, dist % 4 == 0, dist % 16 == 0]
    m = np.stack([np.where(x, 0.0, -1e30) for x in seen])
    c["dil"] = m.reshape(3, 2, P, S).transpose(2, 1, 0, 3).reshape(P, 6 * S)
    c["reset"] = np.tile(np.concatenate([t % CH != 0, t % CH != CH - 1]).astype(np.float64), (P, 1))
    row = np.arange(P)
    c["rowsel"] = np.stack([row < 8, (row >= 8) & (row < 16), row >= 16], 1).astype(np.float64)
    c["gsign"] = np.where(row < 16, 1.0, -1.0)[:, None].repeat(2, 1)
    c["sel"] = np.stack([row % 2 == 0, row % 2 == 1], 1).astype(np.float64) * (row < 4)[:, None]
    freq = (500000.0 ** (-np.arange(0, 32, 2) / 32)).astype(np.float32)
    c["ropef"] = np.concatenate([freq, freq, np.zeros(96)])[:, None].repeat(2, 1)
    c["ropes"] = np.concatenate([-np.ones(16), np.ones(112)])[:, None].repeat(2, 1)
    c["notfirst"] = np.stack([row != 0, row >= 0], 1).astype(np.float64)
    k = (np.arange(S) + 0.5) * (2 * np.pi / (2 * S))
    ang = t[:, None] * k[None, :]
    cos, sin = np.cos(ang), np.sin(ang)
    f = np.concatenate([cos, sin], 1)
    c["dft"] = f.reshape(2, P, 2 * S).transpose(1, 0, 2).reshape(P, -1)
    inv = np.stack([cos.T, sin.T], 0) / S
    c["idft"] = inv.reshape(2, 2, P, S).transpose(2, 0, 1, 3).reshape(P, -1)
    names, cols, at = list(c), {}, 0
    for n in names:
        cols[n] = (at, c[n].shape[1])
        at += c[n].shape[1]
    table = np.concatenate([c[n] for n in names], 1).astype(np.float32)
    f32 = np.float32
    pos = np.arange(S, dtype=f32)[:, None]
    tt = pos / f32(S - 1)
    bands = np.linspace(1e-4, 15, 16, dtype=f32)[None, :]
    a = bands * f32(2.0 * np.pi) * pos / f32(S)
    z = np.concatenate([tt, np.cos(a), -np.sin(a)], -1).T.astype(f32)
    deltas = np.abs(np.linspace(np.log(1e-2) / 1.5, np.log(1e-2) / 0.3, 1024, dtype=f32))
    win = np.exp(-tt * deltas[None, :]) + f32(0.05)
    win = win.reshape(2, P, 1024).transpose(1, 0, 2).reshape(P, -1).astype(f32)
    jj = np.arange(P)
    same = (jj[:, None] // CH) == (jj[None, :] // CH)
    hm = np.stack([same & fwd_i, same & fwd_i, same & bwd_i, same & bwd_i], 1)
    return table, cols, np.ascontiguousarray(z), np.ascontiguousarray(win), \
        hm.reshape(P, 4 * P).astype(np.int32)


def blocks_of(w, tiles):
    kt = w.shape[0] // P
    return [(w, r, c) for c in tiles for r in range(kt)]


def stream(blocks, nb):
    n = len(blocks) // nb
    assert n * nb == len(blocks) and n % RAW == 0
    out = np.empty((n, P, nb * P), np.float32)
    for b, (w, r, c) in enumerate(blocks):
        out[b // nb, :, (b % nb) * P:(b % nb + 1) * P] = w[r * P:(r + 1) * P, c:c + P]
    return out


def cm(v):
    return np.ascontiguousarray(v.reshape(-1, P).T)


def lay_out(a):
    out = {}
    w_in, w_in2 = a["w_in"][0], a["w_in_2"][0]
    T = lambda *cols: list(cols)
    gate = [(w_in, r, GATE_COL) for r in range(KT)]
    delta, dil, ctx, hg, hy = [], [], [], [], []
    for h in range(NH):
        delta += blocks_of(w_in, [kind * DELTA_W + h * HD for kind in range(4)])
        dil += blocks_of(w_in, [DIL_COL + kind * 3 * 1024 + b * 1024 + h * HD
                                for kind in range(3) for b in range(3)])
        ctx += blocks_of(w_in2, T(1024 + h * HD, 2048 + h * HD, 3072 + h * HD))
        hg += blocks_of(w_in2, [kind * 1024 + h * HD for kind in range(5)])
        hy += blocks_of(w_in2, [5120 + kind * 1024 + h * HD for kind in range(3)])
    out["w_gate"] = stream(gate, 2)
    out["w_delta"] = stream(delta, 8)
    out["w_dil"] = stream(dil, 6)
    out["w_ctx"] = stream(ctx, 6)
    out["w_hg"] = stream(hg, 5)
    out["w_hy"] = stream(hy, 6)
    ada = a["w_ada_2"][0]
    out["w_ada"] = stream([(ada, r, n * 512 + c * P) for n in range(24) for r in range(KT)
                           for c in range(4)], 8)
    out["w_out"] = stream(blocks_of(a["w_out"][0], range(0, D, P)), 8)
    out["w_out2"] = stream(blocks_of(a["w_out_2"][0], range(0, D, P)), 8)
    fi, fo = a["w_ffn_in"][0], a["w_ffn_out"][0]
    up = []
    for t0, n in FFN_PARTS:
        for t in range(t0, t0 + n):
            up += blocks_of(fi, [t * P, DFF + t * P])
        out[f"w_down_{t0}"] = stream(blocks_of(fo[t0 * P:(t0 + n) * P], range(0, D, P)), n // 2)
    out["w_up"] = stream(up, 8)
    out["w_mlp1"] = stream(blocks_of(a["w_mlp1_2"][0], range(0, DFF2, P)), 8)
    m2 = []
    for t0, n in MLP_PARTS:
        m2 += blocks_of(a["w_mlp2_2"][0][t0 * P:(t0 + n) * P], range(0, D, P))
    out["w_mlp2"] = stream(m2, 8)

    tok = lambda x: np.ascontiguousarray(x[0].T.reshape(KT, P, S).transpose(1, 0, 2))
    out["x"], out["ctx"] = tok(a["x"]), tok(a["ctx_2"])
    out["cvec"] = np.ascontiguousarray(
        np.stack([a["c_2"][0], a["c_ctx_2"]]).reshape(2, KT, P).transpose(2, 1, 0))
    out["positions"] = np.ascontiguousarray(a["positions"])
    out["gains"] = np.concatenate(
        [cm(a["norm_mix_w"][0]), cm(a["norm_ffn_w"][0]), cm(a["norm_final_w"]),
         cm(a["norm1_g_2"][0]), cm(a["norm2_g_2"][0]), cm(a["final_norm_g_2"]),
         cm(a["b_ada_2"][0])], 1)
    conv = a["conv_qkv_w"][0].reshape(5, 3, NH, P).transpose(3, 2, 1, 0).reshape(P, NH, 15)
    nw = np.broadcast_to(a["delta_norm_w"][0][:, None, None], (P, NH, 1))
    out["delta_par"] = np.ascontiguousarray(np.concatenate([conv, nw], 2))
    out["ffn_par"] = np.ascontiguousarray(
        a["conv_ffn_w"][0].reshape(3, 2, 44, P).transpose(3, 2, 1, 0))
    lb = a["hgrn_lb_logits_2"].reshape(2, 2, NH, P).transpose(3, 0, 1, 2)
    out["lb_logits"] = np.ascontiguousarray(lb)
    out["hg_gain"] = cm(a["hgrn_norm_g_2"][0])
    cw = a["hy_conv_w_2"][0].reshape(3, 3, NH, P).transpose(3, 2, 1, 0).reshape(P, NH, 9)
    cb = a["hy_conv_b_2"][0].reshape(3, NH, P).transpose(2, 1, 0)
    bi = a["hy_bias_2"][0].reshape(NH, P).T[:, :, None]
    out["hy_par"] = np.ascontiguousarray(np.concatenate([cw, cb, bi], 2))
    z16 = np.zeros(16, np.float32)
    out["gate_par"] = np.ascontiguousarray(np.stack(
        [np.concatenate([a["dt_bias_fwd"][0], a["dt_bias_bwd"][0], z16]),
         np.concatenate([a["a_log_fwd"][0], a["a_log_bwd"][0], z16])], 1))
    out["flt_w1"] = np.ascontiguousarray(a["flt_w1_2"][0])
    out["flt_w2"] = np.ascontiguousarray(a["flt_w2_2"][0])
    out["flt_w3"] = np.ascontiguousarray(a["flt_w3_2"][0])
    out["flt_vec"] = np.ascontiguousarray(
        np.stack([a["flt_b1_2"][0], a["flt_b2_2"][0], a["flt_freq_2"][0]], 1))
    table, _, z, win, hm = shape_constants()
    out["const"], out["flt_z"], out["flt_win"], out["hg_mask"] = table, z, win, hm
    return out


class Phase:

    def __init__(self, name, n, items, tiles, first=0, turn=None, done=0, banks=3, unroll=1):
        self.done = done
        self.banks = banks
        self.unroll = unroll
        self.name, self.n, self.items, self.tiles = name, n, items, tiles
        self.first = first
        self.turn, self.late = turn, False
        self.ada_base = 0 if name == "up" else ADA_FIRST
        self.ipb, self.tpb = len(items), len(tiles)
        assert self.ipb % RAW == 0
        self.walk = [(k, kt, kt == 0, kt == kb - 1) for k, kb in enumerate(tiles) for kt in range(kb)]
        at = 0
        self.blocks = []
        for name_, nb in items:
            self.blocks.append(None if name_ == "w_ada" else self.walk[at:at + nb])
            at += 0 if name_ == "w_ada" else nb
        self.evac = [[] for _ in items]
        if tiles:
            assert at == len(self.walk)
            for t, bl in enumerate(self.blocks):
                for k, _, _, last in bl or ():
                    if last:
                        self.evac[(t + 1) % self.ipb].append((-1 if t + 1 == self.ipb else 0, k))

    def hops_at(self, t):
        return self.blocks[t] is not None

    def ada_items(self):
        return [t for t, bl in enumerate(self.blocks) if bl is None]

    def split_by(self, t):
        if self.name == "two":
            return "dve" if t % 5 in (1, 4) else "pool"
        if None in self.blocks:
            return "pool" if self.blocks[t] is None else "dve"
        return "pool" if t % 2 else "dve"

    def lo_ready(self, i, t):
        if t < 0 and isinstance(i, int) and i == 0:
            if not self.prev:
                return "lo_ready_dve", 0
            return self.prev.lo_ready(self.prev.n - 1, self.prev.ipb + t)
        i, t = (i, t) if t >= 0 else (i - 1, t + self.ipb)
        who = self.split_by(t)
        mine = [self.split_by(q) == who for q in range(self.ipb)]
        return f"lo_ready_{who}", i * sum(mine) + (self.lo0[who] + sum(mine[:t + 1]))

    def tile_number(self, i, k):
        return i * self.tpb + (self.t0 + k)

    def tile_done(self, i, k):
        t = next(t for t, bl in enumerate(self.blocks) for b in bl or () if b[0] == k and b[3])
        return i * self.ipb + (self.g0 + t + 1)

    def bank_free_after(self, i, k):
        before = [q for q in range(k) if self.bank(q) == self.bank(k)]
        if before:
            return self.tile_number(i, before[-1]) + 1
        if isinstance(i, int) and i == 0:
            return self.t0 + (k + 1 - self.tpb if self.prev and self.same_banks(self.prev) else 0)
        last = max(q for q in range(self.tpb) if self.bank(q) == self.bank(k))
        return (i - 1) * self.tpb + (self.t0 + last + 1)

    def bank(self, k):
        return 1 if self.banks == 3 and k and k == self.tpb - 1 and k % 3 == 0 else k % self.banks

    def half_free_after(self, i, k):
        alternate = k >= 2 or (self.tpb % 2 == 0 and not (isinstance(i, int) and i == 0))
        return self.tile_number(i, k) - (1 if alternate else 0)

    def same_banks(self, other):
        return self.banks == other.banks == self.tpb == other.tpb


def phases():
    four = dict(banks=4, unroll=0)
    ps = [
        Phase("gate", 1, [("w_gate", 2)] * 8, [KT]),
        Phase("one", NH, [("w_delta", 8)] * 8 + [("w_dil", 6)] * 24, [KT] * 13),
        Phase("out", 4, [("w_out", 8)] * 8, [KT] * 4, **four),
    ]
    u, m = [("w_up", 8)], [("w_ada", 8)]
    for t0, n in FFN_PARTS:
        items = u * 8 if t0 else u * 2 + m + (u + m) * 6 + m
        ps.append(Phase("up", n // 2, items, [KT] * 4, first=t0 // 2, done=t0,
                        banks=4, unroll=n // 2 // 2 - 1))
        ps.append(Phase("down", 4, [(f"w_down_{t0}", n // 2)] * 8, [n] * 4, **four))
    ps.append(Phase("ctx", NH, [("w_ctx", 6)] * 8, [KT] * 3, unroll=3))
    three = [("w_hg", 5)] * 16 + [("w_hy", 6)] * 8
    two = []
    for q in range(8):
        a, b, c = three[3 * q:3 * q + 3]
        two += [a, b, c] + m * 2 if q % 4 == 0 else [a, b] + m + [c] + m
    ps.append(Phase("two", NH, two, [KT] * 8, turn=NH // 2, banks=2))
    ps.append(Phase("out2", 4, [("w_out2", 8)] * 8, [KT] * 4, **four))
    for t0, n in MLP_PARTS:
        ps.append(Phase("mlp1", 4, [("w_mlp1", 8)] * 8, [KT] * 4, first=t0 // 4, done=t0, **four))
        ps.append(Phase("mlp2", 4, [("w_mlp2", 8)] * 8, [n] * 4, first=t0 // 4, **four))
    g, t, lo = 0, 0, dict(dve=0, pool=0)
    for o, p, q in zip([None] + ps, ps, ps[1:] + [None]):
        p.g0, p.t0, p.prev, p.next, p.lo0 = g, t, o, q, dict(lo)
        for k in range(p.ipb):
            lo[p.split_by(k)] += p.n
        g += p.n * p.ipb
        t += p.n * p.tpb
    return ps


def build(nc, io, out_dram, stop=None):
    import concourse.bass as bass

    PH = phases()
    table, cols, _, _, _ = shape_constants()
    NCONST = table.shape[1]
    es = ExitStack()
    with es:
        def sb(name, shape, dt=F32):
            return es.enter_context(nc.sbuf_tensor(name, shape, dt))

        sems = {}

        def sem(name):
            if name not in sems:
                sems[name] = es.enter_context(nc.semaphore(name))
            return sems[name]

        def wait(eng, name, value):
            if not (isinstance(value, int) and value <= 0):
                eng.wait_ge(sem(name), value)

        class Chain:

            def __init__(self, name, per=None):
                self.name, self.per = name, per

            def begin(self, eng, i):
                assert self.per is not None or (isinstance(i, int) and i == 0), self.name
                self.eng, self.i, self.k = eng, i, 0

            def step(self, ins):
                ins.then_inc(sem(self.name), 1)
                self.k += 1

            def settle(self):
                i0 = 0 if self.per is None else self.i * self.per
                self.eng.wait_ge(sem(self.name), i0 + self.k)

            def end(self):
                assert self.per in (None, self.k), (self.name, self.per, self.k)
                self.per = self.k

        raw = sb("raw", [P, RAW, NB * P])
        w_hi = sb("w_hi", [P, SPLIT, NB * P], F32R)
        w_lo = sb("w_lo", [P, SPLIT, NB * P], F32R)
        act_a = sb("act_a", [P, KT, 2 * S], F32R)
        act_b = sb("act_b", [P, KT, 2 * S], F32R)
        half = sb("half", [P, 2, S])
        gains = sb("gains_sb", [P, 192])
        mod = sb("mod", [P, 2, 96])
        eye1 = sb("eye1", [P, 2 * P])
        stat = sb("stat", [P, KT, 4], F32R)
        y_rs, y_ss = sb("filter_rsqrt", [P, NH])[:, :], sb("filter_power_sb", [P, NH])[:, :]
        ada_row = sb("ada_row", [4, 512])
        sel_sb = sb("sel_sb", [P, 2])
        WORK = 18560
        work = sb("work", [P, WORK])
        x = work[:, 0:KT * S].rearrange("p (k t) -> p k t", k=KT)

        class Area:

            def __init__(self, at=0):
                self.at = at

            def take(self, *shape):
                n = int(np.prod(shape))
                v = work[:, self.at:self.at + n]
                self.at += n
                assert self.at <= WORK, (self.at, WORK)
                if len(shape) == 2:
                    v = v.rearrange("p (a b) -> p a b", a=shape[0])
                elif len(shape) == 3:
                    v = v.rearrange("p (a b c) -> p a b c", a=shape[0], b=shape[1])
                elif len(shape) == 4:
                    v = v.rearrange("p (a b c d) -> p a b c d", a=shape[0], b=shape[1], c=shape[2])
                return v

        acc = es.enter_context(nc.psum_tensor("psum", [P, 8, 512], F32))
        mix = acc[:, 3:8, :]
        ident, ones = eye1[:, 0:P], eye1[:, P:2 * P]
        A2 = lambda v, **k: v.rearrange("p (a b) -> p a b", **k)

        def raw_loaded(g0, i, ipb, t):
            return (i * (ipb // RAW)) * 16 + ((g0 + t) // RAW + 1) * 16

        def load_items(sp, ph, i, t):
            name, nb = ph.items[t]
            same = [q for q, (nm, _) in enumerate(ph.items) if nm == name]
            base = ph.ada_base * 8 if name == "w_ada" else ph.first * len(same)
            src = io[name][i * len(same) + (base + same.index(t))]
            wait(sp, *ph.lo_ready(i, t - RAW))
            sp.dma_start(raw[:, t % RAW, 0:nb * P], src)\
              .then_inc(sem(f"raw_loaded{t % RAW}"), 16)

        def split_hi(act, ph, i, t):
            nb = ph.items[t][1]
            wait(act, f"raw_loaded{t % RAW}", raw_loaded(ph.g0, i, ph.ipb, t))
            wait(act, "item_used", i * ph.ipb + (ph.g0 + t + 1 - SPLIT))
            act.activation(w_hi[:, t % SPLIT, 0:nb * P], raw[:, t % RAW, 0:nb * P], ACT.Copy)\
               .then_inc(sem("hi_ready"), 1)

        def split_lo(who):
            def split(eng, ph, i, t):
                if ph.split_by(t) != who:
                    return
                nb = ph.items[t][1]
                wait(eng, "hi_ready", i * ph.ipb + (ph.g0 + t + 1))
                eng.tensor_tensor(w_lo[:, t % SPLIT, 0:nb * P], raw[:, t % RAW, 0:nb * P],
                                  w_hi[:, t % SPLIT, 0:nb * P], ALU.subtract)\
                   .then_inc(sem(f"lo_ready_{who}"), 1)
            return split

        def bodies(eng, ph, body):
            ph.late = False
            if not ph.unroll:
                for i in range(ph.n):
                    body(i, i == 0, i == ph.n - 1)
                return
            body(0, True, ph.n == 1)
            at = 1
            for late, end in ((False, ph.turn), (True, ph.n - 1)):
                if end is not None and end > at:
                    ph.late, u = late, ph.unroll
                    assert (end - at) % u == 0
                    with eng.Fori(0, (end - at) // u) as j:
                        for r in range(u):
                            body(j * u + (at + r), False, False)
                    at = end
            if ph.n > 1:
                body(ph.n - 1, False, True)

        def hop(live, q):
            for _, rate, gen in live:
                if q < rate:
                    next(gen, None)

        def run_out(gen):
            for _ in gen:
                pass

        class Mixers:

            def __init__(self, plan):
                self.plan = plan

            def start(self, t, i, first):
                got = []
                for at, length, rate, fn, off in self.plan:
                    if at == t and not (first and off < 0):
                        got.append([at + length, rate, fn(i + off)])
                return got

            def finish(self, n):
                for _, _, _, fn, off in self.plan:
                    if off < 0:
                        run_out(fn(n - 1))

        def stroll(slow, t):
            if slow:
                next(slow, None)

        def drive(eng, ph, split, evac, mixers, tiles=True, slow=None):
            def body(i, first, last):
                live = []
                for t in range(ph.ipb):
                    if t + AHEAD < ph.ipb:
                        split(eng, ph, i, t + AHEAD)
                    elif not last:
                        split(eng, ph, i + 1, t + AHEAD - ph.ipb)
                    elif ph.next:
                        split(eng, ph.next, 0, t + AHEAD - ph.ipb)
                    for off, k in ph.evac[t] if tiles else ():
                        if not (first and off < 0):
                            evac(i + off, k)
                    live = [m for m in live if m[0] > t] + mixers.start(t, i, first)
                    for q in range(2):
                        if ph.hops_at(t):
                            hop(live, q)
                    for m in live:
                        if m[0] == t + 1:
                            assert next(m[2], "end") == "end", ph.name
                    stroll(slow, t)
            bodies(eng, ph, body)
            assert slow is None or next(slow, "end") == "end"
            for off, k in ph.evac[0] if tiles else ():
                if off < 0:
                    evac(ph.n - 1, k)
            mixers.finish(ph.n)

        def drive_pe(pe, ph, block, mixers, slow=None):
            def body(i, first, last):
                live = []
                for t in range(ph.ipb):
                    nb = ph.items[t][1]
                    wait(pe, *ph.lo_ready(i, t))
                    live = [m for m in live if m[0] > t] + mixers.start(t, i, first)
                    cuts, ins = [nb * q // 2 for q in range(3)], None
                    for q in range(2):
                        for b in range(cuts[q], cuts[q + 1]):
                            ins = block(i, t, b) or ins
                        if q == 1:
                            ins.then_inc(sem("item_used"), 1)
                        if ph.hops_at(t):
                            hop(live, q)
                    stroll(slow, t)
            bodies(pe, ph, body)
            assert slow is None or next(slow, "end") == "end"
            mixers.finish(ph.n)

        def gemm_block(pe, ph, src, hidden=None):
            def block(i, t, b):
                if ph.blocks[t] is None:
                    return ada_block(pe, ph)(i, t, b)
                k, kt, first, last = ph.blocks[t][b]
                if hidden and k == 0 and isinstance(i, int) and i == 0:
                    wait(pe, *hidden(kt))
                if first:
                    wait(pe, "tile_out", ph.bank_free_after(i, k))
                wh = w_hi[:, t % SPLIT, b * P:(b + 1) * P]
                wl = w_lo[:, t % SPLIT, b * P:(b + 1) * P]
                bank = acc[:, ph.bank(k), :]
                if last:
                    pe.matmul(bank[:, 0:S], wl, src[:, kt, 0:S], start=False, stop=False)
                    ins = pe.matmul(bank, wh, src[:, kt, :], start=False, stop=True)
                else:
                    pe.matmul(bank, wh, src[:, kt, :], start=first, stop=False)
                    ins = pe.matmul(bank[:, 0:S], wl, src[:, kt, 0:S], start=False, stop=False)
                return ins
            return block

        ends = {"pe": 0, "act": 0, "dve": 0}
        LATER = NH + 1

        def act_half(act, ph, scale=None):
            def evac(i, k):
                wait(act, "item_used", ph.tile_done(i, k))
                wait(act, "tile_out", ph.half_free_after(i, k))
                kw = {} if scale is None else {"scale": scale(i, k)}
                act.activation(half[:, k % 2, :], acc[:, ph.bank(k), S:2 * S], ACT.Copy, **kw)\
                   .then_inc(sem("half_ready"), 1)
            return evac

        def dve_whole(dve, ph, dst, order=None):
            def evac(i, k):
                wait(dve, "half_ready", ph.tile_number(i, k) + 1)
                a, b = acc[:, ph.bank(k), 0:S], half[:, k % 2, :]
                o = dst(i, k)
                if order is not None and order(i, k):
                    a = a.rearrange("p (r c) -> p c r", c=64)
                    b = b.rearrange("p (r c) -> p c r", c=64)
                    o = o.rearrange("p (c r) -> p c r", r=4)
                dve.tensor_tensor(o, a, b, ALU.add).then_inc(sem("tile_out"), 1)
            return evac

        class Norm:

            count = splits = 0

            def __init__(self, src, gain, dst, shift=None, plain=None):
                ar = Area(WORK - 4096)
                self.sq, self.u = ar.take(2, 512), ar.take(4, S)
                self.v, self.y, self.t, self.h = [ar.take(S) for _ in range(4)]
                self.src, self.gain, self.dst, self.shift, self.plain = src, gain, dst, shift, plain
                self.n = Norm.count
                Norm.count += 1
                self.m = Norm.splits
                Norm.splits += plain is None
                self.chain = "norm_dve_steps"

            def pe(self, pe):
                n = self.n
                for j in range(8):
                    wait(pe, "norm_square", 8 * n + j + 1)
                    pe.matmul(mix[:, 0, :], ones, self.sq[:, j % 2, :], start=(j == 0), stop=(j == 7))\
                      .then_inc(sem("norm_summed"), 1)

            def act(self, act):
                n = self.n
                for j in range(8):
                    if j >= 2:
                        wait(act, "norm_summed", 8 * n + j - 1)
                    act.activation(self.sq[:, j % 2, :], self.src[:, 2 * j:2 * j + 2, :], ACT.Square)\
                       .then_inc(sem("norm_square"), 1)
                wait(act, "norm_summed", 8 * n + 8)
                act.activation(self.h, mix[:, 0, S:2 * S], ACT.Copy).then_inc(sem("norm_half"), 1)
                wait(act, "norm_mean", n + 1)
                act.activation(self.t, self.v, ACT.Ln).then_inc(sem("norm_act_steps"), 1)
                act.wait_ge(sem("norm_act_steps"), n + 1)
                act.activation(self.y, self.t, ACT.Exp, scale=-0.5).then_inc(sem("norm_guess"), 1)
                for j in range(KT if self.plain is None else 0):
                    wait(act, "norm_scaled", KT * n + j + 1)
                    kw = {} if self.shift is None else {"bias": self.shift[:, j:j + 1]}
                    act.activation(self.dst[:, j, 0:S], self.u[:, j % 4, :],
                                   ACT.Copy if self.shift is None else ACT.Identity, **kw)\
                       .then_inc(sem("norm_hi"), 1)

            def dve(self, dve):
                n, c = self.n, sem(self.chain)
                k = 4 * n
                wait(dve, "norm_half", n + 1)
                dve.tensor_tensor(self.v, mix[:, 0, 0:S], self.h, ALU.add).then_inc(c, 1)
                dve.wait_ge(c, k + 1)
                dve.tensor_scalar(self.v, self.v, 1.0 / D, EPS, ALU.mult, ALU.add)\
                   .then_inc(sem("norm_mean"), 1)
                wait(dve, "norm_guess", n + 1)
                dve.tensor_tensor(self.t, self.y, self.y, ALU.mult).then_inc(c, 1)
                dve.wait_ge(c, k + 2)
                dve.scalar_tensor_tensor(self.t, self.t, -0.5, self.v, ALU.mult, ALU.mult).then_inc(c, 1)
                dve.wait_ge(c, k + 3)
                dve.scalar_tensor_tensor(self.y, self.t, 1.5, self.y, ALU.add, ALU.mult).then_inc(c, 1)
                dve.wait_ge(c, k + 4)

                def lo(j):
                    wait(dve, "norm_hi", KT * self.m + j + 1)
                    if self.shift is None:
                        dve.tensor_tensor(self.dst[:, j, S:2 * S], self.u[:, j % 4, :],
                                          self.dst[:, j, 0:S], ALU.subtract)\
                           .then_inc(sem("norm_lo"), 1)
                    else:
                        dve.scalar_tensor_tensor(self.dst[:, j, S:2 * S], self.u[:, j % 4, :],
                                                 self.shift[:, j:j + 1], self.dst[:, j, 0:S],
                                                 ALU.add, ALU.subtract).then_inc(sem("norm_lo"), 1)
                for j in range(KT):
                    if self.plain is None and j >= 4:
                        wait(dve, "norm_lo", KT * self.m + j - 3)
                    o = self.u[:, j % 4, :] if self.plain is None else self.plain[:, j, :]
                    dve.scalar_tensor_tensor(o, self.src[:, j, :], self.gain[:, j:j + 1], self.y,
                                             ALU.mult, ALU.mult).then_inc(sem("norm_scaled"), 1)
                    if self.plain is None and j >= 2:
                        lo(j - 2)
                if self.plain is None:
                    lo(KT - 2)
                    lo(KT - 1)

        def rsqrt_act(act, ch, v, y, t, scale, bias, ready):
            ch.step(act.activation(t, v, ACT.Ln, scale=scale, bias=bias))
            ch.settle()
            act.activation(y, t, ACT.Exp, scale=-0.5).then_inc(sem(ready), 1)

        def newton(ch, dve, v, y, t, w, scale, bias):
            ch.step(dve.tensor_scalar(w, v, scale, bias, ALU.mult, ALU.add))
            ch.step(dve.tensor_tensor(t, y, y, ALU.mult))
            ch.settle()
            ch.step(dve.scalar_tensor_tensor(t, t, -0.5, w, ALU.mult, ALU.mult))
            ch.settle()
            ch.step(dve.scalar_tensor_tensor(t, t, 1.5, y, ALU.add, ALU.mult))
            ch.settle()

        def bc(v, n):
            return v.unsqueeze(1).to_broadcast([v.shape[0], n, v.shape[1]])

        def const(ar, name):
            at, n = cols[name]
            v = ar.take(n)
            return v, (v, io["const"][:, at:at + n])

        g_scr = nc.dram_tensor("gate_rows", (NH, 4, S), F32, kind="Internal").ap()
        k_scr = nc.dram_tensor("filter_spectra", (NH, P, 4 * P), F32, kind="Internal").ap()
        x_scr = nc.dram_tensor("residual", (P, KT, S), F32, kind="Internal").ap()

        ar = Area(KT * S + 2048 + 1024 + 512)
        ada_c, ada_th, ada_lo = ar.take(KT, 2), ar.take(KT, 2), ar.take(KT, 2)
        at_, n_ = cols["sel"]
        ada_sel, ld_sel = sel_sb, (sel_sb[:, :], io["const"][:, at_:at_ + n_])
        lbl = ar.take(2, 2, NH)

        def ada_prologue_act(act):
            act.wait_ge(sem("small2_loaded"), 48)
            act.activation(ada_th, ada_c, ACT.Tanh, scale=0.5).then_inc(sem("c_steps"), 1)
            act.wait_ge(sem("c_steps"), 3)
            act.wait_ge(sem("stat_clear"), 1)
            act.activation(stat[:, :, 0:2], ada_c, ACT.Copy).then_inc(sem("c_steps"), 1)
            act.wait_ge(sem("c_lo"), 1)

        def ada_prologue_dve(dve):
            dve.memset(stat[:, :, :].bitcast(F32), 0.0).then_inc(sem("stat_clear"), 1)
            dve.wait_ge(sem("c_steps"), 1)
            dve.scalar_tensor_tensor(ada_c, ada_th, 1.0, ada_c, ALU.add, ALU.mult)\
               .then_inc(sem("c_steps"), 1)
            dve.wait_ge(sem("c_steps"), 2)
            dve.tensor_scalar(ada_c, ada_c, 0.5, None, ALU.mult).then_inc(sem("c_steps"), 1)
            dve.wait_ge(sem("c_steps"), 4)
            dve.tensor_tensor(stat[:, :, 2:4], ada_c, stat[:, :, 0:2], ALU.subtract)\
               .then_inc(sem("c_lo"), 1)

        def ada_bank(ph):
            return acc[:, ph.banks, :]

        def ada_group(ph, i, part):
            return i * (len(ph.ada_items()) // 8) + (ph.ada_base + part)

        def ada_block(pe, ph):
            def block(i, t, b):
                if b % 4:
                    return None
                q = ph.ada_items().index(t)
                kt, bank = (2 * q + b // 4) % KT, ada_bank(ph)
                if kt == 0:
                    pe.wait_ge(sem("c_lo"), 1)
                    pe.wait_ge(sem("small2_loaded"), 48)
                    wait(pe, "ada_mod", ada_group(ph, i, q // 8))
                ws = slice(b * P, (b + 4) * P)
                pe.matmul(bank[0:4, :], stat[:, kt, :], w_hi[:, t % SPLIT, ws], start=(kt == 0), stop=False)
                ins = pe.matmul(bank[0:4, :], stat[:, kt, :], w_lo[:, t % SPLIT, ws], start=False,
                                stop=(kt == KT - 1))
                return ins
            return block

        def ada_mix(who, eng, ph, part):
            def act(i):
                n = ada_group(ph, i, part)
                wait(eng, "item_used", i * ph.ipb + (ph.g0 + ph.ada_items()[8 * part + 7] + 1))
                wait(eng, "ada_turned", n)
                eng.activation(ada_row[0:4, :], ada_bank(ph)[0:4, :], ACT.Copy)\
                   .then_inc(sem("ada_row_ready"), 1)
                yield
                yield

            def pe(i):
                yield
                n = ada_group(ph, i, part)
                wait(eng, "ada_row_ready", n + 1)
                wait(eng, "ada_mod", n)
                to = ada_bank(ph)
                for c in range(4):
                    ins = eng.matmul(to[:, 2 * c:2 * c + 2], ada_row[0:4, c * P:(c + 1) * P],
                                     ada_sel[0:4, :], start=True, stop=True)
                ins.then_inc(sem("ada_turned"), 1)
                yield

            def dve(i):
                yield
                n = ada_group(ph, i, part)
                wait(eng, "ada_turned", n + 1)
                b = gains[:, bass.ds(n * 4 + 96, 4)]
                eng.tensor_tensor(mod[:, :, bass.ds(n * 4, 4)],
                                  ada_bank(ph)[:, 0:8].rearrange("p (c v) -> p v c", v=2),
                                  bc(b, 2), ALU.add).then_inc(sem("ada_mod"), 1)
                yield
            return dict(act=act, pe=pe, dve=dve)[who]

        ar = Area(KT * S)
        s0 = ar.take(NH, 2, HD)
        lbs = ar.take(NH, 2, 3)
        two_base = ar.at
        lbt = ar.take(2, 2, NH)
        c_z = ar.take(3, S)
        c_p = ar.take(2, 3)
        c_th, c_kk, c_lf, c_w = ar.take(2, S), ar.take(2, S), ar.take(2, S), ar.take(2, S)
        c_one = ar.take(S)
        c_cum = ar.take(2, S + 1)
        c_vT, c_kT = ar.take(2, P), ar.take(4, P)
        c_d = Chain("ctx_dve_steps", per=5)

        def ctx_prologue_act(act):
            act.wait_ge(sem("lb_handoff"), 1)
            act.activation(lbt[:, 1], lbt[:, 0], ACT.Tanh, scale=0.5).then_inc(sem("lb_handoff"), 1)

        def ctx_prologue_dve(dve):
            dve.wait_ge(sem("small2_loaded"), 48)
            dve.tensor_tensor(lbt[:, 0], lbl[:, :, 0, :], lbl[:, :, 1, :], ALU.subtract)\
               .then_inc(sem("lb_handoff"), 1)
            dve.wait_ge(sem("lb_handoff"), 2)
            v = lambda k: lbs[:, :, :, k].rearrange("p h d -> p d h")
            dve.tensor_scalar(v(0), lbt[:, 1], -0.25, 0.25, ALU.mult, ALU.add)
            dve.tensor_scalar(v(1), lbt[:, 1], 0.25, 0.75, ALU.mult, ALU.add)
            dve.tensor_scalar(v(2), lbt[:, 1], 0.25, -0.25, ALU.mult, ALU.add)
            dve.memset(c_one, 1.0)
            dve.memset(c_cum, 0.0).then_inc(sem("ctx_ready"), 1)
            dve.wait_ge(sem("ctx_ready"), 1)

        def ctx_mix_act(act):
            def gen(i):
                wait(act, "tile_out", PHD["ctx"].tile_number(i, 1) + 1)
                act.activation(c_th, c_z[:, 0:2, :], ACT.Tanh, scale=0.5).then_inc(sem("hgrn_tanh"), 1)
                yield
                wait(act, "hgrn_par", i + 1)
                act.wait_ge(sem("hgrn_tanh"), i + 1)
                for d in range(2):
                    ins = act.activation(c_lf[:, d, :], c_th[:, d, :], ACT.Ln, scale=c_p[:, d, 0:1],
                                         bias=c_p[:, d, 1:2])
                ins.then_inc(sem("hgrn_log"), 1)
                yield
                yield
                wait(act, "ctx_cum", i + 1)
                act.activation(c_w[:, 0, :], c_cum[:, 0, 1:S + 1], ACT.Exp)
                act.activation(c_w[:, 1, :], c_cum[:, 1, 0:S], ACT.Exp).then_inc(sem("ctx_decay"), 1)
                yield
                yield
                wait(act, "hgrn_kT", i + 1)
                act.activation(c_kT, mix[:, 1, :].rearrange("p (a b) -> p a b", a=4), ACT.Copy)\
                   .then_inc(sem("hgrn_kT_out"), 1)
                yield
                yield
                yield
            return gen

        def ctx_mix_dve(dve):
            ch = c_d

            def gen(i):
                ch.begin(dve, i)
                dve.tensor_copy(c_p, lbs[:, bass.ds(i, 1), :, :].squeeze(1)).then_inc(sem("hgrn_par"), 1)
                yield
                wait(dve, "hgrn_vT", i + 1)
                ch.step(dve.tensor_copy(c_vT, A2(mix[:, 0, 0:2 * P], a=2)))
                wait(dve, "hgrn_tanh", i + 1)
                dve.wait_ge(sem("hgrn_par"), i + 1)
                for d in range(2):
                    ch.step(dve.tensor_scalar(c_kk[:, d, :], c_th[:, d, :], c_p[:, d, 2:3],
                                              c_p[:, d, 0:1], ALU.mult, ALU.add))
                yield
                wait(dve, "hgrn_log", i + 1)
                ch.step(dve.tensor_tensor_scan(c_cum[:, 0, 0:S][:, ::-1], c_one, c_lf[:, 0, ::-1], 0.0,
                                               ALU.mult, ALU.add))
                dve.tensor_tensor_scan(c_cum[:, 1, 1:S + 1], c_one, c_lf[:, 1, :], 0.0,
                                       ALU.mult, ALU.add).then_inc(sem("ctx_cum"), 1)
                yield
                wait(dve, "ctx_decay", i + 1)
                ch.settle()
                dve.tensor_tensor(c_w, c_w, c_kk, ALU.mult).then_inc(sem("ctx_kw"), 1)
                yield
                yield
                yield
                yield
                wait(dve, "ctx_state", i + 1)
                ch.step(dve.tensor_copy(s0[:, bass.ds(i, 1), :, :].squeeze(1),
                                        A2(mix[:, 2, 0:2 * P], a=2)))
                yield
                ch.end()
            return gen

        def ctx_mix_pe(pe):
            def gen(i):
                wait(pe, "tile_out", PHD["ctx"].tile_number(i, 2) + 1)
                for k in range(2):
                    ins = pe.transpose(mix[:, 0, k * P:(k + 1) * P], c_z[:, 2, k * P:(k + 1) * P], ident)
                ins.then_inc(sem("hgrn_vT"), 1)
                yield
                yield
                yield
                yield
                wait(pe, "ctx_kw", i + 1)
                for d in range(2):
                    for k in range(2):
                        ins = pe.transpose(mix[:, 1, (2 * d + k) * P:(2 * d + k + 1) * P],
                                           c_w[:, d, k * P:(k + 1) * P], ident)
                ins.then_inc(sem("hgrn_kT"), 1)
                yield
                yield
                wait(pe, "hgrn_kT_out", i + 1)
                for d in range(2):
                    for k in range(2):
                        ins = pe.matmul(mix[:, 2, d * P:(d + 1) * P], c_kT[:, 2 * d + k, :],
                                        c_vT[:, k, :], start=(k == 0), stop=(k == 1))
                ins.then_inc(sem("ctx_state"), 1)
                yield
                yield
            return gen

        ar = Area(0)
        d_t, dl = ar.take(4, S), ar.take(9, S)
        dil_mask, ld_dil = const(ar, "dil")
        rope_cs, rope_sn = ar.take(S), ar.take(S)
        dl_vT = ar.take(6, P)
        g_par = ar.take(2)
        r0 = ar.at
        dl_p, dl_pT = ar.take(6, S), ar.take(6, S)
        one_alt = Area(r0)
        d_bc, d_e, d_x, d_z = one_alt.take(2, 2, S), one_alt.take(2, 2, S), one_alt.take(4, P), \
            one_alt.take(4, P)
        d_bq, d_y = ar.take(2, 2, S), ar.take(4, P)
        d_bv, d_bk, d_kt = ar.take(4, P), ar.take(2, P), ar.take(2, P)
        d_wn, d_v1, d_v2 = ar.take(2, P), ar.take(2, P), ar.take(2, P)
        d_s, d_qd = ar.take(2, P), ar.take(2, P)
        d_c = ar.take(3, S)
        d_th = ar.take(3, S)
        d_kq = ar.take(2, S)
        lev, ld_lev = const(ar, "level")
        neg, ld_neg = const(ar, "neg")
        d_par, d_gt = ar.take(NH, 16), ar.take(NH, 16)
        d_hp, d_gs = ar.take(16), ar.take(16)
        dl_m = ar.take(2, 4)
        g_row = ar.take(S)
        ar = Area(r0)
        tri, ld_tri = const(ar, "tri")
        gsign, ld_gsign = const(ar, "gsign")
        ropef, ld_ropef = const(ar, "ropef")
        ropes, ld_ropes = const(ar, "ropes")
        g_x, g_a, g_b, g_l = [ar.take(S) for _ in range(4)]
        g_T, g_T2, g_tot = ar.take(2, 32), ar.take(2, 32), ar.take(2, 16)
        g_na = ar.take(2)
        r_ang, r_k, r_cos, r_sin = [ar.take(S) for _ in range(4)]
        r_pos = ar.take(S)
        assert ar.at <= r0 + 6000
        GQ = dict(g=0, b=4, gb=8, tail=12)

        def gate_dve(dve):
            c = sem("gate_dve_steps")
            n = [0]

            def do(ins):
                ins.then_inc(c, 1)
                n[0] += 1

            def settle():
                dve.wait_ge(c, n[0])
            R = slice(0, 32)
            dve.wait_ge(sem("one_loaded"), 16 * GATE_LOADS)
            do(dve.tensor_copy(r_ang[R], r_pos[R].bitcast(I32)))
            settle()
            do(dve.tensor_scalar(r_ang[R], r_ang[R], ropef[R, 0:1], None, ALU.mult))
            settle()
            MAGIC = 12582912.0
            two_pi = 2 * np.pi
            c1 = float(np.float32(6.28125))
            c2 = float(np.float32(two_pi - c1))
            c3 = float(np.float32(two_pi - c1 - c2))
            for out, shift in ((r_cos, 0.25), (r_sin, 0.0)):
                do(dve.tensor_scalar(r_k[R], r_ang[R], float(1 / two_pi), shift, ALU.mult, ALU.add))
                settle()
                do(dve.tensor_scalar(r_k[R], r_k[R], MAGIC, None, ALU.add))
                settle()
                do(dve.tensor_scalar(r_k[R], r_k[R], MAGIC, None, ALU.subtract))
                settle()
                do(dve.scalar_tensor_tensor(out[R], r_k[R], -c1, r_ang[R], ALU.mult, ALU.add))
                settle()
                do(dve.scalar_tensor_tensor(out[R], r_k[R], -c2, out[R], ALU.mult, ALU.add))
                settle()
                do(dve.scalar_tensor_tensor(out[R], r_k[R], -c3, out[R], ALU.mult, ALU.add))
                settle()
                do(dve.tensor_scalar(out[R], out[R], float(shift * two_pi), 3.1415925, ALU.add, ALU.min))
                settle()
                ins = dve.tensor_scalar(out[R], out[R], -3.1415925, None, ALU.max)
                ins.then_inc(sem("rope_angle"), 1)
            dve.wait_ge(sem("rope_sine"), 2)
            do(dve.tensor_scalar(rope_sn[R], rope_sn[R], ropes[R, 0:1], None, ALU.mult))

            wait(dve, "tile_out", PHD["gate"].t0 + 1)
            do(dve.tensor_scalar(g_x[R], d_t[R, 0, :], gsign[R, 0:1], g_par[R, 0:1], ALU.mult, ALU.add))
            settle()
            do(dve.tensor_scalar(g_b[R], g_x[R], 0.0, None, ALU.max))
            dve.scalar_tensor_tensor(g_a[R], g_x[R], -1.0, g_x[R], ALU.mult, ALU.min)\
               .then_inc(sem("gate_minus_abs"), 1)
            dve.wait_ge(sem("gate_soft"), 1)
            do(dve.tensor_tensor(g_b[R], g_b[R], g_l[R], ALU.add))
            do(dve.tensor_scalar(g_na[R, 1:2], g_na[R, 0:1], -1.0, None, ALU.mult))
            settle()
            dve.tensor_scalar(g_l[R], g_b[R], g_na[R, 1:2], None, ALU.mult).then_inc(sem("gate_handoff"), 1)
            dve.wait_ge(sem("gate_handoff"), 2)
            dve.tensor_copy(g_T, A2(mix[:, 0, 0:64], a=2)).then_inc(sem("gate_handoff"), 1)
            dve.wait_ge(sem("gate_handoff"), 4)
            for k in range(2):
                f = mix[:, 1, 64 * k:64 * k + 8]
                b = mix[:, 1, 64 * k + 40:64 * k + 48]
                do(dve.tensor_copy(g_T2[:, k, 0:8], f))
                do(dve.tensor_copy(g_T2[:, k, 8:16], b))
                do(dve.tensor_copy(g_tot[:, k, :], mix[:, 1, 128 + 32 * k:128 + 32 * k + 16]))
            settle()
            dve.tensor_tensor(g_T2[:, :, 16:32], g_T2[:, :, 0:16], g_T[:, :, 16:32], ALU.add)\
               .then_inc(sem("gate_handoff"), 1)
            dve.wait_ge(sem("gate_handoff"), 5)

            def hv(kind):
                return d_gt[:, :, GQ[kind]:GQ[kind] + 4].rearrange("p h (d k) -> p k d h", d=2)

            def tv(v, at):
                return v[:, :, at:at + 16].rearrange("p k (d h) -> p k d h", d=2)
            for k in range(2):
                do(dve.tensor_scalar(hv("g")[:, k], tv(g_T2, 0)[:, k], -1.0, None, ALU.mult))
                do(dve.tensor_copy(hv("b")[:, k], tv(g_T, 16)[:, k]))
                do(dve.tensor_copy(hv("gb")[:, k], tv(g_T2, 16)[:, k]))
                do(dve.tensor_tensor(hv("tail")[:, k], tv(g_tot, 0)[:, k], tv(g_T2, 0)[:, k],
                                     ALU.subtract))
            settle()
            dve.wait_ge(sem("gate_handoff"), 6)
            dve.tensor_copy(g_row[R], mix[0:32, 2, 0:S]).then_inc(sem("gate_row_out"), 1)
            dve.wait_ge(sem("gate_exp"), 1)
            dve.tensor_scalar(d_gt[:, :, 4:8], d_gt[:, :, 4:8], 0.5, None, ALU.mult)\
               .then_inc(sem("gate_done"), 1)
            dve.wait_ge(sem("gate_done"), 1)

        def gate_act(act):
            R = slice(0, 32)
            for k, (out, a) in enumerate(((rope_cs, r_cos), (rope_sn, r_sin))):
                wait(act, "rope_angle", k + 1)
                act.activation(out[R], a[R], ACT.Sin).then_inc(sem("rope_sine"), 1)
            act.wait_ge(sem("gate_minus_abs"), 1)
            act.activation(g_a[R], g_a[R], ACT.Exp).then_inc(sem("gate_act_steps"), 1)
            act.activation(g_na[R, 0:1], g_par[R, 1:2], ACT.Exp).then_inc(sem("gate_act_steps"), 1)
            act.wait_ge(sem("gate_act_steps"), 2)
            act.activation(g_l[R], g_a[R], ACT.Ln, bias=1.0).then_inc(sem("gate_soft"), 1)
            act.wait_ge(sem("gate_row_out"), 1)
            act.activation(d_gt[:, :, 4:16], d_gt[:, :, 4:16], ACT.Exp).then_inc(sem("gate_exp"), 1)

        def gate_pe(pe):
            pe.wait_ge(sem("gate_handoff"), 1)
            for k in range(2):
                ins = pe.transpose(mix[:, 0, 32 * k:32 * k + 32], g_l[0:32, k * P:(k + 1) * P],
                                   ident[0:32, 0:32])
            ins.then_inc(sem("gate_handoff"), 1)
            pe.wait_ge(sem("gate_handoff"), 3)
            for k in range(2):
                for d in range(2):
                    pe.matmul(mix[:, 1, 64 * k + 32 * d:64 * k + 32 * d + 32],
                              tri[:, d * P:(d + 1) * P], g_T[:, k, :], start=True, stop=True)
                ins = pe.matmul(mix[:, 1, 128 + 32 * k:128 + 32 * k + 32], ones, g_T[:, k, :],
                                start=True, stop=True)
            ins.then_inc(sem("gate_handoff"), 1)
            pe.wait_ge(sem("gate_handoff"), 5)
            for k in range(2):
                ins = pe.transpose(mix[0:32, 2, k * P:(k + 1) * P], g_T2[:, k, :], ident)
            ins.then_inc(sem("gate_handoff"), 1)

        FIRST, SECOND = (0, 1), (1, 0)
        dd = {n: Chain(f"delta_{n}_steps") for n in ("act", "dve")}

        def delta_act(act):
            ch = dd["act"]

            def gen(i):
                ch.begin(act, i)
                yield
                yield
                yield
                yield
                wait(act, "delta_conv", i + 1)
                act.activation(d_th, d_c, ACT.Tanh, scale=0.5).then_inc(sem("delta_tanh"), 1)
                yield
                wait(act, "delta_silu", i + 1)
                act.activation(d_th[:, 0:2, :], d_c[:, 0:2, :], ACT.Square, scale=0.5)\
                   .then_inc(sem("delta_square"), 1)
                yield
                wait(act, "delta_norm", i + 1)
                rsqrt_act(act, ch, A2(mix[:, 0, :], a=2), d_kq, d_e[:, 0, :, :], 1.0, EPS,
                          "delta_guess")
                yield
                yield
                yield
                wait(act, "delta_diff", i + 1)
                act.activation(d_e, d_e, ACT.Exp).then_inc(sem("delta_gamma"), 1)
                for d in range(2):
                    k = SECOND[d]
                    ins = act.activation(d_wn[:, d, :], d_bc[:, d, 1, k * P:(k + 1) * P], ACT.Exp)
                ins.then_inc(sem("delta_eg"), 1)
                wait(act, "delta_turned", i + 1)
                kT = lambda k: mix[:, 1, k * P:(k + 1) * P]
                vT = lambda k: mix[:, 1, (2 + k) * P:(3 + k) * P]
                for d in range(2):
                    for k in range(2):
                        g = GQ["b"] + 2 * d + k
                        act.activation(d_bv[:, 2 * d + k, :], vT(k), ACT.Copy, scale=d_gs[:, g:g + 1])
                    g = GQ["gb"] + 2 * d + SECOND[d]
                    act.activation(d_bk[:, d, :], kT(SECOND[d]), ACT.Copy, scale=d_gs[:, g:g + 1])
                    g = GQ["tail"] + 2 * d + FIRST[d]
                    ins = act.activation(d_kt[:, d, :], kT(FIRST[d]), ACT.Copy, scale=d_gs[:, g:g + 1])
                ins.then_inc(sem("delta_TM"), 1)
                yield
                for s in range(13):
                    yield
                wait(act, "delta_v1", i + 1)
                act.activation(d_wn, A2(mix[:, 3, 2 * P:4 * P], a=2), ACT.Copy, scale=-1.0)\
                   .then_inc(sem("delta_wn"), 1)
                act.activation(d_th[:, 2, :], d_t[:, 3, :], ACT.Tanh, scale=0.5)\
                   .then_inc(sem("rule_gtanh"), 1)
                yield
                yield
                yield
                wait(act, "rule_o", i + 1)
                act.activation(d_th[:, 0, :], mix[:, 0, 0:S], ACT.Square).then_inc(sem("rule_osq"), 1)
                yield
                wait(act, "rule_onorm", i + 1)
                rsqrt_act(act, ch, mix[:, 1, 0:S], d_y[:, 0:2, :].rearrange("p a b -> p (a b)"),
                          d_y[:, 2:4, :].rearrange("p a b -> p (a b)"), 1.0 / HD, EPS, "rule_guess")
                yield
                wait(act, "rule_out", i + 1)
                act.activation(act_b[:, bass.ds(i, 1), 0:S].squeeze(1), d_c[:, 0, :], ACT.Copy)\
                   .then_inc(sem("rule_hi"), 1)
                yield
                ch.end()
            return gen

        def delta_dve(dve):
            ch = dd["dve"]

            def gen(i):
                ch.begin(dve, i)
                wait(dve, "rule_hi", i)
                ch.step(dve.tensor_copy(d_hp, d_par[:, bass.ds(i, 1), :].squeeze(1)))
                ch.step(dve.tensor_copy(d_gs, d_gt[:, bass.ds(i, 1), :].squeeze(1)))
                ch.settle()
                for c in range(3):
                    wait(dve, "tile_out", PHD["one"].tile_number(i, c) + 1)
                    ch.step(dve.tensor_scalar(d_c[:, c, :], d_t[:, c, :], d_hp[:, 5 * c + 2:5 * c + 3],
                                              None, ALU.mult))
                    for j in (0, 1, 3, 4):
                        s = j - 2
                        o = slice(max(0, -s), S - max(0, s))
                        a = slice(max(0, s), S + min(0, s))
                        ch.settle()
                        ins = dve.scalar_tensor_tensor(d_c[:, c, o], d_t[:, c, a],
                                                       d_hp[:, 5 * c + j:5 * c + j + 1], d_c[:, c, o],
                                                       ALU.mult, ALU.add)
                        if c < 2 or j < 4:
                            ch.step(ins)
                    if c < 2:
                        yield
                    if c == 0:
                        yield
                ins.then_inc(sem("delta_conv"), 1)
                yield
                wait(dve, "delta_tanh", i + 1)
                dve.scalar_tensor_tensor(d_c, d_th, 1.0, d_c, ALU.add, ALU.mult)\
                   .then_inc(sem("delta_silu"), 1)
                yield
                yield
                wait(dve, "delta_guess", i + 1)
                ch.step(dve.tensor_scalar(d_bq[:, 0, :, :], A2(mix[:, 0, :], a=2), EPS, None, ALU.add))
                y, t, w = d_kq, d_bq[:, 1, :, :], d_bq[:, 0, :, :]
                ch.step(dve.tensor_tensor(t, y, y, ALU.mult))
                ch.settle()
                ch.step(dve.scalar_tensor_tensor(t, t, -0.5, w, ALU.mult, ALU.mult))
                ch.settle()
                ch.step(dve.scalar_tensor_tensor(t, t, 1.5, y, ALU.add, ALU.mult))
                ch.settle()
                ch.step(dve.scalar_tensor_tensor(d_kq[:, 0, :], d_c[:, 1, :], 0.5, t[:, 1, :],
                                                 ALU.mult, ALU.mult))
                dve.scalar_tensor_tensor(d_kq[:, 1, :], d_c[:, 0, :], 0.5 * HD ** -0.5, t[:, 0, :],
                                         ALU.mult, ALU.mult).then_inc(sem("delta_kq"), 1)
                wait(dve, "bc_loaded", i * 16 + 16)
                for d in range(2):
                    for k in range(2):
                        ins = dve.scalar_tensor_tensor(
                            d_e[:, d, :, k * P:(k + 1) * P], d_bc[:, d, :, k * P:(k + 1) * P],
                            d_gs[:, 2 * d + k:2 * d + k + 1],
                            A2(neg[:, 2 * d * P:(2 * d + 2) * P], a=2), ALU.add, ALU.add)
                ins.then_inc(sem("delta_diff"), 1)
                yield
                yield
                yield
                wait(dve, "delta_gamma", i + 1)
                wait(dve, "delta_gram", i + 1)
                for d in range(2):
                    for kind in range(2):
                        g = mix[:, 2, :].rearrange("p (k c j) -> p k c j", k=2, c=2)[:, :, kind, :]
                        dve.tensor_tensor(A2(d_bq[:, d, kind, :], a=2), A2(d_e[:, d, kind, :], a=2), g,
                                          ALU.mult)
                wait(dve, "delta_eg", i + 1)
                wait(dve, "delta_kq", i + 1)
                for d in range(2):
                    k = SECOND[d]
                    ins = dve.tensor_tensor(d_qd[:, d, :], d_kq[:, 1, k * P:(k + 1) * P],
                                            d_wn[:, d, :], ALU.mult)
                ins.then_inc(sem("delta_bq"), 1)
                yield
                dve.wait_ge(sem("delta_bq"), i + 1)
                for d in range(2):
                    ins = dve.tensor_tensor(d_z[:, 2 * d:2 * d + 2, :], A2(d_bq[:, d, 0, :], a=2),
                                            bc(lev[:, 0:P], 2), ALU.mult)
                ch.step(ins)
                wait(dve, "delta_ax", i * 7 + 1)
                ch.step(dve.tensor_tensor(d_y, A2(mix[:, 2, :], a=4), bc(lev[:, 0:P], 4), ALU.mult))
                ch.settle()
                dve.tensor_tensor(d_z, bc(ident, 4), d_z, ALU.subtract)
                dve.tensor_tensor(d_x, bc(ident, 4), d_y, ALU.subtract).then_inc(sem("delta_level"), 1)
                yield
                for s in range(1, 7):
                    wait(dve, "delta_ax", i * 7 + (s + 1))
                    dve.tensor_tensor(d_y, A2(mix[:, 2, :], a=4), bc(lev[:, s * P:(s + 1) * P], 4),
                                      ALU.mult).then_inc(sem("delta_y"), 1)
                    yield
                    wait(dve, "delta_xy", i * 6 + s)
                    ins = dve.tensor_tensor(d_z, d_z, A2(mix[:, 4, :], a=4), ALU.subtract)
                    if s < 6:
                        ins = dve.tensor_tensor(d_x, d_x, A2(mix[:, 3, :], a=4), ALU.subtract)
                    ins.then_inc(sem("delta_level"), 1)
                    yield
                wait(dve, "delta_first", i + 1)
                dve.tensor_copy(d_v1, A2(mix[:, 3, 0:2 * P], a=2)).then_inc(sem("delta_v1"), 1)
                yield
                wait(dve, "delta_st", i + 1)
                dve.tensor_copy(d_s, A2(mix[:, 4, 0:2 * P], a=2)).then_inc(sem("delta_s"), 1)
                yield
                wait(dve, "delta_second", i + 1)
                dve.tensor_copy(d_v2, A2(mix[:, 2, 0:2 * P], a=2)).then_inc(sem("delta_v2"), 1)
                yield
                wait(dve, "rule_gtanh", i + 1)
                ch.step(dve.scalar_tensor_tensor(d_c[:, 1, :], d_th[:, 2, :], 1.0, d_t[:, 3, :],
                                                 ALU.add, ALU.mult))
                yield
                wait(dve, "rule_guess", i + 1)
                y = d_y[:, 0:2, :].rearrange("p a b -> p (a b)")
                w = d_y[:, 2:4, :].rearrange("p a b -> p (a b)")
                newton(ch, dve, mix[:, 1, 0:S], y, d_th[:, 1, :], w, 1.0 / HD, EPS)
                ch.step(dve.scalar_tensor_tensor(d_c[:, 0, :], mix[:, 0, 0:S], d_hp[:, 15:16],
                                                 d_th[:, 1, :], ALU.mult, ALU.mult))
                ch.settle()
                dve.scalar_tensor_tensor(d_c[:, 0, :], d_c[:, 0, :], 0.5, d_c[:, 1, :], ALU.mult,
                                         ALU.mult).then_inc(sem("rule_out"), 1)
                yield
                wait(dve, "rule_hi", i + 1)
                o = act_b[:, bass.ds(i, 1), :].squeeze(1)
                ch.step(dve.tensor_tensor(o[:, S:2 * S], d_c[:, 0, :], o[:, 0:S], ALU.subtract))
                yield
                ch.end()
            return gen

        def delta_pe(pe):
            def gen(i):
                yield
                yield
                yield
                yield
                yield
                yield
                wait(pe, "dil_lo", i)
                wait(pe, "delta_square", i + 1)
                pe.matmul(mix[:, 0, :], ones, d_th[:, 0:2, :], start=True, stop=True)\
                  .then_inc(sem("delta_norm"), 1)
                yield
                yield
                yield
                wait(pe, "delta_kq", i + 1)
                for k in range(2):
                    pe.transpose(mix[:, 1, k * P:(k + 1) * P], d_kq[:, 0, k * P:(k + 1) * P], ident)
                for k in range(2):
                    ins = pe.transpose(mix[:, 1, (2 + k) * P:(3 + k) * P], d_c[:, 2, k * P:(k + 1) * P],
                                       ident)
                ins.then_inc(sem("delta_turned"), 1)
                for k in range(2):
                    ins = pe.matmul(mix[:, 2, 2 * k * P:2 * (k + 1) * P], d_kq[:, 0, k * P:(k + 1) * P],
                                    d_kq[:, :, k * P:(k + 1) * P], start=True, stop=True)
                ins.then_inc(sem("delta_gram"), 1)
                yield
                wait(pe, "delta_bq", i + 1)
                for m in range(4):
                    b = d_bq[:, m // 2, 0, (m % 2) * P:(m % 2 + 1) * P]
                    ins = pe.transpose(mix[:, 2, m * P:(m + 1) * P], b, ident)
                ins.then_inc(sem("delta_ax"), 1)
                yield
                for s in range(1, 7):
                    wait(pe, "delta_level", i * 7 + s)
                    for m in range(4):
                        b = d_bq[:, m // 2, 0, (m % 2) * P:(m % 2 + 1) * P]
                        ins = pe.matmul(mix[:, 2, m * P:(m + 1) * P], b, d_x[:, m, :], start=True,
                                        stop=True)
                    ins.then_inc(sem("delta_ax"), 1)
                    yield
                    wait(pe, "delta_y", i * 6 + s)
                    for m in range(4):
                        if s < 6:
                            pe.matmul(mix[:, 3, m * P:(m + 1) * P], d_z[:, m, :], d_y[:, m, :],
                                      start=True, stop=True)
                        ins = pe.matmul(mix[:, 4, m * P:(m + 1) * P], d_y[:, m, :], d_z[:, m, :],
                                        start=True, stop=True)
                    ins.then_inc(sem("delta_xy"), 1)
                    yield
                wait(pe, "delta_level", i * 7 + 7)
                wait(pe, "delta_TM", i + 1)
                for d in range(2):
                    pe.matmul(mix[:, 3, d * P:(d + 1) * P], d_z[:, 2 * d + FIRST[d], :],
                              d_bv[:, 2 * d + FIRST[d], :], start=True, stop=True)
                    ins = pe.matmul(mix[:, 3, (2 + d) * P:(3 + d) * P], d_bk[:, d, :],
                                    d_z[:, 2 * d + SECOND[d], :], start=True, stop=True)
                ins.then_inc(sem("delta_first"), 1)
                yield
                wait(pe, "delta_v1", i + 1)
                for d in range(2):
                    ins = pe.matmul(mix[:, 4, d * P:(d + 1) * P], d_kt[:, d, :], d_v1[:, d, :],
                                    start=True, stop=True)
                ins.then_inc(sem("delta_st"), 1)
                yield
                wait(pe, "delta_s", i + 1)
                wait(pe, "delta_wn", i + 1)
                for d in range(2):
                    pe.matmul(mix[:, 2, d * P:(d + 1) * P], d_z[:, 2 * d + SECOND[d], :],
                              d_bv[:, 2 * d + SECOND[d], :], start=True, stop=False)
                    ins = pe.matmul(mix[:, 2, d * P:(d + 1) * P], d_wn[:, d, :], d_s[:, d, :],
                                    start=False, stop=True)
                ins.then_inc(sem("delta_second"), 1)
                yield
                wait(pe, "delta_v2", i + 1)
                for k in range(2):
                    o, ks = mix[:, 0, k * P:(k + 1) * P], slice(k * P, (k + 1) * P)
                    f, b = (0, 1) if k == 0 else (1, 0)
                    pe.matmul(o, d_v1[:, f, :], d_bq[:, f, 1, ks], start=True, stop=False)
                    pe.matmul(o, d_s[:, b, :], d_qd[:, b, :], start=False, stop=False)
                    ins = pe.matmul(o, d_v2[:, b, :], d_bq[:, b, 1, ks], start=False, stop=True)
                ins.then_inc(sem("rule_o"), 1)
                yield
                wait(pe, "rule_osq", i + 1)
                pe.matmul(mix[:, 1, 0:S], ones, d_th[:, 0, :], start=True, stop=True)\
                  .then_inc(sem("rule_onorm"), 1)
                yield
                yield
            return gen

        dl_d = Chain("dil_dve_steps", per=3)
        dl_r = Chain("rope_dve_steps")

        def rope_dve(dve):
            ch = dl_r

            def gen(i):
                ch.begin(dve, i)
                R = slice(0, 32)
                for half_ in range(2):
                    t = dl[R, 3 * half_:3 * half_ + 3, :]
                    wait(dve, "tile_out", PHD["one"].tile_number(i, 6 + 3 * half_) + 1)
                    ch.step(dve.tensor_tensor(d_c[R], t, bc(rope_cs[R], 3), ALU.mult))
                    ch.step(dve.stream_shuffle(d_th[R], t, [(m + 16) % 32 for m in range(32)]))
                    yield
                    ch.settle()
                    ch.step(dve.tensor_tensor(d_th[R], d_th[R], bc(rope_sn[R], 3), ALU.mult))
                    ch.settle()
                    ins = dve.tensor_tensor(t, d_c[R], d_th[R], ALU.add)
                    if half_:
                        ins.then_inc(sem("dil_rope"), 1)
                        yield
                    else:
                        ch.step(ins)
                        for _ in range(6):
                            yield
                        ch.settle()
                ch.end()
            return gen

        def dil_dve(dve):
            ch = dl_d

            def gen(i):
                ch.begin(dve, i)
                wait(dve, "dil_scores", i + 1)
                ch.step(dve.scalar_tensor_tensor(
                    dl_p.rearrange("p a b -> p (a b)"), mix[:, 0:3, :].rearrange("p a b -> p (a b)"),
                    HD ** -0.5, dil_mask, ALU.mult, ALU.add))
                yield
                ch.settle()
                ch.step(dve.tensor_reduce(dl_m[:, :, 0], dl_p.rearrange("p (q b) s -> p q (b s)", q=2),
                                          AX.X, ALU.max))
                ch.settle()
                dve.tensor_scalar(dl_m[:, :, 1], dl_m[:, :, 0], -1.0, None, ALU.mult)\
                   .then_inc(sem("dil_max"), 1)
                yield
                yield
                wait(dve, "dil_exp", i + 1)
                ch.step(dve.reciprocal(dl_m[:, :, 3], dl_m[:, :, 2]))
                ch.settle()
                for q in range(2):
                    ins = dve.tensor_scalar(dl_p[:, 3 * q:3 * q + 3, :], dl_p[:, 3 * q:3 * q + 3, :],
                                            dl_m[:, q, 3:4], None, ALU.mult)
                ins.then_inc(sem("dil_probs"), 1)
                yield
                yield
                wait(dve, "dil_turned", i + 1)
                dve.tensor_copy(dl_pT[:, 4:6, :], A2(mix[:, 2, :], a=2))\
                   .then_inc(sem("dil_pT_dve"), 1)
                yield
                wait(dve, "pair_hi", i + 1)
                o = act_b[:, bass.ds(i + NH, 1), S:2 * S].squeeze(1)
                dve.tensor_tensor(o, mix[:, 3, 0:S], act_b[:, bass.ds(i + NH, 1), 0:S].squeeze(1),
                                  ALU.subtract).then_inc(sem("dil_lo"), 1)
                yield
                ch.end()
            return gen

        def dil_act(act):
            def gen(i):
                yield
                wait(act, "dil_vT", i + 1)
                v = mix[:, 3:5, :].rearrange("p a (b c) -> p (a b) c", b=4)
                act.activation(dl_vT, v[:, 0:6, :], ACT.Copy).then_inc(sem("dil_vT_out"), 1)
                yield
                wait(act, "dil_max", i + 1)
                for q in range(2):
                    ins = act.activation(dl_p[:, 3 * q:3 * q + 3, :], dl_p[:, 3 * q:3 * q + 3, :],
                                         ACT.Exp, bias=dl_m[:, q, 1:2], accum_out=dl_m[:, q, 2:3])
                ins.then_inc(sem("dil_exp"), 1)
                yield
                yield
                yield
                wait(act, "dil_turned", i + 1)
                act.activation(dl_pT[:, 0:4, :],
                               mix[:, 0:2, :].rearrange("p a (b c) -> p (a b) c", b=2),
                               ACT.Copy).then_inc(sem("dil_pT_act"), 1)
                yield
                wait(act, "dil_out", i + 1)
                act.activation(act_b[:, bass.ds(i + NH, 1), 0:S].squeeze(1), mix[:, 3, 0:S], ACT.Copy)\
                   .then_inc(sem("pair_hi"), 1)
                yield
            return gen

        def dil_pe(pe):
            def gen(i):
                wait(pe, "dil_rope", i + 1)
                wait(pe, "rule_out", i + 1)
                for q in range(2):
                    for b in range(3):
                        m = 3 * q + b
                        ins = pe.matmul(mix[:, m // 2, (m % 2) * S:(m % 2 + 1) * S],
                                        dl[:, b, q * P:(q + 1) * P], dl[:, 3 + b, :], start=True,
                                        stop=True)
                ins.then_inc(sem("dil_scores"), 1)
                yield
                wait(pe, "tile_out", PHD["one"].tile_number(i, 12) + 1)
                for m in range(6):
                    ins = pe.transpose(mix[:, 3 + m // 4, (m % 4) * P:(m % 4 + 1) * P],
                                       dl[:, 6 + m // 2, (m % 2) * P:(m % 2 + 1) * P], ident)
                ins.then_inc(sem("dil_vT"), 1)
                yield
                yield
                yield
                yield
                wait(pe, "dil_probs", i + 1)
                for m in range(6):
                    for q in range(2):
                        at = (m % 2) * S + q * P
                        ins = pe.transpose(mix[:, m // 2, at:at + P],
                                           dl_p[:, 3 * q + m // 2, (m % 2) * P:(m % 2 + 1) * P], ident)
                ins.then_inc(sem("dil_turned"), 1)
                yield
                wait(pe, "dil_pT_dve", i + 1)
                wait(pe, "dil_pT_act", i + 1)
                wait(pe, "dil_vT_out", i + 1)
                for m in range(6):
                    ins = pe.matmul(mix[:, 3, 0:S], dl_vT[:, m, :], dl_pT[:, m, :], start=(m == 0),
                                    stop=(m == 5))
                ins.then_inc(sem("dil_out"), 1)
                yield
            return gen

        ar = Area(KT * S)
        up, cv, u_th = ar.take(4, S), ar.take(4, S), ar.take(2, S)
        ffn_par = ar.take(44, 6)

        def up_dve(dve, ph):
            def gen(i):
                wait(dve, "tile_out", ph.tile_number(i, 3) + 1)
                for pr in range(2):
                    n = ph.done + pr
                    w = [ffn_par[:, bass.ds(i * 2 + n, 1), :].squeeze(1)[:, c:c + 1]
                         for c in range(6)]
                    c0 = 2 * pr
                    k = sem("up_dve_steps")
                    for h in range(2):
                        ins = dve.tensor_scalar(cv[:, c0 + h, :], up[:, c0 + h, :], w[3 * h + 1], None,
                                                ALU.mult)
                    ins.then_inc(k, 1)
                    dve.wait_ge(k, (i * 2 + n) * 2 + 1)
                    for h in range(2):
                        ins = dve.scalar_tensor_tensor(cv[:, c0 + h, 1:S], up[:, c0 + h, 0:S - 1],
                                                       w[3 * h], cv[:, c0 + h, 1:S], ALU.mult, ALU.add)
                    ins.then_inc(k, 1)
                    dve.wait_ge(k, (i * 2 + n) * 2 + 2)
                    for h in range(2):
                        ins = dve.scalar_tensor_tensor(cv[:, c0 + h, 0:S - 1], up[:, c0 + h, 1:S],
                                                       w[3 * h + 2], cv[:, c0 + h, 0:S - 1], ALU.mult,
                                                       ALU.add)
                    ins.then_inc(sem("up_conv"), 1)
                    yield
                for pr in range(2):
                    n, c0 = ph.done + pr, 2 * pr
                    wait(dve, "up_tanh", i * 2 + (n + 1))
                    dve.scalar_tensor_tensor(cv[:, c0, :], u_th[:, pr, :], 1.0, cv[:, c0, :], ALU.add,
                                             ALU.mult).then_inc(sem("up_silu"), 1)
                    dve.wait_ge(sem("up_silu"), i * 2 + (n + 1))
                    dve.scalar_tensor_tensor(cv[:, c0, :], cv[:, c0, :], 0.5, cv[:, c0 + 1, :],
                                             ALU.mult, ALU.mult).then_inc(sem("up_prod"), 1)
                    yield
                for pr in range(2):
                    n = ph.done + pr
                    wait(dve, "up_hi", i * 2 + (n + 1))
                    o = act_b[:, bass.ds(i * 2 + pr, 1), :].squeeze(1)
                    dve.tensor_tensor(o[:, S:2 * S], cv[:, 2 * pr, :], o[:, 0:S], ALU.subtract)\
                       .then_inc(sem("up_lo"), 1)
                    yield
            return gen

        def up_act(act, ph):
            def gen(i):
                for pr in range(2):
                    wait(act, "up_conv", i * 2 + (ph.done + pr + 1))
                    act.activation(u_th[:, pr, :], cv[:, 2 * pr, :], ACT.Tanh, scale=0.5)\
                       .then_inc(sem("up_tanh"), 1)
                    yield
                for pr in range(2):
                    wait(act, "up_prod", i * 2 + (ph.done + pr + 1))
                    act.activation(act_b[:, bass.ds(i * 2 + pr, 1), 0:S].squeeze(1), cv[:, 2 * pr, :],
                                   ACT.Copy).then_inc(sem("up_hi"), 1)
                    yield
                yield
                yield
            return gen

        def mlp_dve(dve, ph):
            def gen(i):
                n = ph.done // 4
                wait(dve, "tile_out", ph.tile_number(i, 3) + 1)
                dve.scalar_tensor_tensor(cv, up, 0.0, up, ALU.max, ALU.mult)\
                   .then_inc(sem("mlp_square"), 1)
                yield
                wait(dve, "mlp_hi", i + (n + 1))
                o = act_b[:, bass.ds(i * 4, 4), :]
                dve.tensor_tensor(o[:, :, S:2 * S], cv, o[:, :, 0:S], ALU.subtract)\
                   .then_inc(sem("mlp_lo"), 1)
                yield
            return gen

        def mlp_act(act, ph):
            def gen(i):
                n = ph.done // 4
                wait(act, "mlp_square", i + (n + 1))
                act.activation(act_b[:, bass.ds(i * 4, 4), 0:S], cv, ACT.Copy)\
                   .then_inc(sem("mlp_hi"), 1)
                yield
                yield
            return gen

        ar = Area(KT * S + 2048 + 1024)
        part = ar.take(2, S)

        def dve_residual(dve, ph, gate=None):
            def evac(i, k):
                n = ph.tile_number(i, k)
                wait(dve, "half_ready", n + 1)
                a, b, t = acc[:, ph.bank(k), 0:S], half[:, k % 2, :], part[:, k % 2, :]
                if gate is None:
                    ins = dve.tensor_tensor(t, a, b, ALU.add)
                else:
                    ins = dve.scalar_tensor_tensor(t, a, gate(i, k), b, ALU.mult, ALU.add)
                ins.then_inc(sem("tile_out"), 1)
                wait(dve, "tile_out", n + 1)
                xt = x[:, bass.ds(i * 4 + k, 1), :].squeeze(1)
                dve.tensor_tensor(xt, xt, t, ALU.add)
            return evac

        ar = Area(0)
        h_z, y_t = ar.take(5, S), ar.take(3, S)
        dft, ld_dft = const(ar, "dft")
        idft, ld_idft = const(ar, "idft")
        assert ar.at <= KT * S
        ar = Area(two_base)
        y_par, h_gain = ar.take(NH, 13), ar.take(NH)
        h_reset, ld_reset = const(ar, "reset")
        h_reset = A2(h_reset, a=2)
        h_mask = ar.take(4, P)
        h_p, h_g1 = ar.take(2, 3), ar.take(1)
        h_th, h_lf, h_kk, h_a = ar.take(2, S), ar.take(2, S), ar.take(2, S), ar.take(2, S)
        h_e1, h_e2, h_e3, h_e4, h_qa = [ar.take(2, S) for _ in range(5)]
        h_sc, h_vT, h_kT = ar.take(4, P), ar.take(2, P), ar.take(4, P)
        h_s = ar.take(2, 4, P)
        h_o = ar.take(3, S)
        y_hp = ar.take(13)
        y_rs1 = ar.take(1)
        y_c, y_u, y_uT, y_k, y_y, y_w = ar.take(3, S), ar.take(S), ar.take(2, P), ar.take(4, P), \
            ar.take(4, P), ar.take(4, P)
        hh = {n: Chain(f"hg_{n}_steps") for n in ("act", "dve")}

        def update_place(d, c):
            at = [(dd_, cc) for dd_ in range(2) for cc in range(3)
                  if (cc if dd_ == 0 else 3 - cc) % 2 == (c if d == 0 else 3 - c) % 2].index((d, c))
            return mix[:, 3 + (c if d == 0 else 3 - c) % 2, at * P:(at + 1) * P]

        MID, END = (31, 32), (63, 0)

        ar = Area(KT * S)
        f_dft, ld_fdft = const(ar, "dft")
        f_h, f_r, f_h2, f_t = ar.take(S), ar.take(S), ar.take(S), ar.take(512)
        assert ar.at <= KT * S + 2048 + 512
        ar = Area(KT * S + 2048 + 1024 + 512 + 128)
        f_z, f_w1, f_w2, f_w3, f_vec = ar.take(S), ar.take(64), ar.take(64), ar.take(2048), ar.take(3)
        f_nf, ld_nf = const(ar, "notfirst")
        f_win = ar.take(2, 1024)
        f_a, f_b, f_q = ar.take(2, 512), ar.take(2, 512), ar.take(2, 512)
        f_k = ar.take(4, 512)
        f_ps = acc[:, 4:8, :]

        FILTER_START = 4

        def filter_dve(dve):
            for _ in range(FILTER_START + 1):
                yield
            c, n = sem("filter_dve_steps"), [0]

            def do(ins):
                ins.then_inc(c, 1)
                n[0] += 1

            def settle():
                dve.wait_ge(c, n[0])
            R = slice(0, 64)
            dve.wait_ge(sem("two_loaded"), 16 * FILTER_LOADS)
            MAGIC = 12582912.0
            two_pi = 2 * np.pi
            c1 = float(np.float32(6.28125))
            c2 = float(np.float32(two_pi - c1))
            for layer in range(2):
                dve.wait_ge(sem("filter_pre"), layer + 1)
                do(dve.tensor_scalar(f_h[R], f_ps[0:64, 0, 0:S], f_vec[R, layer:layer + 1],
                                     f_vec[R, 2:3], ALU.add, ALU.mult))
                settle()
                do(dve.tensor_scalar(f_r[R], f_h[R], float(1 / two_pi), None, ALU.mult))
                settle()
                do(dve.tensor_scalar(f_r[R], f_r[R], MAGIC, None, ALU.add))
                settle()
                do(dve.tensor_scalar(f_r[R], f_r[R], MAGIC, None, ALU.subtract))
                settle()
                do(dve.scalar_tensor_tensor(f_h[R], f_r[R], -c1, f_h[R], ALU.mult, ALU.add))
                settle()
                do(dve.scalar_tensor_tensor(f_h[R], f_r[R], -c2, f_h[R], ALU.mult, ALU.add))
                settle()
                dve.tensor_scalar(f_h[R], f_h[R], 3.1415925, -3.1415925, ALU.min, ALU.max)\
                   .then_inc(sem("filter_arg"), 1)
                yield
                yield
                yield
            for cb in range(2):
                for k in range(2):
                    win = f_win[:, k, cb * 512:(cb + 1) * 512]
                    m = 2 * cb + k
                    dve.wait_ge(sem("filter_taps"), m + 1)
                    if k == 0 and cb:
                        dve.wait_ge(sem("filter_spec"), 1)
                        dve.wait_ge(sem("filter_power"), 1)
                    do(dve.tensor_tensor(f_t, f_ps[:, 0, :], win, ALU.mult))
                    do(dve.scalar_tensor_tensor(f_q[:, k, :], f_ps[:, 1, :], f_nf[:, k:k + 1], win,
                                                ALU.mult, ALU.mult))
                    settle()
                    do(dve.tensor_tensor(f_a[:, k, :], f_t, f_q[:, k, :], ALU.add))
                    do(dve.tensor_tensor(f_b[:, k, :], f_t, f_q[:, k, :], ALU.subtract))
                    do(dve.tensor_tensor(f_t, f_t, f_t, ALU.mult))
                    do(dve.tensor_tensor(f_q[:, k, :], f_q[:, k, :], f_q[:, k, :], ALU.mult))
                    settle()
                    dve.tensor_tensor(f_q[:, k, :], f_q[:, k, :], f_t, ALU.add)\
                       .then_inc(sem("filter_ab"), 1)
                    yield
                    if k == 0:
                        yield
                dve.wait_ge(sem("filter_power"), cb + 1)
                dve.tensor_copy(y_ss[:, 4 * cb:4 * cb + 4], f_ps[:, 3, 0:4]).then_inc(sem("filter_norm"), 1)
                yield
                yield
                yield
            dve.wait_ge(sem("filter_norm"), 4)
            t, u = f_t[:, 0:NH], f_t[:, 16:16 + NH]
            do(dve.tensor_tensor(u, y_rs, y_rs, ALU.mult))
            settle()
            do(dve.scalar_tensor_tensor(u, u, -0.5, y_ss, ALU.mult, ALU.mult))
            settle()
            do(dve.scalar_tensor_tensor(y_rs, u, 1.5, y_rs, ALU.add, ALU.mult))
            settle()
            dve.drain().then_inc(sem("filter_done"), 1)

        def filter_act(act):
            R = slice(0, 64)
            for _ in range(FILTER_START + 2):
                yield
            for layer in range(2):
                act.wait_ge(sem("filter_arg"), layer + 1)
                act.activation(f_h2[R], f_h[R], ACT.Sin).then_inc(sem("filter_sin"), 1)
                yield
                yield
                yield
            for cb in range(2):
                for _ in range(3 if cb == 0 else 5):
                    yield
                act.wait_ge(sem("filter_spec"), cb + 1)
                if cb:
                    act.wait_ge(sem("scratch_stored"), 64 + 16 * 4)
                act.activation(f_k, f_ps[:, 0:4, :], ACT.Copy).then_inc(sem("filter_spec_out"), 1)
                yield
            act.wait_ge(sem("filter_norm"), 2)
            act.activation(f_t[:, 32:32 + NH], y_ss, ACT.Ln).then_inc(sem("filter_norm"), 1)
            act.wait_ge(sem("filter_norm"), 3)
            act.activation(y_rs, f_t[:, 32:32 + NH], ACT.Exp, scale=-0.5)\
               .then_inc(sem("filter_norm"), 1)
            act.drain().then_inc(sem("filter_done"), 1)
            yield

        def filter_pe(pe):
            for _ in range(FILTER_START):
                yield
            pe.wait_ge(sem("two_loaded"), 16 * FILTER_LOADS)
            pe.matmul(f_ps[0:64, 0, 0:S], f_w1[0:33, :], f_z[0:33, :], start=True, stop=True)\
              .then_inc(sem("filter_pre"), 1)
            yield
            yield
            yield
            pe.wait_ge(sem("filter_sin"), 1)
            pe.matmul(f_ps[0:64, 0, 0:S], f_w2[0:64, :], f_h2[0:64, :], start=True, stop=True)\
              .then_inc(sem("filter_pre"), 1)
            yield
            yield
            yield
            pe.wait_ge(sem("filter_sin"), 2)
            for cb in range(2):
                for k in range(2):
                    m = 2 * cb + k
                    if m:
                        pe.wait_ge(sem("filter_ab"), m)
                    if cb and not k:
                        pe.wait_ge(sem("filter_spec_out"), cb)
                    for d in range(2):
                        at = d * 1024 + cb * 512
                        ins = pe.matmul(f_ps[:, d, :], f_h2[0:64, k * P:(k + 1) * P],
                                        f_w3[0:64, at:at + 512], start=True, stop=True)
                    ins.then_inc(sem("filter_taps"), 1)
                    yield
                    yield
                pe.wait_ge(sem("filter_ab"), 2 * cb + 2)
                for j in range(4):
                    for k in range(2):
                        ins = pe.matmul(f_ps[:, 3, j:j + 1], f_q[:, k, j * P:(j + 1) * P], ones[:, 0:1],
                                        start=(k == 0), stop=(k == 1))
                ins.then_inc(sem("filter_power"), 1)
                for part_, src in enumerate((f_a, f_b)):
                    for q in range(2):
                        if part_ and q:
                            pe.wait_ge(sem("filter_norm"), cb + 1)
                        for k in range(2):
                            at = k * 2 * S + part_ * S + q * P
                            ins = pe.matmul(f_ps[:, 2 * part_ + q, :], f_dft[:, at:at + P], src[:, k, :],
                                            start=(k == 0), stop=(k == 1))
                ins.then_inc(sem("filter_spec"), 1)
                yield
                yield
            pe.drain().then_inc(sem("filter_done"), 1)

        def filter_sp(sp, cb):
            sp.wait_ge(sem("filter_spec_out"), cb + 1)
            for j in range(4):
                sp.dma_start(A2(k_scr[4 * cb + j], a=4), f_k[:, :, j * P:(j + 1) * P])\
                  .then_inc(sem("scratch_stored"), 16)

        def hg_act(act):
            ch = hh["act"]

            def make(columns):
                def gen(i):
                    ch.begin(act, i)
                    wait(act, "tile_out", PHD["two"].tile_number(i, 2) + 1)
                    act.activation(h_th, h_z[:, 1:3, :], ACT.Tanh, scale=0.5).then_inc(sem("hgrn_tanh"), 1)
                    yield
                    wait(act, "hgrn_par", i + LATER)
                    act.wait_ge(sem("hgrn_tanh"), i + LATER)
                    for d in range(2):
                        ins = act.activation(h_lf[:, d, :], h_th[:, d, :], ACT.Ln,
                                             scale=h_p[:, d, 0:1], bias=h_p[:, d, 1:2])
                    ins.then_inc(sem("hgrn_log"), 1)
                    yield
                    yield
                    wait(act, "hg_exponents", i + 1)
                    act.activation(h_e1, h_lf, ACT.Exp)
                    act.activation(h_e2, h_lf, ACT.Exp, scale=-1.0)
                    act.activation(h_e4, h_a, ACT.Exp)
                    act.activation(h_e3, h_e3, ACT.Exp).then_inc(sem("hg_decays"), 1)
                    yield
                    yield
                    wait(act, "hgrn_kT", i + LATER)
                    act.activation(h_kT, A2(mix[:, 2, :], a=4), ACT.Copy).then_inc(sem("hgrn_kT_out"), 1)
                    yield
                    yield
                    wait(act, "rule_o", i + LATER)
                    act.activation(h_o[:, 0, :], mix[:, 0, 0:S], ACT.Square).then_inc(sem("rule_osq"), 1)
                    act.activation(h_o[:, 1, :], h_z[:, 4, :], ACT.Tanh, scale=0.5)\
                       .then_inc(sem("rule_gtanh"), 1)
                    yield
                    wait(act, "rule_onorm", i + LATER)
                    rsqrt_act(act, ch, mix[:, 1, 0:S], h_e1[:, 0, :], h_e1[:, 1, :], 1.0 / HD, EPS,
                              "rule_guess")
                    yield
                    wait(act, "rule_out", i + LATER)
                    act.activation(act_b[:, bass.ds(i, 1), 0:S].squeeze(1), h_o[:, 0, :], ACT.Copy)\
                       .then_inc(sem("rule_hi"), 1)
                    yield
                    ch.end()
                return gen
            return make

        def hg_dve(dve):
            ch = hh["dve"]

            def make(columns):
                def gen(i):
                    ch.begin(dve, i)
                    dve.wait_ge(sem("two_loaded"), 16 * TWO_LOADS)
                    ch.step(dve.tensor_copy(h_g1, h_gain[:, bass.ds(i, 1)]))
                    dve.tensor_copy(h_p, lbs[:, bass.ds(i, 1), :, :].squeeze(1))\
                       .then_inc(sem("hgrn_par"), 1)
                    wait(dve, "hgrn_vT", i + LATER)
                    dve.tensor_copy(h_vT, A2(mix[:, 0, 0:2 * P], a=2)).then_inc(sem("hg_vT_out"), 1)
                    yield
                    wait(dve, "hgrn_tanh", i + LATER)
                    dve.wait_ge(sem("hgrn_par"), i + LATER)
                    for d in range(2):
                        ch.step(dve.tensor_scalar(h_kk[:, d, :], h_th[:, d, :], h_p[:, d, 2:3],
                                                  h_p[:, d, 0:1], ALU.mult, ALU.add))
                    yield
                    wait(dve, "hgrn_log", i + LATER)
                    ch.step(dve.tensor_tensor_scan(h_a[:, 0, :], h_reset[:, 0, :], h_lf[:, 0, :], 0.0,
                                                   ALU.mult, ALU.add))
                    ch.step(dve.tensor_tensor_scan(h_a[:, 1, ::-1], h_reset[:, 1, ::-1],
                                                   h_lf[:, 1, ::-1], 0.0, ALU.mult, ALU.add))
                    ch.settle()
                    for d in range(2):
                        a = h_a[:, d, :].rearrange("p (c t) -> p c t", t=CH)
                        mid = a[:, :, MID[d]:MID[d] + 1].to_broadcast([P, 4, CH])
                        end = a[:, :, END[d]:END[d] + 1].to_broadcast([P, 4, CH])
                        dve.tensor_tensor(h_lf[:, d, :].rearrange("p (c t) -> p c t", t=CH), a, mid,
                                          ALU.subtract)
                        ins = dve.tensor_tensor(h_e3[:, d, :].rearrange("p (c t) -> p c t", t=CH), end,
                                                a, ALU.subtract)
                    ins.then_inc(sem("hg_exponents"), 1)
                    yield
                    wait(dve, "hg_decays", i + 1)
                    q = bc(h_z[:, 0, :], 2)
                    dve.tensor_tensor(h_e1, h_e1, q, ALU.mult)
                    dve.tensor_tensor(h_e2, h_e2, h_kk, ALU.mult)
                    dve.tensor_tensor(h_e3, h_e3, h_kk, ALU.mult)
                    dve.tensor_tensor(h_qa, h_e4, q, ALU.mult).then_inc(sem("hg_products"), 1)
                    yield
                    yield
                    wait(dve, "hg_scores", i + 1)
                    ch.step(dve.tensor_copy(h_s[:, :, 0, :], s0[:, bass.ds(i, 1), :, :].squeeze(1)))
                    dve.copy_predicated(h_sc, h_mask.bitcast(I32), A2(mix[:, 1, :], a=4))\
                       .then_inc(sem("hg_masked"), 1)
                    yield
                    wait(dve, "hg_upd", i + 1)
                    ch.settle()
                    for c in range(3):
                        for d in range(2):
                            chunk = c if d == 0 else 3 - c
                            e = chunk * CH + END[d]
                            ins = dve.scalar_tensor_tensor(
                                h_s[:, d, c + 1, :], h_s[:, d, c, :], h_e4[:, d, e:e + 1],
                                update_place(d, c), ALU.mult, ALU.add)
                            if c < 2:
                                ch.step(ins)
                        if c < 2:
                            ch.settle()
                    ins.then_inc(sem("hg_states"), 1)
                    yield
                    wait(dve, "rule_gtanh", i + LATER)
                    ch.step(dve.scalar_tensor_tensor(h_o[:, 1, :], h_o[:, 1, :], 1.0, h_z[:, 4, :],
                                                     ALU.add, ALU.mult))
                    yield
                    wait(dve, "rule_guess", i + LATER)
                    newton(ch, dve, mix[:, 1, 0:S], h_e1[:, 0, :], h_e2[:, 0, :], h_e2[:, 1, :],
                           1.0 / HD, EPS)
                    ch.step(dve.scalar_tensor_tensor(h_e2[:, 1, :], mix[:, 0, 0:S], h_g1,
                                                     h_e2[:, 0, :], ALU.mult, ALU.mult))
                    ch.settle()
                    o, v, g = h_o[:, 0, :], h_e2[:, 1, :], h_o[:, 1, :]
                    if columns:
                        o = o.rearrange("p (r c) -> p c r", c=64)
                        g = g.rearrange("p (r c) -> p c r", c=64)
                        v = v.rearrange("p (c r) -> p c r", r=4)
                    dve.scalar_tensor_tensor(o, v, 0.5, g, ALU.mult, ALU.mult)\
                       .then_inc(sem("rule_out"), 1)
                    yield
                    wait(dve, "rule_hi", i + LATER)
                    o = act_b[:, bass.ds(i, 1), :].squeeze(1)
                    ch.step(dve.tensor_tensor(o[:, S:2 * S], h_o[:, 0, :], o[:, 0:S], ALU.subtract))
                    yield
                    ch.end()
                return gen
            return make

        def hg_pe(pe):
            def make(columns):
                def gen(i):
                    wait(pe, "tile_out", PHD["two"].tile_number(i, 3) + 1)
                    wait(pe, "hy_out", i)
                    for k in range(2):
                        ins = pe.transpose(mix[:, 0, k * P:(k + 1) * P], h_z[:, 3, k * P:(k + 1) * P],
                                           ident)
                    ins.then_inc(sem("hgrn_vT"), 1)
                    yield
                    yield
                    yield
                    yield
                    yield
                    wait(pe, "hg_products", i + 1)
                    for m in range(4):
                        d, ks = m // 2, slice((m % 2) * P, (m % 2 + 1) * P)
                        ins = pe.matmul(mix[:, 1, m * P:(m + 1) * P], h_e2[:, d, ks], h_e1[:, d, ks],
                                        start=True, stop=True)
                    ins.then_inc(sem("hg_scores"), 1)
                    for m in range(4):
                        d, ks = m // 2, slice((m % 2) * P, (m % 2 + 1) * P)
                        ins = pe.transpose(mix[:, 2, m * P:(m + 1) * P], h_e3[:, d, ks], ident)
                    ins.then_inc(sem("hgrn_kT"), 1)
                    yield
                    wait(pe, "hgrn_kT_out", i + LATER)
                    wait(pe, "hg_vT_out", i + 1)
                    for m in range(6):
                        d, c = m // 3, m % 3
                        chunk = c if d == 0 else 3 - c
                        r = slice((chunk % 2) * CH, (chunk % 2 + 1) * CH)
                        ins = pe.matmul(update_place(d, c),
                                        h_kT[r, 2 * d + chunk // 2, :], h_vT[r, chunk // 2, :],
                                        start=True, stop=True)
                    ins.then_inc(sem("hg_upd"), 1)
                    yield
                    wait(pe, "hg_masked", i + 1)
                    wait(pe, "hg_states", i + 1)
                    for k in range(2):
                        o = mix[:, 0, k * P:(k + 1) * P]
                        for d in range(2):
                            pe.matmul(o, h_vT[:, k, :], h_sc[:, 2 * d + k, :], start=(d == 0),
                                      stop=False)
                        for chunk in (2 * k, 2 * k + 1):
                            oc = mix[:, 0, chunk * CH:(chunk + 1) * CH]
                            for d in range(2):
                                c = chunk if d == 0 else 3 - chunk
                                ins = pe.matmul(oc, h_s[:, d, c, :],
                                                h_qa[:, d, chunk * CH:(chunk + 1) * CH], start=False,
                                                stop=(chunk % 2 == 1 and d == 1))
                    ins.then_inc(sem("rule_o"), 1)
                    yield
                    wait(pe, "rule_osq", i + LATER)
                    pe.matmul(mix[:, 1, 0:S], ones, h_o[:, 0, :], start=True, stop=True)\
                      .then_inc(sem("rule_onorm"), 1)
                    yield
                    yield
                return gen
            return make

        yd = Chain("hy_dve_steps", per=18)

        def hy_dve(dve):
            ch = yd

            def gen(i):
                ch.begin(dve, i)
                ch.step(dve.tensor_copy(y_hp, y_par[:, bass.ds(i, 1), :].squeeze(1)))
                ch.step(dve.tensor_copy(y_rs1, y_rs[:, bass.ds(i, 1)]))
                ch.settle()
                for c in range(3):
                    ch.step(dve.tensor_scalar(y_c[:, c, :], y_t[:, c, :], y_hp[:, 3 * c + 1:3 * c + 2],
                                              y_hp[:, 9 + c:10 + c], ALU.mult, ALU.add))
                for j, o, a in ((0, slice(1, S), slice(0, S - 1)), (2, slice(0, S - 1), slice(1, S))):
                    ch.settle()
                    for c in range(3):
                        ch.step(dve.scalar_tensor_tensor(y_c[:, c, o], y_t[:, c, a],
                                                         y_hp[:, 3 * c + j:3 * c + j + 1], y_c[:, c, o],
                                                         ALU.mult, ALU.add))
                ch.settle()
                dve.tensor_tensor(y_u, y_c[:, 0, :], y_c[:, 1, :], ALU.mult).then_inc(sem("hy_u"), 1)
                yield
                yield
                wait(dve, "hy_uT", i + 1)
                dve.tensor_copy(y_uT, A2(mix[:, 0, 0:2 * P], a=2)).then_inc(sem("hy_uT_out"), 1)
                yield
                wait(dve, "hy_spec", i + 1)
                wait(dve, "spec_loaded", i * 16 + 16)
                u, f, y, w = A2(mix[:, 1, :], a=4), y_k, y_y, y_w
                C, N = slice(0, 2), slice(2, 4)
                ch.step(dve.tensor_tensor(y[:, C], u[:, C], f[:, C], ALU.mult))
                ch.step(dve.tensor_tensor(w[:, C], u[:, N], f[:, N], ALU.mult))
                ch.step(dve.tensor_tensor(y[:, N], u[:, C], f[:, N], ALU.mult))
                ch.step(dve.tensor_tensor(w[:, N], u[:, N], f[:, C], ALU.mult))
                ch.settle()
                dve.tensor_tensor(y[:, C], y[:, C], w[:, C], ALU.subtract)
                dve.tensor_tensor(y[:, N], y[:, N], w[:, N], ALU.add).then_inc(sem("hy_prod"), 1)
                yield
                wait(dve, "hy_back", i + 1)
                ch.step(dve.tensor_scalar(y_c[:, 0, :], mix[:, 2, 0:S], y_rs1, None, ALU.mult))
                ch.settle()
                ch.step(dve.scalar_tensor_tensor(y_c[:, 0, :], y_u, y_hp[:, 12:13], y_c[:, 0, :],
                                                 ALU.mult, ALU.add))
                ch.settle()
                dve.tensor_tensor(y_c[:, 0, :], y_c[:, 0, :], y_c[:, 2, :], ALU.mult)\
                   .then_inc(sem("hy_out"), 1)
                yield
                wait(dve, "pair_hi", i + LATER)
                o = act_b[:, bass.ds(i + NH, 1), :].squeeze(1)
                ch.step(dve.tensor_tensor(o[:, S:2 * S], y_c[:, 0, :], o[:, 0:S], ALU.subtract))
                yield
                ch.end()
            return gen

        def hy_act(act):
            def gen(i):
                for _ in range(4):
                    yield
                wait(act, "hy_out", i + 1)
                act.activation(act_b[:, bass.ds(i + NH, 1), 0:S].squeeze(1), y_c[:, 0, :], ACT.Copy)\
                   .then_inc(sem("pair_hi"), 1)
                yield
                yield
            return gen

        def hy_pe(pe):
            def gen(i):
                yield
                yield
                pe.wait_ge(sem("two_loaded"), 16 * TWO_LOADS)
                wait(pe, "rule_out", i + LATER)
                wait(pe, "hy_u", i + 1)
                for k in range(2):
                    ins = pe.transpose(mix[:, 0, k * P:(k + 1) * P], y_u[:, k * P:(k + 1) * P], ident)
                ins.then_inc(sem("hy_uT"), 1)
                yield
                wait(pe, "hy_uT_out", i + 1)
                for m in range(4):
                    for k in range(2):
                        at = k * 2 * S + m * P
                        ins = pe.matmul(mix[:, 1, m * P:(m + 1) * P], dft[:, at:at + P], y_uT[:, k, :],
                                        start=(k == 0), stop=(k == 1))
                ins.then_inc(sem("hy_spec"), 1)
                yield
                wait(pe, "hy_prod", i + 1)
                for m in range(4):
                    ins = pe.matmul(mix[:, 2, 0:S], y_y[:, m, :], idft[:, m * S:(m + 1) * S],
                                    start=(m == 0), stop=(m == 3))
                ins.then_inc(sem("hy_back"), 1)
                yield
                yield
            return gen

        PHD = {}
        for p_ in PH:
            PHD.setdefault(p_.name, p_)
        ups = [p_ for p_ in PH if p_.name == "up"]
        downs = [p_ for p_ in PH if p_.name == "down"]
        mlp1s = [p_ for p_ in PH if p_.name == "mlp1"]
        mlp2s = [p_ for p_ in PH if p_.name == "mlp2"]

        MEETS = ["normed_mix", "one_done", "out_done", "normed_ffn", "ffn_done", "normed_final",
                 "normed_ctx", "ctx_done", "normed_two", "two_done", "out2_done",
                 "normed_mlp", "mlp_done"]

        def at_meet(eng, name):
            eng.wait_ge(sem("phase_end"), 3 * (MEETS.index(name) + 1))

        def meet(eng, who, name, go_on=False):
            assert MEETS[ends[who]] == name, (name, MEETS[ends[who]])
            ends[who] += 1
            eng.drain().then_inc(sem("phase_end"), 1)
            if not go_on:
                eng.wait_ge(sem("phase_end"), 3 * ends[who])

        tokens_in = Area(WORK - 8192).take(KT, S)
        gm = sb("gain_mod", [P, 3, KT])
        norms = [
            Norm(tokens_in, gains[:, 0:16], act_a),
            Norm(x, gains[:, 16:32], act_a),
            Norm(x, gains[:, 32:48], None, plain=x),
            Norm(tokens_in, gm[:, 0, :], act_a, shift=mod[:, 1, 0:16]),
            Norm(x, gm[:, 1, :], act_a, shift=mod[:, 0, 0:16]),
            Norm(x, gm[:, 2, :], act_a, shift=mod[:, 0, 48:64]),
            Norm(x, gains[:, 80:96], None, plain=x),
        ]
        g1 = lambda i, k: mod[:, 0, bass.ds(i * 4 + (32 + k), 1)]
        g2 = lambda i, k: mod[:, 0, bass.ds(i * 4 + (80 + k), 1)]

        GATE = [ld_tri, ld_gsign, ld_ropef, ld_ropes, (g_par[0:32], io["gate_par"]),
                (r_pos[0:32].bitcast(I32), io["positions"][0].partition_broadcast(32)), ld_dil]
        ONE = [ld_lev, ld_neg, (d_par, io["delta_par"])]
        GATE_LOADS, ONE_LOADS = len(GATE), len(GATE) + len(ONE)
        FILTER = [ld_nf, (f_z[0:33], io["flt_z"]), (f_w1[0:33], io["flt_w1"]),
                  (f_w2[0:64], io["flt_w2"]), (f_w3[0:64], io["flt_w3"]),
                  (f_vec[0:64], io["flt_vec"]), (f_win.rearrange("p a b -> p (a b)"), io["flt_win"])]
        TWO = [ld_dft, ld_idft, ld_reset, (y_par, io["hy_par"]), (h_gain, io["hg_gain"]),
               (h_mask.rearrange("p a b -> p (a b)").bitcast(I32), io["hg_mask"])]
        FILTER_LOADS, TWO_LOADS = len(FILTER) + 1, len(FILTER) + 1 + len(TWO)

        def up_mixers(who, eng, ph):
            plan = [(0, 2, 1, ada_mix(who, eng, ph, 0), -1)] if ph.ada_items() else []
            if who != "pe":
                hidden = up_act if who == "act" else up_dve
                plan.append((0, ph.ipb, 1, hidden(eng, ph), -1))
            return plan

        def two_mixers(who, eng, hyena, hgrn):
            ph = PHD["two"]
            return [(0, 2, 1, ada_mix(who, eng, ph, 1), -1), (0, 10, 1, hyena(eng), -1),
                    (20, 3, 1, ada_mix(who, eng, ph, 0), 0),
                    (21, 19, 1, lambda i: hgrn(ph.late)(i), 0)]

        block = es.enter_context(nc.Block())

        @block.sync
        def _(sp):
            def load(dst, src, name):
                sp.dma_start(dst, src).then_inc(sem(name), 16)

            def run(ph, once=None, extra=None):
                def body(i, first, last):
                    for t in range(ph.ipb):
                        load_items(sp, ph, i, t)
                        if once and first and t == AHEAD:
                            once()
                        if extra:
                            extra(i, t, first)
                bodies(sp, ph, body)

            def load_for_one():
                at_meet(sp, "normed_mix")
                sp.wait_ge(sem("one_loaded"), 16 * GATE_LOADS)
                for dst, src in ONE:
                    load(dst, src, "one_loaded")

            def rows(i, t, first):
                if t != 15:
                    return
                if first:
                    sp.wait_ge(sem("gate_row_out"), 1)
                    for d in range(2):
                        for kind in range(2):
                            r = 16 * (1 - kind) + 8 * d
                            load(g_scr[:, 2 * d + kind, :], g_row[r:r + 8, :], "scratch_stored")
                    sp.wait_ge(sem("scratch_stored"), 64)
                src = g_scr[i].rearrange("a s -> (a s)").partition_broadcast(P)
                wait(sp, "dil_lo", i)
                load(d_bc.rearrange("p a b s -> p (a b s)"), src, "bc_loaded")

            def load_residual():
                at_meet(sp, "one_done")
                load(ada_c.rearrange("p a b -> p (a b)"), io["cvec"], "small2_loaded")
                load(*ld_sel, "small2_loaded")
                load(lbl, io["lb_logits"], "small2_loaded")
                load(x, io["x"], "x_loaded")

            def load_for_ffn():
                at_meet(sp, "out_done")
                load(ffn_par.rearrange("p a b -> p (a b)"), io["ffn_par"], "ffn_par_loaded")

            def beside_last_down(i, t, first):
                at = 8 * i + t
                if at == 2:
                    at_meet(sp, "normed_ffn")
                    for dst, src in FILTER:
                        load(dst, src, "two_loaded")
                if at == 11:
                    sp.wait_ge(sem("up_lo"), sum(n for _, n in FFN_PARTS))
                    load(*ld_fdft, "two_loaded")
                if at in (22, 28):
                    filter_sp(sp, (22, 28).index(at))
                if at == 31:
                    sp.wait_ge(sem("filter_done"), 3)
                    sp.wait_ge(sem("scratch_stored"), 64 + 16 * NH)
                    load(tokens_in, io["ctx"], "ctx_loaded")

            def spill_residual():
                at_meet(sp, "normed_final")
                load(x_scr, x, "scratch_stored")

            def load_for_two():
                at_meet(sp, "normed_two")
                sp.wait_ge(sem("scratch_stored"), 64 + 16 * NH + 16)
                for dst, src in TWO:
                    load(dst, src, "two_loaded")

            def spectra(i, t, first):
                if t == 24:
                    wait(sp, "hy_prod", i)
                    load(y_k.rearrange("p a b -> p (a b)"), k_scr[i], "spec_loaded")

            def reload_residual():
                at_meet(sp, "two_done")
                load(x, x_scr, "x_loaded")

            def load_first():
                for c in range(4):
                    load(tokens_in[:, 4 * c:4 * c + 4, :], io["x"][:, 4 * c:4 * c + 4, :], "x_loaded")
                    if c == 0:
                        load(eye1[:, :], io["const"][:, 0:2 * P], "small_loaded")
                load(gains[:, :], io["gains"], "small_loaded")
                for dst, src in GATE:
                    load(dst, src, "one_loaded")

            run(PHD["gate"], load_first)
            run(PHD["one"], load_for_one, rows)
            run(PHD["out"], load_residual)
            for u, dn in zip(ups, downs):
                run(u, load_for_ffn if u is ups[0] else None)
                run(dn, None, beside_last_down if dn is downs[-1] else None)
            run(PHD["ctx"], spill_residual)
            run(PHD["two"], load_for_two, spectra)
            run(PHD["out2"], reload_residual)
            for u, dn in zip(mlp1s, mlp2s):
                run(u)
                run(dn)
            for c in range(4):
                sp.wait_ge(sem("norm_scaled"), KT * norms[6].n + 4 * c + 4)
                load(out_dram[:, 4 * c:4 * c + 4, :], x[:, 4 * c:4 * c + 4, :], "out_stored")
            sp.wait_ge(sem("out_stored"), 64)

        @block.scalar
        def _(act):
            def phase(ph, evac, plan=(), slow=None):
                drive(act, ph, split_hi, evac, Mixers(plan), slow=slow)
            for t in range(AHEAD):
                split_hi(act, PHD["gate"], 0, t)
            act.wait_ge(sem("x_loaded"), 64)
            norms[0].act(act)
            meet(act, "act", "normed_mix")
            phase(PHD["gate"], act_half(act, PHD["gate"]))
            gate_act(act)
            ph = PHD["one"]
            phase(ph, act_half(act, ph), [(0, 8, 1, dil_act(act), -1), (3, 29, 1, delta_act(act), 0)])
            meet(act, "act", "one_done")
            ada_prologue_act(act)
            phase(PHD["out"], act_half(act, PHD["out"]))
            meet(act, "act", "out_done")
            norms[1].act(act)
            meet(act, "act", "normed_ffn")
            for k, (u, dn) in enumerate(zip(ups, downs)):
                phase(u, act_half(act, u), up_mixers("act", act, u))
                phase(dn, act_half(act, dn), slow=filter_act(act) if dn is downs[-1] else None)
            meet(act, "act", "ffn_done")
            norms[2].act(act)
            meet(act, "act", "normed_final")
            act.wait_ge(sem("ctx_loaded"), 16)
            norms[3].act(act)
            ctx_prologue_act(act)
            meet(act, "act", "normed_ctx")
            phase(PHD["ctx"], act_half(act, PHD["ctx"]), [(0, 8, 1, ctx_mix_act(act), -1)])
            meet(act, "act", "ctx_done")
            norms[4].act(act)
            meet(act, "act", "normed_two")
            ph = PHD["two"]
            hg = hg_act(act)
            phase(ph, act_half(act, ph), two_mixers("act", act, hy_act, hg))
            meet(act, "act", "two_done")
            phase(PHD["out2"], act_half(act, PHD["out2"], g1))
            meet(act, "act", "out2_done")
            norms[5].act(act)
            meet(act, "act", "normed_mlp")
            for k, (u, dn) in enumerate(zip(mlp1s, mlp2s)):
                phase(u, act_half(act, u), [(0, 2, 1, mlp_act(act, u), -1)])
                phase(dn, act_half(act, dn, g2))
            meet(act, "act", "mlp_done")
            norms[6].act(act)

        @block.vector
        def _(dve):
            def phase(ph, evac, plan=(), slow=None):
                drive(dve, ph, split_lo("dve"), evac, Mixers(plan), slow=slow)
            for t in range(AHEAD):
                split_lo("dve")(dve, PHD["gate"], 0, t)
            dve.wait_ge(sem("x_loaded"), 64)
            dve.wait_ge(sem("small_loaded"), 32)
            norms[0].dve(dve)
            meet(dve, "dve", "normed_mix")
            ph = PHD["gate"]
            phase(ph, dve_whole(dve, ph, lambda i, k: d_t[:, 0, :]))
            gate_dve(dve)
            dve.wait_ge(sem("one_loaded"), 16 * ONE_LOADS)
            ph = PHD["one"]
            phase(ph, dve_whole(dve, ph, lambda i, k: d_t[:, k, :] if k < 4 else dl[:, k - 4, :]),
                  [(0, 8, 1, dil_dve(dve), -1), (3, 29, 1, delta_dve(dve), 0),
                   (17, 9, 1, rope_dve(dve), 0)])
            meet(dve, "dve", "one_done")
            ada_prologue_dve(dve)
            dve.wait_ge(sem("x_loaded"), 80)
            phase(PHD["out"], dve_residual(dve, PHD["out"]))
            meet(dve, "dve", "out_done")
            norms[1].dve(dve)
            meet(dve, "dve", "normed_ffn")
            dve.wait_ge(sem("ffn_par_loaded"), 16)
            for k, (u, dn) in enumerate(zip(ups, downs)):
                phase(u, dve_whole(dve, u, lambda i, k: up[:, k, :]), up_mixers("dve", dve, u))
                phase(dn, dve_residual(dve, dn), slow=filter_dve(dve) if dn is downs[-1] else None)
            meet(dve, "dve", "ffn_done")
            norms[2].dve(dve)
            meet(dve, "dve", "normed_final")
            for m, v in enumerate((1, 0)):
                ins = dve.scalar_tensor_tensor(gm[:, m, :], mod[:, v, 16:32], 1.0, gains[:, 48:64],
                                               ALU.add, ALU.mult)
            ins.then_inc(sem("gains_ready"), 1)
            dve.wait_ge(sem("gains_ready"), 1)
            dve.wait_ge(sem("ctx_loaded"), 16)
            norms[3].dve(dve)
            ctx_prologue_dve(dve)
            meet(dve, "dve", "normed_ctx")
            ph = PHD["ctx"]
            phase(ph, dve_whole(dve, ph, lambda i, k: c_z[:, k, :]), [(0, 8, 1, ctx_mix_dve(dve), -1)])
            meet(dve, "dve", "ctx_done")
            norms[4].dve(dve)
            meet(dve, "dve", "normed_two")
            dve.memset(h_sc, 0.0).then_inc(sem("scores_clear"), 1)
            dve.wait_ge(sem("scores_clear"), 1)
            ph = PHD["two"]
            hg = hg_dve(dve)
            phase(ph, dve_whole(dve, ph, lambda i, k: h_z[:, k, :] if k < 5 else y_t[:, k - 5, :],
                                lambda i, k: PHD["two"].late and k < 4),
                  two_mixers("dve", dve, hy_dve, hg))
            meet(dve, "dve", "two_done")
            dve.wait_ge(sem("x_loaded"), 96)
            phase(PHD["out2"], dve_residual(dve, PHD["out2"], g1))
            meet(dve, "dve", "out2_done")
            dve.scalar_tensor_tensor(gm[:, 2, :], mod[:, 0, 64:80], 1.0, gains[:, 64:80], ALU.add,
                                     ALU.mult).then_inc(sem("gains_ready"), 1)
            dve.wait_ge(sem("gains_ready"), 2)
            norms[5].dve(dve)
            meet(dve, "dve", "normed_mlp")
            for k, (u, dn) in enumerate(zip(mlp1s, mlp2s)):
                phase(u, dve_whole(dve, u, lambda i, k: up[:, k, :]), [(0, 2, 1, mlp_dve(dve, u), -1)])
                phase(dn, dve_residual(dve, dn, g2))
            meet(dve, "dve", "mlp_done")
            norms[6].dve(dve)

        @block.gpsimd
        def _(pool):
            for t in range(AHEAD):
                split_lo("pool")(pool, PHD["gate"], 0, t)
            for ph in PH:
                drive(pool, ph, split_lo("pool"), None, Mixers(()), tiles=False)

        @block.tensor
        def _(pe):
            def normed(norm):
                return lambda kt: ("norm_lo", KT * norm.m + kt + 1)

            def phase(ph, src, plan=(), hidden=None, slow=None):
                drive_pe(pe, ph, gemm_block(pe, ph, src, hidden), Mixers(plan), slow)
            pe.wait_ge(sem("small_loaded"), 32)
            norms[0].pe(pe)
            meet(pe, "pe", "normed_mix", go_on=True)
            phase(PHD["gate"], act_a, hidden=normed(norms[0]))
            pe.wait_ge(sem("one_loaded"), 16 * GATE_LOADS)
            gate_pe(pe)
            phase(PHD["one"], act_a, [(0, 8, 1, dil_pe(pe), -1), (3, 29, 1, delta_pe(pe), 0)])
            meet(pe, "pe", "one_done")
            phase(PHD["out"], act_b)
            meet(pe, "pe", "out_done")
            norms[1].pe(pe)
            meet(pe, "pe", "normed_ffn", go_on=True)
            for k, (u, dn) in enumerate(zip(ups, downs)):
                phase(u, act_a, up_mixers("pe", pe, u), normed(norms[1]))
                phase(dn, act_b, hidden=lambda kt, n=u.done: ("up_lo", n + kt + 1),
                      slow=filter_pe(pe) if dn is downs[-1] else None)
            meet(pe, "pe", "ffn_done")
            norms[2].pe(pe)
            meet(pe, "pe", "normed_final")
            norms[3].pe(pe)
            meet(pe, "pe", "normed_ctx", go_on=True)
            phase(PHD["ctx"], act_a, [(0, 8, 1, ctx_mix_pe(pe), -1)], normed(norms[3]))
            meet(pe, "pe", "ctx_done")
            norms[4].pe(pe)
            meet(pe, "pe", "normed_two", go_on=True)
            ph = PHD["two"]
            hg = hg_pe(pe)
            phase(ph, act_a, two_mixers("pe", pe, hy_pe, hg), normed(norms[4]))
            meet(pe, "pe", "two_done")
            phase(PHD["out2"], act_b)
            meet(pe, "pe", "out2_done")
            norms[5].pe(pe)
            meet(pe, "pe", "normed_mlp", go_on=True)
            for k, (u, dn) in enumerate(zip(mlp1s, mlp2s)):
                phase(u, act_a, hidden=normed(norms[5]))
                phase(dn, act_b, hidden=lambda kt, n=u.done: ("mlp_lo", (n + kt) // 4 + 1))
            meet(pe, "pe", "mlp_done")
            norms[6].pe(pe)

    return nc


def kernel(**inputs):
    import concourse.bacc as bacc
    from concourse.bass_utils import run_bass_kernel_spmd

    arrays = lay_out({k: np.asarray(v) for k, v in inputs.items()})
    nc = bacc.Bacc("TRN2", target_bir_lowering=False, num_devices=1)
    io = {}
    for name, a in arrays.items():
        io[name] = nc.dram_tensor(name, a.shape, mybir.dt.from_np(a.dtype), kind="ExternalInput").ap()
    out = nc.dram_tensor("out", (P, KT, S), F32, kind="ExternalOutput").ap()
    build(nc, io, out)
    got = run_bass_kernel_spmd(nc, [arrays], core_ids=[0]).results[0]["out"]
    return np.ascontiguousarray(np.asarray(got).transpose(2, 1, 0).reshape(1, S, D))
```
